# Optimizing a Trainium2 kernel written in Bass

```python
import jax, jax.numpy as jnp
from jax import lax
import numpy as np

D_MODEL = 1024
BATCH = 1
SEQ = 256
DEPTH = 1

GRID_W = 64
CTX_LEN = 256
MIX_WIDTH = D_MODEL
POOL_WIDTH = MIX_WIDTH // 2
N_POOL_GROUPS = 4
POOL_GROUP_DIM = POOL_WIDTH // N_POOL_GROUPS
POOL_WINDOWS = (2, 4, 8, 16)
ATTN_WIDTH = MIX_WIDTH - POOL_WIDTH
N_HEADS = 8
HEAD_DIM = ATTN_WIDTH // N_HEADS
NA_KH = 8
NA_KW = 16
NA_QB = 16
NA_KB = 32
NA_NCB = GRID_W // NA_QB
D_FF = 4 * D_MODEL
N_MOD = 6
EPS = 1e-6


def _rmsnorm(x, g):
    x32 = x.astype(jnp.float32)
    y = x32 * lax.rsqrt(jnp.mean(x32 * x32, axis=-1, keepdims=True) + EPS)
    return (y * g.astype(jnp.float32)).astype(x.dtype)

def _modulate(x, gain, shift, scale):
    return _rmsnorm(x, gain) * (1 + scale) + shift

def _project(h, w_in_l):
    p = h @ w_in_l
    B, L, _ = p.shape
    u = p[..., :POOL_WIDTH]
    q, k, v = jnp.split(p[..., POOL_WIDTH:], 3, axis=-1)
    shp = (B, L, N_HEADS, HEAD_DIM)
    return u, q.reshape(shp), k.reshape(shp), v.reshape(shp)

def _pool_mixer(u, pool_w, pool_scale):
    B, L, _ = u.shape
    u32 = u.reshape(B, L, N_POOL_GROUPS, POOL_GROUP_DIM).astype(jnp.float32)
    cs = jnp.concatenate([jnp.zeros_like(u32[:, :1]), jnp.cumsum(u32, axis=1)], axis=1)
    t = jnp.arange(L)
    diffs = []
    for g, w in enumerate(POOL_WINDOWS):
        lo = w // 2
        hi = w - 1 - lo
        start = jnp.clip(t - lo, 0, L)
        end = jnp.clip(t + hi + 1, 0, L)
        count = (end - start).astype(jnp.float32)[None, :, None]
        diffs.append((cs[:, end, g] - cs[:, start, g]) / count - u32[:, :, g])
    d = jnp.stack(diffs, axis=2).astype(u.dtype)
    y = jnp.einsum('blgc,gcd->blgd', d, pool_w)
    return y.reshape(B, L, POOL_WIDTH) * pool_scale

def _na_column_tables():
    qcol = np.arange(GRID_W).reshape(NA_NCB, NA_QB)
    q_start = np.clip(qcol - NA_KW // 2, 0, GRID_W - NA_KW)
    kc0 = np.clip(np.arange(NA_NCB) * NA_QB - NA_KW // 2, 0, GRID_W - NA_KB)
    col_idx = kc0[:, None] + np.arange(NA_KB)
    kc = col_idx[:, None, :]
    mask = (kc >= q_start[:, :, None]) & (kc < q_start[:, :, None] + NA_KW)
    dc = np.clip(kc - qcol[:, :, None] + NA_KW - 1, 0, 2 * NA_KW - 2)
    return col_idx.astype(np.int32), mask, dc.astype(np.int32)

def _neighbourhood_attention(q, k, v, k_ctx, v_ctx, rpb):
    B, L, H, Dh = q.shape
    rows = L // GRID_W
    kh = min(NA_KH, rows)
    col_np, mask_np, dc_np = _na_column_tables()
    col_idx = jnp.asarray(col_np)
    col_mask = jnp.asarray(mask_np)[:, :, None, :]
    dc_idx = jnp.asarray(dc_np)[:, :, None, :]
    qg = q.reshape(B, rows, GRID_W, H, Dh)
    kg = k.reshape(B, rows, GRID_W, H, Dh)
    vg = v.reshape(B, rows, GRID_W, H, Dh)
    scale = Dh ** -0.5
    n_loc = kh * NA_KB

    def row_block(r):
        rs = jnp.clip(r - kh // 2, 0, rows - kh)
        q_r = lax.dynamic_index_in_dim(qg, r, axis=1, keepdims=False).reshape(B, NA_NCB, NA_QB, H, Dh)
        k_b = lax.dynamic_slice_in_dim(kg, rs, kh, axis=1)[:, :, col_idx]
        v_b = lax.dynamic_slice_in_dim(vg, rs, kh, axis=1)[:, :, col_idx]
        s_loc = jnp.einsum('bnqhd,brnkhd->bhnqrk', q_r, k_b).astype(jnp.float32) * scale
        dr_idx = rs + jnp.arange(kh) - r + (NA_KH - 1)
        bias = rpb[:, dr_idx[None, None, :, None], dc_idx]
        s_loc = jnp.where(col_mask, s_loc + bias.astype(jnp.float32), -jnp.inf)
        s_ctx = jnp.einsum('bnqhd,bkhd->bhnqk', q_r, k_ctx).astype(jnp.float32) * scale
        s = jnp.concatenate([s_loc.reshape(B, H, NA_NCB, NA_QB, n_loc), s_ctx], axis=-1)
        p = jax.nn.softmax(s, axis=-1).astype(v.dtype)
        p_loc = p[..., :n_loc].reshape(B, H, NA_NCB, NA_QB, kh, NA_KB)
        p_ctx = p[..., n_loc:]
        o = (jnp.einsum('bhnqrk,brnkhd->bnqhd', p_loc, v_b)
             + jnp.einsum('bhnqk,bkhd->bnqhd', p_ctx, v_ctx))
        return o.reshape(B, GRID_W, H, Dh)

    out = lax.map(row_block, jnp.arange(rows))
    return jnp.moveaxis(out, 0, 1).reshape(B, L, H * Dh)

def _context_attention(q, k, v):
    B, C, H, Dh = q.shape
    s = jnp.einsum('bqhd,bkhd->bhqk', q, k).astype(jnp.float32) * (Dh ** -0.5)
    p = jax.nn.softmax(s, axis=-1).astype(v.dtype)
    return jnp.einsum('bhqk,bkhd->bqhd', p, v).reshape(B, C, H * Dh)

def _sq_relu_mlp(h, w1, w2):
    return jnp.square(jax.nn.relu(h @ w1)) @ w2

def first_inputs(seed: int = 0) -> dict:
    key = jax.random.key(seed)
    ks = jax.random.split(key, 17)
    D = D_MODEL
    nrm = jax.random.normal
    return {
        'x': nrm(ks[0], (BATCH, SEQ, D), jnp.float32),
        'c': nrm(ks[1], (BATCH, D), jnp.float32),
        'ctx': nrm(ks[2], (BATCH, CTX_LEN, D), jnp.float32),
        'c_ctx': nrm(ks[3], (D,), jnp.float32),
        'w_mod': nrm(ks[4], (DEPTH, D, N_MOD * D), jnp.float32) * (0.5 * D ** -0.5),
        'b_mod': nrm(ks[5], (DEPTH, N_MOD * D), jnp.float32) * 0.02,
        'g_pre_mix': 1.0 + 0.1 * nrm(ks[6], (DEPTH, D), jnp.float32),
        'g_post_mix': 1.0 + 0.1 * nrm(ks[7], (DEPTH, D), jnp.float32),
        'g_pre_mlp': 1.0 + 0.1 * nrm(ks[8], (DEPTH, D), jnp.float32),
        'g_post_mlp': 1.0 + 0.1 * nrm(ks[9], (DEPTH, D), jnp.float32),
        'w_in': nrm(ks[10], (DEPTH, D, POOL_WIDTH + 3 * ATTN_WIDTH), jnp.float32) * D ** -0.5,
        'pool_w': nrm(ks[11], (DEPTH, N_POOL_GROUPS, POOL_GROUP_DIM, POOL_GROUP_DIM), jnp.float32) * POOL_GROUP_DIM ** -0.5,
        'pool_scale': 1.0 + 0.1 * nrm(ks[12], (DEPTH, POOL_WIDTH), jnp.float32),
        'rpb': 0.1 * nrm(ks[13], (DEPTH, N_HEADS, 2 * NA_KH - 1, 2 * NA_KW - 1), jnp.float32),
        'w_out': nrm(ks[14], (DEPTH, MIX_WIDTH, D), jnp.float32) * MIX_WIDTH ** -0.5,
        'w_mlp_in': nrm(ks[15], (DEPTH, D, D_FF), jnp.float32) * D ** -0.5,
        'w_mlp_out': nrm(ks[16], (DEPTH, D_FF, D), jnp.float32) * D_FF ** -0.5,
    }

def first_block(x, c, ctx, c_ctx, w_mod, b_mod, g_pre_mix, g_post_mix, g_pre_mlp, g_post_mlp,
              w_in, pool_w, pool_scale, rpb, w_out, w_mlp_in, w_mlp_out):
    for l in range(DEPTH):
        last = l == DEPTH - 1
        mod_x = (jax.nn.silu(c) @ w_mod[l] + b_mod[l])[:, None, :]
        mod_c = jax.nn.silu(c_ctx) @ w_mod[l] + b_mod[l]
        sh1, sc1, gt1, sh2, sc2, gt2 = jnp.split(mod_x, N_MOD, axis=-1)
        csh1, csc1, cgt1, csh2, csc2, cgt2 = jnp.split(mod_c, N_MOD, axis=-1)

        h_x = _modulate(x, g_pre_mix[l], sh1, sc1)
        h_c = _modulate(ctx, g_pre_mix[l], csh1, csc1)
        u_x, q_x, k_x, v_x = _project(h_x, w_in[l])
        u_c, q_c, k_c, v_c = _project(h_c, w_in[l])
        attn_x = _neighbourhood_attention(q_x, k_x, v_x, k_c, v_c, rpb[l])
        mix_x = jnp.concatenate([_pool_mixer(u_x, pool_w[l], pool_scale[l]), attn_x], axis=-1) @ w_out[l]
        x = x + gt1 * _rmsnorm(mix_x, g_post_mix[l])
        y_x = _sq_relu_mlp(_modulate(x, g_pre_mlp[l], sh2, sc2), w_mlp_in[l], w_mlp_out[l])
        x = x + gt2 * _rmsnorm(y_x, g_post_mlp[l])

        if not last:
            attn_c = _context_attention(q_c, k_c, v_c)
            mix_c = jnp.concatenate([_pool_mixer(u_c, pool_w[l], pool_scale[l]), attn_c], axis=-1) @ w_out[l]
            ctx = ctx + cgt1 * _rmsnorm(mix_c, g_post_mix[l])
            y_c = _sq_relu_mlp(_modulate(ctx, g_pre_mlp[l], csh2, csc2), w_mlp_in[l], w_mlp_out[l])
            ctx = ctx + cgt2 * _rmsnorm(y_c, g_post_mlp[l])
    return x


CHUNK = 64
A_HEADS = D_MODEL // 128
A_HEAD_DIM = 64
A_LEFT_CHUNKS = 8
A_BAND = A_LEFT_CHUNKS + 1
A_MAX_REL = 128
B_HEADS = D_MODEL // 128
B_Q_LORA = D_MODEL // 4
B_KV_LORA = D_MODEL // 8
B_NOPE = 64
B_ROPE = 32
B_V_DIM = 64
B_QK_DIM = B_NOPE + B_ROPE
ROPE_THETA = 10000.0
Q_BLOCK = 128
A_WIDTH = A_HEADS * A_HEAD_DIM
B_WIDTH = B_HEADS * B_V_DIM
D_MIX = A_WIDTH + B_WIDTH
IN_COLS = 3 * A_WIDTH + B_Q_LORA + B_KV_LORA + B_ROPE
D_FF_2 = ((8 * D_MODEL // 3 + 127) // 128) * 128
NEG_INF = -1e30


def rmsnorm(x, g):
    xf = x.astype(jnp.float32)
    y = xf * lax.rsqrt(jnp.mean(xf * xf, axis=-1, keepdims=True) + EPS)
    return (y * g.astype(jnp.float32)).astype(x.dtype)

def swiglu(h, w_gate, w_up, w_down):
    return (jax.nn.silu(h @ w_gate) * (h @ w_up)) @ w_down

def rope_tables(seq, dim):
    inv = 1.0 / (ROPE_THETA ** (jnp.arange(0, dim, 2, dtype=jnp.float32) / dim))
    ang = jnp.arange(seq, dtype=jnp.float32)[:, None] * inv[None, :]
    return jnp.cos(ang), jnp.sin(ang)

def apply_rope(x, cos, sin):
    x1, x2 = jnp.split(x, 2, axis=-1)
    c = cos[None, :, None, :].astype(x.dtype)
    s = sin[None, :, None, :].astype(x.dtype)
    return jnp.concatenate([x1 * c - x2 * s, x1 * s + x2 * c], axis=-1)

def chunked_relbias_attention(q, k, v, rel_bias):
    b, s, h, dh = q.shape
    nc = s // CHUNK
    band_len = A_BAND * CHUNK
    pad = ((0, 0), (A_LEFT_CHUNKS * CHUNK, 0), (0, 0), (0, 0))
    kp = jnp.pad(k, pad)
    vp = jnp.pad(v, pad)
    qc = q.reshape(b, nc, CHUNK, h, dh).transpose(1, 0, 2, 3, 4)
    qi = jnp.arange(CHUNK)
    kj = jnp.arange(band_len) - A_LEFT_CHUNKS * CHUNK
    rel = jnp.clip(qi[:, None] - kj[None, :], -A_MAX_REL, A_MAX_REL) + A_MAX_REL
    bias = rel_bias.astype(jnp.float32)[:, rel]
    scale = dh ** -0.5

    def one_chunk(args):
        q_blk, c = args
        kb = lax.dynamic_slice_in_dim(kp, c * CHUNK, band_len, axis=1)
        vb = lax.dynamic_slice_in_dim(vp, c * CHUNK, band_len, axis=1)
        sc = jnp.einsum('bihd,bjhd->bhij', q_blk, kb).astype(jnp.float32) * scale
        sc = sc + bias[None]
        valid = jnp.arange(band_len) >= (A_LEFT_CHUNKS - c) * CHUNK
        sc = jnp.where(valid[None, None, None, :], sc, NEG_INF)
        p = jax.nn.softmax(sc, axis=-1).astype(vb.dtype)
        return jnp.einsum('bhij,bjhd->bihd', p, vb)

    o = lax.map(one_chunk, (qc, jnp.arange(nc, dtype=jnp.int32)))
    return o.transpose(1, 0, 2, 3, 4).reshape(b, s, h * dh)

def block_causal_attention(q, k, v):
    b, s, h, dq = q.shape
    dv = v.shape[-1]
    nb = s // Q_BLOCK
    qb = q.reshape(b, nb, Q_BLOCK, h, dq).transpose(1, 0, 2, 3, 4)
    k_chunk = jnp.arange(s) // CHUNK
    scale = dq ** -0.5

    def one_block(args):
        q_blk, i = args
        q_chunk = (i * Q_BLOCK + jnp.arange(Q_BLOCK)) // CHUNK
        sc = jnp.einsum('bqhd,bkhd->bhqk', q_blk, k).astype(jnp.float32) * scale
        mask = k_chunk[None, :] <= q_chunk[:, None]
        sc = jnp.where(mask[None, None], sc, NEG_INF)
        p = jax.nn.softmax(sc, axis=-1).astype(v.dtype)
        return jnp.einsum('bhqk,bkhd->bqhd', p, v)

    o = lax.map(one_block, (qb, jnp.arange(nb, dtype=jnp.int32)))
    return o.transpose(1, 0, 2, 3, 4).reshape(b, s, h * dv)

def mla_attention(c_q, c_kv, k_rope, q_lat_norm, w_uq, kv_lat_norm, w_ukv,
                  q_nope_norm, q_rope_norm, k_nope_norm, k_rope_norm, cos, sin):
    b, s, _ = c_q.shape
    q = (rmsnorm(c_q, q_lat_norm) @ w_uq).reshape(b, s, B_HEADS, B_QK_DIM)
    kv = (rmsnorm(c_kv, kv_lat_norm) @ w_ukv).reshape(b, s, B_HEADS, B_NOPE + B_V_DIM)
    q_nope = rmsnorm(q[..., :B_NOPE], q_nope_norm)
    q_pe = apply_rope(rmsnorm(q[..., B_NOPE:], q_rope_norm), cos, sin)
    k_nope = rmsnorm(kv[..., :B_NOPE], k_nope_norm)
    v = kv[..., B_NOPE:]
    k_pe = apply_rope(rmsnorm(k_rope, k_rope_norm)[:, :, None, :], cos, sin)
    q_full = jnp.concatenate([q_nope, q_pe], axis=-1)
    k_full = jnp.concatenate([k_nope, jnp.broadcast_to(k_pe, (b, s, B_HEADS, B_ROPE))], axis=-1)
    return block_causal_attention(q_full, k_full, v)

def second_inputs(seed: int = 0) -> dict:
    key = jax.random.key(seed)
    ks = iter(jax.random.split(key, 32))
    f32 = jnp.float32

    def w(shape, fan_in):
        return jax.random.normal(next(ks), (DEPTH,) + shape, f32) * fan_in ** -0.5

    def gain(n):
        return 1.0 + 0.05 * jax.random.normal(next(ks), (DEPTH, n), f32)

    x = jax.random.normal(next(ks), (BATCH, SEQ, D_MODEL), f32)
    return {
        "x": x,
        "ffn1_norm": gain(D_MODEL),
        "ffn1_w_gate": w((D_MODEL, D_FF_2), D_MODEL),
        "ffn1_w_up": w((D_MODEL, D_FF_2), D_MODEL),
        "ffn1_w_down": w((D_FF_2, D_MODEL), D_FF_2),
        "mix_norm": gain(D_MODEL),
        "w_in": w((D_MODEL, IN_COLS), D_MODEL),
        "a_q_norm": gain(A_HEAD_DIM),
        "a_k_norm": gain(A_HEAD_DIM),
        "a_rel_bias": 0.5 * jax.random.normal(next(ks), (DEPTH, A_HEADS, 2 * A_MAX_REL + 1), f32),
        "b_q_lat_norm": gain(B_Q_LORA),
        "b_w_uq": w((B_Q_LORA, B_HEADS * B_QK_DIM), B_Q_LORA),
        "b_kv_lat_norm": gain(B_KV_LORA),
        "b_w_ukv": w((B_KV_LORA, B_HEADS * (B_NOPE + B_V_DIM)), B_KV_LORA),
        "b_q_nope_norm": gain(B_NOPE),
        "b_q_rope_norm": gain(B_ROPE),
        "b_k_nope_norm": gain(B_NOPE),
        "b_k_rope_norm": gain(B_ROPE),
        "w_out": w((D_MIX, D_MODEL), D_MIX),
        "ffn2_norm": gain(D_MODEL),
        "ffn2_w_gate": w((D_MODEL, D_FF_2), D_MODEL),
        "ffn2_w_up": w((D_MODEL, D_FF_2), D_MODEL),
        "ffn2_w_down": w((D_FF_2, D_MODEL), D_FF_2),
        "final_norm": gain(D_MODEL),
    }

def second_block(x, ffn1_norm, ffn1_w_gate, ffn1_w_up, ffn1_w_down, mix_norm, w_in,
              a_q_norm, a_k_norm, a_rel_bias, b_q_lat_norm, b_w_uq, b_kv_lat_norm,
              b_w_ukv, b_q_nope_norm, b_q_rope_norm, b_k_nope_norm, b_k_rope_norm,
              w_out, ffn2_norm, ffn2_w_gate, ffn2_w_up, ffn2_w_down, final_norm):
    b, s, _ = x.shape
    cos, sin = rope_tables(s, B_ROPE)
    o_qa, o_ka, o_va = 0, A_WIDTH, 2 * A_WIDTH
    o_cq = 3 * A_WIDTH
    o_ckv = o_cq + B_Q_LORA
    o_kr = o_ckv + B_KV_LORA
    for l in range(DEPTH):
        x = x + 0.5 * swiglu(rmsnorm(x, ffn1_norm[l]), ffn1_w_gate[l], ffn1_w_up[l], ffn1_w_down[l])
        proj = rmsnorm(x, mix_norm[l]) @ w_in[l]
        qa = rmsnorm(proj[..., o_qa:o_ka].reshape(b, s, A_HEADS, A_HEAD_DIM), a_q_norm[l])
        ka = rmsnorm(proj[..., o_ka:o_va].reshape(b, s, A_HEADS, A_HEAD_DIM), a_k_norm[l])
        va = proj[..., o_va:o_cq].reshape(b, s, A_HEADS, A_HEAD_DIM)
        out_a = chunked_relbias_attention(qa, ka, va, a_rel_bias[l])
        out_b = mla_attention(proj[..., o_cq:o_ckv], proj[..., o_ckv:o_kr], proj[..., o_kr:],
                              b_q_lat_norm[l], b_w_uq[l], b_kv_lat_norm[l], b_w_ukv[l],
                              b_q_nope_norm[l], b_q_rope_norm[l], b_k_nope_norm[l],
                              b_k_rope_norm[l], cos, sin)
        x = x + jnp.concatenate([out_a, out_b], axis=-1) @ w_out[l]
        x = x + 0.5 * swiglu(rmsnorm(x, ffn2_norm[l]), ffn2_w_gate[l], ffn2_w_up[l], ffn2_w_down[l])
        x = rmsnorm(x, final_norm[l])
    return x


def setup_inputs(seed=0):
    out = dict(first_inputs(seed))
    for name, value in second_inputs(seed + 1).items():
        if name != "x":
            out[name + "_2"] = value
    return out


def reference(
    x, c, ctx, c_ctx, w_mod, b_mod, g_pre_mix, g_post_mix, g_pre_mlp, g_post_mlp, w_in, pool_w,
    pool_scale, rpb, w_out, w_mlp_in, w_mlp_out, ffn1_norm_2, ffn1_w_gate_2, ffn1_w_up_2,
    ffn1_w_down_2, mix_norm_2, w_in_2, a_q_norm_2, a_k_norm_2, a_rel_bias_2, b_q_lat_norm_2,
    b_w_uq_2, b_kv_lat_norm_2, b_w_ukv_2, b_q_nope_norm_2, b_q_rope_norm_2, b_k_nope_norm_2,
    b_k_rope_norm_2, w_out_2, ffn2_norm_2, ffn2_w_gate_2, ffn2_w_up_2, ffn2_w_down_2,
    final_norm_2,
):
    x = first_block(
        x, c, ctx, c_ctx, w_mod, b_mod, g_pre_mix, g_post_mix, g_pre_mlp, g_post_mlp, w_in,
        pool_w, pool_scale, rpb, w_out, w_mlp_in, w_mlp_out,
    )
    return second_block(
        x, ffn1_norm_2, ffn1_w_gate_2, ffn1_w_up_2, ffn1_w_down_2, mix_norm_2, w_in_2,
        a_q_norm_2, a_k_norm_2, a_rel_bias_2, b_q_lat_norm_2, b_w_uq_2, b_kv_lat_norm_2,
        b_w_ukv_2, b_q_nope_norm_2, b_q_rope_norm_2, b_k_nope_norm_2, b_k_rope_norm_2, w_out_2,
        ffn2_norm_2, ffn2_w_gate_2, ffn2_w_up_2, ffn2_w_down_2, final_norm_2,
    )


_drawn_inputs = setup_inputs


def setup_inputs(seed=0):
    import zlib

    import numpy as np

    out = dict(_drawn_inputs(seed))
    spreads = {}
    factors = {'rpb': 8.0,
     'ffn1_norm_2': 2.842,
     'mix_norm_2': 4.282,
     'a_q_norm_2': 8.0,
     'a_k_norm_2': 8.0,
     'b_q_lat_norm_2': 8.0,
     'b_kv_lat_norm_2': 6.834,
     'b_q_nope_norm_2': 8.0,
     'b_q_rope_norm_2': 8.0,
     'b_k_nope_norm_2': 8.0,
     'b_k_rope_norm_2': 8.0,
     'ffn2_norm_2': 2.886}
    for name, (base, spread) in spreads.items():
        noise = np.random.default_rng([zlib.crc32(name.encode()), seed]).standard_normal(out[name].shape)
        drawn = base * np.exp(spread * noise) if base else spread * noise
        out[name] = __import__('jax').numpy.asarray(drawn.astype(out[name].dtype))
    for name, factor in factors.items():
        out[name] = (out[name] * factor).astype(out[name].dtype)
    return out
```

```python
from contextlib import ExitStack

import numpy as np

import concourse.bass as bass
from concourse import mybir

F32 = mybir.dt.float32
F32R = mybir.dt.float32r
ALU = mybir.AluOpType
ACT = mybir.ActivationFunctionType
AX_X = mybir.AxisListType.X

P = 128
D = 1024
KT = D // P
L = 256
FM = 32
F2 = 22
EPS = 1e-6
NEG = -1e30
W = 1024
RAW = 7
RING = 5

COLS = {}
_at = 0
for _name, _n in [("ident", 128), ("cc", 16), ("b_sh1", 8), ("b_sc1", 8), ("b_sh2", 8), ("b_sc2", 8),
                  ("g_mix", 8), ("g_mlp", 8), ("pool_scale", 4), ("g_ffn1", 8), ("g_mix2", 8), ("g_ffn2", 8),
                  ("g_aq", 1), ("g_ak", 1), ("g_bq", 1), ("g_bk", 1), ("g_ql", 2), ("g_kvl", 1),
                  ("g_qr", 32), ("g_kr", 32), ("cos2", 64), ("sin2", 64), ("invd", 16), ("mask", 512),
                  ("pool_w", 512)]:
    COLS[_name] = (_at, _n)
    _at += _n
NCOLS = _at


def mlp_order(n, lag):
    out = []
    for f in range(n + lag):
        if f < n:
            out.append(("up", f))
        if f >= lag:
            out.append(("down", f - lag))
    return out


MLP_LAG = 2
FFN_LAG = 1


def stream_plan():
    s = [("w_mod_c", j, 1024, "C") for j in range(16)]
    h = [("w_in_u", j, 1024, "H") for j in range(4)] + [("w_in_k", j, 1024, "H") for j in range(4)]
    h += [("w_in_q", j, 1024, "H") for j in range(4)] + [("w_in_v", j, 1024, "H") for j in range(4)]
    m = [("w_mod_r", j, 1024, "M") for j in range(32)]
    s += h[:5]
    mi = 0
    for c in h[5:]:
        s += m[mi:mi + 2]
        mi += 2
        s.append(c)
    s += m[mi:24]
    mi = 24
    s += [("w_out", k, 1024, "H") for k in range(8)]
    for n, (what, f) in enumerate(mlp_order(FM, MLP_LAG)):
        s.append(("w_mlp_in" if what == "up" else "w_mlp_out", f, 1024, "H"))
        if n >= 4 and n % 2 == 0 and mi < 32:
            s.append(m[mi])
            mi += 1

    def ffn(a):
        for what, f in mlp_order(F2, FFN_LAG):
            if what == "up":
                s.append((a + "_gate", f, 1024, "H"))
                s.append((a + "_up", f, 1024, "H"))
            else:
                s.append((a + "_down", f, 1024, "H"))

    ffn("ffn1")
    s.extend(("w_in2_l", j, 832, "H") for j in range(4))
    s.extend(("w_in2_q", j, 1024, "H") for j in range(4))
    s.extend(("w_uq", j, 768, "H") for j in range(2))
    s.append(("w_ukv", 0, 1024, "H"))
    s.extend(("w_in2_k", j, 1024, "H") for j in range(4))
    s.extend(("w_in2_v", j, 1024, "H") for j in range(4))
    s.extend(("w_out2", k, 1024, "H") for k in range(8))
    ffn("ffn2")
    return s


class Queue:

    def __init__(self, sem):
        self.sem, self.n, self.items = sem, 0, []

    def do(self, fn, *after):
        self.n += 1
        self.items.append((fn, after, True))
        return (self.sem, self.n)

    def go(self, fn, *after):
        self.items.append((fn, after, False))

    def play(self, eng):
        passed = {}
        for fn, after, counts in self.items:
            for w in after:
                if w is not None and passed.get(w[0].name, 0) < w[1]:
                    eng.wait_ge(w[0], w[1])
                    passed[w[0].name] = w[1]
            ins = fn(eng)
            if counts:
                ins.then_inc(self.sem, 1)


def build(nc, t):
    ctx = ExitStack()
    with ctx:
        def sb(name, shape, dt=F32):
            return ctx.enter_context(nc.sbuf_tensor(name, shape, dt))

        def sem(name):
            return ctx.enter_context(nc.semaphore(name))

        raw = [sb(f"raw{i}", [P, W]) for i in range(RAW)]
        hi = [sb(f"hi{i}", [P, W], F32R) for i in range(RING)]
        lo = [sb(f"lo{i}", [P, W], F32R) for i in range(RING)]
        x = sb("x", [P, 2, D])
        arena = sb("arena", [P, 4096 + 256])
        Th = sb("Th", [P, KT, 512], F32R)
        Tl = sb("Tl", [P, KT, 512], F32R)
        G1 = sb("G1", [P, D])
        G2 = sb("G2", [P, D])
        gp = sb("gp", [P, D])
        cols = sb("cols", [P, NCOLS])
        sc = [sb(f"sc{i}", [P, 512]) for i in range(3)]
        PT = [sb(f"PT{i}", [P, 4, L]) for i in range(2)]
        big = sb("big", [P, 11776])
        st = sb("st", [P, 768])
        ones = sb("ones", [P, P])
        ps = [ctx.enter_context(nc.psum_tensor(f"ps{i}", [P, 512], F32)) for i in range(8)]

        pe, act, dve, pool, sp = (Queue(sem("s_" + n)) for n in ("pe", "act", "dve", "pool", "sp"))
        s_raw = [sem(f"s_raw{i}") for i in range(RAW)]

        def col(name, a=0, b=None):
            at, n = COLS[name]
            return cols[:, at + a:at + (n if b is None else b)]

        ident = col("ident")
        xn = arena[:, 0:2048].rearrange("p (t d) -> p t d", t=2)
        cx = arena[:, 2048:4096].rearrange("p (t d) -> p t d", t=2)
        stat_at = [0]

        def stat(n):
            a = stat_at[0]
            stat_at[0] += n
            assert stat_at[0] <= 768
            return st[:, a:a + n]

        def load(name, dst, src, *after):
            s = sem("s_" + name)
            sp.go(lambda e: e.dma_start(dst, src).then_inc(s, 16), *after)
            return (s, 16)

        d_cols = load("cols", cols[:, :], t["cols"])
        d_x = [load(f"x{i}", x[:, i, :], t["x"][i * P:(i + 1) * P, :]) for i in range(2)]
        d_cx = [load(f"cx{i}", cx[:, i, :], t["ctx"][i * P:(i + 1) * P, :]) for i in range(2)]

        plan = stream_plan()
        freed = {}
        H = [n for n, c in enumerate(plan) if c[3] == "H"]
        used, ready = {}, {}
        state = {"h": 0, "m": 0, "split": 0, "owed": [], "acc": None}
        extra = {}

        def landed(n):
            return (s_raw[n % RAW], 16 * (n // RAW + 1))

        M = [n for n, c in enumerate(plan) if c[3] == "M"]
        acc = [big[:, 0:1024], big[:, 1024:2048]]
        acc_read = {}
        acc_done = {}

        def sum_mod():
            m = state["m"]
            state["m"] += 1
            n, q, k = M[m], m // 8, m % 8
            a = acc[q % 2]
            r = raw[n % RAW]
            s_k = silu_c[:, 2 * k:2 * k + 1]
            if k == 0:
                tk = dve.do(lambda e: e.tensor_scalar(a, r[:, :], s_k, None, ALU.mult), landed(n), t_silu,
                            acc_read.get(q - 2))
            else:
                tk = dve.do(lambda e: e.scalar_tensor_tensor(out=a, in0=r[:, :], scalar=s_k, in1=a,
                                                             op0=ALU.mult, op1=ALU.add),
                            landed(n), state["acc"])
            state["acc"] = tk
            acc_done[q] = tk
            freed[n] = tk

        def split(h):
            n = H[h]
            while state["m"] < len(M) and M[state["m"]] < n:
                sum_mod()
            w, s, r = plan[n][2], h % RING, raw[n % RAW]
            t_hi = act.do(lambda e: e.activation(hi[s][:, 0:w], r[:, 0:w], ACT.Copy), landed(n), used.get(h - RING))
            t_lo = dve.do(lambda e: e.tensor_tensor(lo[s][:, 0:w], r[:, 0:w], hi[s][:, 0:w], ALU.subtract), t_hi)
            ready[h] = t_lo
            freed[n] = t_lo

        def refill():
            for h in state["owed"]:
                if h < len(H):
                    split(h)
            state["owed"] = []

        def feed(body, *after):
            refill()
            h = state["h"]
            state["h"] += 1
            a, b = hi[h % RING], lo[h % RING]
            tk = pe.do(lambda e: body(e, a, b), ready[h], *after)
            used[h] = tk
            state["owed"].append(h + RING)
            return tk

        free = [None] * 8

        def wstat(bank, c0, c1):
            def body(e, a, b):
                for k in range(KT):
                    w1, w2 = a[:, k * P:(k + 1) * P], b[:, k * P:(k + 1) * P]
                    o = ps[bank][:, 0:c1 - c0]
                    e.matmul(o, w1, Th[:, k, c0:c1], start=(k == 0), stop=False)
                    e.matmul(o, w1, Tl[:, k, c0:c1], start=False, stop=False)
                    m = e.matmul(o, w2, Th[:, k, c0:c1], start=False, stop=(k == KT - 1))
                return m
            return body

        def tstat(banks, lhs, n_w, first, last):
            def body(e, a, b):
                for i, tiles in enumerate(lhs):
                    for j, (lh, ll) in enumerate(tiles):
                        nb = len(banks[j])
                        at = [i * nb * n_w + n * n_w for n in range(nb)]
                        f, z = first and i == 0, last and i == len(lhs) - 1
                        for n in range(nb):
                            e.matmul(ps[banks[j][n]][:, 0:n_w], lh, a[:, at[n]:at[n] + n_w], start=f, stop=False)
                        for n in range(nb):
                            e.matmul(ps[banks[j][n]][:, 0:n_w], lh, b[:, at[n]:at[n] + n_w], start=False, stop=False)
                        for n in range(nb):
                            m = e.matmul(ps[banks[j][n]][:, 0:n_w], ll, a[:, at[n]:at[n] + n_w],
                                         start=False, stop=z)
                return m
            return body

        def xt(k, off, i):
            return (Th[:, k, off + i * P:off + (i + 1) * P], Tl[:, k, off + i * P:off + (i + 1) * P])

        half = stat(8)
        t_half = pool.do(lambda e: e.memset(half, -0.5))
        t_ones = dve.do(lambda e: e.memset(ones[:, :], 1.0))
        t_zero = dve.do(lambda e: e.memset(arena[:, 4096:4352], 0.0))

        junk_free = [None, None]
        junk_n = [0]

        def square_sum(src, n, scale, dst, *after):
            i = junk_n[0] % 2
            junk_n[0] += 1
            j = PT[1][:, 2 * i:2 * i + 2, :].rearrange("p a b -> p (a b)")[:, 0:n]
            tk = act.do(lambda e: e.activation(j, src, ACT.Square, scale=scale, accum_out=dst), junk_free[i], *after)
            junk_free[i] = tk
            return tk

        def rsqrt(dst, src, n, *after):
            return pool.do(lambda e: e.tensor_tensor(dst, src, half[:, 0:n], ALU.pow), t_half, *after)

        silu_c = stat(16)
        t_silu = act.do(lambda e: e.activation(silu_c, col("cc"), ACT.Silu), d_cols)

        ss1, v1, r1 = stat(8), stat(4), stat(4)
        srcs = [x[:, 0, :], x[:, 1, :], cx[:, 0, :], cx[:, 1, :]]
        dsts = [xn[:, 0, :], xn[:, 1, :], cx[:, 0, :], cx[:, 1, :]]
        t_xn = []
        for i in range(4):
            d = (d_x + d_cx)[i]
            for n in range(2):
                tk = square_sum(srcs[i][:, n * 512:(n + 1) * 512], 512, 1 / 32, ss1[:, 2 * i + n:2 * i + n + 1], d)
            tk = dve.do(lambda e, i=i: e.tensor_scalar(v1[:, i:i + 1], ss1[:, 2 * i:2 * i + 1],
                                                       ss1[:, 2 * i + 1:2 * i + 2], EPS, ALU.add, ALU.add), tk)
            tk = rsqrt(r1[:, i:i + 1], v1[:, i:i + 1], 1, tk)
            t_xn.append(dve.do(lambda e, i=i: e.tensor_scalar(dsts[i], srcs[i], r1[:, i:i + 1], None, ALU.mult), tk))

        def turn4(k, b):
            def body(e):
                for i in range(4):
                    m = e.transpose(ps[b][:, i * P:(i + 1) * P], dsts[i][:, k * P:(k + 1) * P], ident)
                return m
            return body

        t_turn = {}
        for k in range(7):
            t_turn[k] = pe.do(turn4(k, k), d_cols, *t_xn, free[k])

        def mod_cols(j, n):
            def body(e):
                for k in range(KT):
                    m = e.matmul(ps[7][:, 2 * j:2 * j + 2], raw[n % RAW][:, k * P:(k + 1) * P],
                                 silu_c[:, 2 * k:2 * k + 2], start=(k == 0), stop=(k == KT - 1))
                return m
            return body

        for j in range(16):
            tk = pe.do(mod_cols(j, j), landed(j), t_silu)
            freed[j] = tk
        modc, A1 = stat(32), stat(16)
        b2 = cols[:, COLS["b_sh1"][0]:COLS["b_sh1"][0] + 16]
        tk = dve.do(lambda e: e.tensor_tensor(modc.rearrange("p (j c) -> p j c", c=2),
                                              ps[7][:, 0:32].rearrange("p (j c) -> p j c", c=2),
                                              b2.unsqueeze(2).broadcast_to([P, 16, 2]), ALU.add), tk, d_cols)
        free[7] = tk
        t_mod = dve.do(lambda e: e.scalar_tensor_tensor(
            out=A1.rearrange("p (j c) -> p j c", c=2), in0=modc[:, 16:32].rearrange("p (j c) -> p j c", c=2),
            scalar=1.0, in1=col("g_mix").unsqueeze(2).broadcast_to([P, 8, 2]), op0=ALU.add, op1=ALU.mult), tk)
        t_turn[7] = pe.do(turn4(7, 7), free[7])

        sc_free = [None] * 3
        t_T = []
        for k in range(KT):
            f = sc[k % 3]
            for c in range(2):
                tk = act.do(lambda e, k=k, c=c, f=f: e.activation(
                    f[:, c * L:(c + 1) * L], ps[k][:, c * L:(c + 1) * L], ACT.Identity,
                    bias=modc[:, 2 * k + c:2 * k + c + 1], scale=A1[:, 2 * k + c:2 * k + c + 1]),
                    t_turn[k], t_mod, sc_free[k % 3])
            free[k] = tk
            th = dve.do(lambda e, k=k, f=f: e.tensor_copy(Th[:, k, :], f[:, :]), tk)
            sc_free[k % 3] = dve.do(lambda e, k=k, f=f: e.tensor_tensor(Tl[:, k, :], f[:, :], Th[:, k, :],
                                                                        ALU.subtract), th)
            t_T.append(sc_free[k % 3])
            if k >= 3:
                split(k - 3)
        t_T = t_T[-1]
        extra[16] = [("bias1", arena[:, 0:4096], t["bias1"], t_turn[7])]

        UP = 8 + L + 8
        uT = big[:, 2048:2048 + 4 * UP].rearrange("p (g w) -> p g w", g=4)
        qT = big[:, 3200:4224].rearrange("p (a b) -> p a b", a=4)
        kT = big[:, 4224:6272].rearrange("p (a b) -> p a b", a=4)
        V = big[:, 6272:8320].rearrange("p (a b) -> p a b", a=4)
        t_uz = dve.do(lambda e: e.memset(big[:, 2048:2048 + 4 * UP], 0.0))
        t_u, t_q, t_k = [], [], []
        rot = [0]

        def take(group):
            rot[0] += 1
            return group[rot[0] % len(group)]

        ALL = list(range(8))
        for g in range(4):
            b = take(ALL)
            tk = feed(wstat(b, 0, L), t_T, free[b])
            free[b] = act.do(lambda e, b=b, g=g: e.activation(uT[:, g, 8:8 + L], ps[b][:, 0:L], ACT.Copy), tk, t_uz)
            t_u.append(free[b])
        for a in range(4):
            b = take(ALL)
            tk = feed(wstat(b, 0, 512), t_T, free[b])
            free[b] = act.do(lambda e, b=b, a=a: e.activation(kT[:, a, :], ps[b][:, :], ACT.Copy), tk)
            t_k.append(free[b])

        def mod_row(q, g, t_b, t_g):
            bb = [take(ALL), take(ALL)]

            def body(e):
                for n in range(2):
                    m = e.matmul(ps[bb[n]][:, :], ones[:, :], acc[q % 2][:, n * 512:(n + 1) * 512], start=True,
                                 stop=True)
                return m
            tk = pe.do(body, acc_done[q], t_ones, free[bb[0]], free[bb[1]])
            acc_read[q] = tk
            for n in range(2):
                sl = slice(n * 512, (n + 1) * 512)
                tk2 = dve.do(lambda e, n=n, sl=sl: e.tensor_tensor(g[:, sl], ps[bb[n]][:, :], g[:, sl], ALU.add),
                             tk, t_b)
                free[bb[n]] = tk2
                tk2 = dve.do(lambda e, sl=sl: e.tensor_tensor(g[:, sl], g[:, sl], gp[:, sl], ALU.mult), tk2, t_g)
            return tk2

        def mod_col(q, dst):
            b = take(ALL)

            def body(e):
                for j in range(8):
                    m = e.matmul(ps[b][:, j:j + 1], acc[q % 2][:, j * P:(j + 1) * P], ones[:, 0:1], start=True,
                                 stop=True)
                return m
            tk = pe.do(body, acc_done[q], t_ones, free[b])
            acc_read[q] = tk
            free[b] = dve.do(lambda e: e.tensor_tensor(dst, ps[b][:, 0:8], bias_of[q], ALU.add), tk)
            return free[b]

        bias_of = {1: col("b_sh2"), 2: col("b_sc2")}
        s_g1, s_g2, s_gp = sem("s_g1"), sem("s_g2"), sem("s_gp")
        extra[16].append(("g1", G1[:, :], t["rows"][0:1, :].partition_broadcast(P), s_g1))
        extra[16].append(("gp", gp[:, :], t["rows"][1:2, :].partition_broadcast(P), s_gp))
        extra[16].append(("g2", G2[:, :], t["rows"][2:3, :].partition_broadcast(P), s_g2))

        refill()
        t_G1 = mod_row(0, G1, (s_g1, 16), (s_gp, 16))
        extra[60] = [("gp2", gp[:, :], t["rows"][3:4, :].partition_broadcast(P), s_gp, t_G1)]
        for a in range(4):
            b = take(ALL)
            tk = feed(wstat(b, 0, L), t_T, free[b])
            free[b] = act.do(lambda e, b=b, a=a: e.activation(qT[:, a, :], ps[b][:, 0:L], ACT.Copy, scale=0.125), tk)
            t_q.append(free[b])
        refill()
        sh2 = stat(8)
        t_sh2 = mod_col(1, sh2)
        vb = [take(ALL) for _ in range(4)]
        for j in range(4):
            lhs = [[xt(2 * j + i, 0, 0), xt(2 * j + i, 0, 1), xt(2 * j + i, L, 0), xt(2 * j + i, L, 1)]
                   for i in range(2)]
            tk = feed(tstat([[b] for b in vb], lhs, 512, j == 0, j == 3), *[free[b] for b in vb])
        t_v = []
        for i, b in enumerate(vb):
            free[b] = act.do(lambda e, b=b, i=i: e.activation(V[:, i, :], ps[b][:, :], ACT.Copy), tk)
            t_v.append(free[b])
        refill()

        pw = [big[:, 8320 + i * UP:8320 + (i + 1) * UP] for i in range(4)]
        dT = big[:, 9408:10432].rearrange("p (g w) -> p g w", g=4)
        inv = big[:, 10432:11456].rearrange("p (g w) -> p g w", g=4)
        s_inv = sem("s_inv")
        extra[16].append(("inv", big[:, 10432:11456], t["invcnt"].partition_broadcast(P), s_inv))
        t_pw = dve.do(lambda e: e.memset(big[:, 8320:8320 + 4 * UP], 0.0))
        tk_pool = []
        for g in range(4):
            prev, tk, lo_, hi_ = uT[:, g, :], t_u[g], 1, 0
            for s in range(g + 1):
                a0, a1 = (lo_, hi_) if s == 0 else (1 << (s - 1), 1 << (s - 1))
                o = pw[s]
                c0, c1 = 8, 8 + L
                e0, e1 = (1, UP - 0) if s == 0 else (a0 + 1, UP - a1)
                tk = dve.do(lambda e, o=o, p=prev, e0=e0, e1=e1, a0=a0, a1=a1:
                            e.tensor_tensor(o[:, e0:e1], p[:, e0 - a0:e1 - a0], p[:, e0 + a1:e1 + a1], ALU.add),
                            tk, t_pw)
                prev = o
            tk = dve.do(lambda e, g=g, p=prev: e.tensor_tensor(dT[:, g, :], p[:, 8:8 + L], inv[:, g, :], ALU.mult),
                        tk, (s_inv, 16))
            tk = dve.do(lambda e, g=g: e.tensor_tensor(dT[:, g, :], dT[:, g, :], uT[:, g, 8:8 + L], ALU.subtract), tk)
            t_pw = tk
            tk_pool.append(tk)
        for g in range(4):
            b = take(ALL)
            tk = pe.do(lambda e, b=b, g=g: e.matmul(ps[b][:, 0:L], col("pool_w", g * P, (g + 1) * P), dT[:, g, :],
                                                    start=True, stop=True), tk_pool[g], free[b])
            tk = act.do(lambda e, b=b, g=g: e.activation(Th[:, g, L:], ps[b][:, 0:L], ACT.Copy,
                                                         scale=col("pool_scale", g, g + 1)), tk)
            free[b] = dve.do(lambda e, b=b, g=g: e.scalar_tensor_tensor(
                out=Tl[:, g, L:], in0=ps[b][:, 0:L], scalar=col("pool_scale", g, g + 1), in1=Th[:, g, L:],
                op0=ALU.mult, op1=ALU.subtract), tk)
        t_mixT = [free[b]]

        SB, TB, OB = [0, 1, 2], [3, 4], [5, 6]
        pt_read = [None, None]
        scn = [0]

        def attention(n_heads, tiles, s_mm, s_after, bias, scale, v_of, v_after, out_k):
            items = [(h, i) for h in range(n_heads) for i in range(2)]
            live = {}
            turned = {}
            done = []

            def scores(h, i):
                b = take(SB)
                n = tiles[i]
                s = scn[0] % 3
                scn[0] += 1
                tk = pe.do(lambda e: s_mm(e, ps[b], h, i, n), free[b], *s_after(h))
                m, r, ri = stat(1), stat(1), stat(1)
                tk = dve.do(lambda e: e.tensor_tensor_reduce(
                    out=sc[s][:, 0:n], in0=ps[b][:, 0:n], in1=bias[0](h, i, n), scale=-scale, scalar=3e38,
                    op0=ALU.add, op1=ALU.min, accum_out=m), tk, sc_free[s], *bias[1])
                free[b] = tk
                tk = act.do(lambda e: e.activation(sc[s][:, 0:n], sc[s][:, 0:n], ACT.Exp, bias=m, scale=-1.0,
                                                   accum_out=r), tk)
                tk = dve.do(lambda e: e.reciprocal(ri, r), tk)
                live[(h, i)] = (s, dve.do(lambda e: e.tensor_scalar(sc[s][:, 0:n], sc[s][:, 0:n], ri, None, ALU.mult),
                                          tk))

            def turn(h, i):
                s, tk = live.pop((h, i))
                b = take(TB)
                n = tiles[i] // P

                def body(e):
                    for c in range(n):
                        m = e.transpose(ps[b][:, c * P:(c + 1) * P], sc[s][:, c * P:(c + 1) * P], ident)
                    return m
                tk = pe.do(body, tk, free[b])
                sc_free[s] = tk
                dst = PT[h % 2][:, 0:n, i * P:(i + 1) * P]
                src = ps[b][:, 0:n * P].rearrange("p (c q) -> p c q", c=n)
                if (2 * h + i) % 3 == 2:
                    tk = dve.do(lambda e: e.tensor_copy(dst, src), tk, pt_read[h % 2], *junk_free)
                else:
                    tk = act.do(lambda e: e.activation(dst, src, ACT.Copy), tk, pt_read[h % 2])
                free[b] = tk
                turned[(h, i)] = tk

            def values(h):
                if h % 2 == 0:
                    done.append(take(OB))
                b = done[-1]
                r0 = 64 * (h % 2)
                nk = tiles[1] // P

                def body(e):
                    for c in range(nk):
                        q0 = 0 if c * P < tiles[0] else P
                        m = e.matmul(ps[b][r0:r0 + 64, q0:L], v_of(h, c), PT[h % 2][:, c, q0:L], start=(c == 0),
                                     stop=(c == nk - 1), skip_group_check=True)
                    return m
                tk = pe.do(body, turned[(h, 0)], turned[(h, 1)], free[b], *v_after)
                pt_read[h % 2] = tk
                if h % 2 == 1:
                    k = out_k + h // 2
                    tk = act.do(lambda e: e.activation(Th[:, k, L:], ps[b][:, 0:L], ACT.Copy), tk)
                    free[b] = dve.do(lambda e: e.tensor_tensor(Tl[:, k, L:], ps[b][:, 0:L], Th[:, k, L:],
                                                               ALU.subtract), tk)
                    return free[b]
                return None

            out = None
            for n in range(len(items) + 3):
                if n < len(items):
                    scores(*items[n])
                if 2 <= n < len(items) + 2:
                    turn(*items[n - 2])
                if n >= 3 and items[n - 3][1] == 1:
                    out = values(items[n - 3][0]) or out
            return out

        def s1(e, o, h, i, n):
            r0 = 64 * (h % 2)
            return e.matmul(o[:, 0:n], qT[r0:r0 + 64, h // 2, i * P:(i + 1) * P], kT[r0:r0 + 64, h // 2, 0:n],
                            start=True, stop=True)

        def bias1(h, i, n):
            j = 8 * i + h
            a = arena[:, j * L:4352].rearrange("p (c w) -> p c w", w=L)
            return a[:, 0::(16 - j), :]

        s_b1 = sem("s_bias1")
        t_mixT.append(attention(8, (512, 512), s1, lambda h: (t_q[h // 2], t_k[h // 2]),
                                (bias1, [(s_b1, 16), t_zero]), 1.0, lambda h, c: V[:, c, h * 64:(h + 1) * 64], t_v, 4))
        t_attn1 = t_mixT[-1]
        extra[16][0] = ("bias1", arena[:, 0:4096], t["bias1"], s_b1, t_turn[7])

        ACC = [[0, 1], [2, 3]]
        ROT = [4, 5, 6, 7]
        sc2, A2 = stat(8), stat(8)
        t_sc2 = mod_col(2, sc2)
        t_A2 = dve.do(lambda e: e.scalar_tensor_tensor(out=A2, in0=sc2, scalar=1.0, in1=col("g_mlp"), op0=ALU.add,
                                                       op1=ALU.mult), t_sc2)

        def project_out(after):
            for k in range(8):
                tk = feed(tstat(ACC, [[xt(k, L, 0), xt(k, L, 1)]], 512, k == 0, k == 7),
                          *(after + [free[b] for r in ACC for b in r] if k == 0 else []))
            return tk

        def ssq_psum(after):
            s, v, r = stat(4), stat(2), stat(2)
            tks = []
            for i in range(2):
                for n in range(2):
                    tk = square_sum(ps[ACC[i][n]][:, :], 512, 1 / 32, s[:, 2 * i + n:2 * i + n + 1], after)
                tk = dve.do(lambda e, i=i: e.tensor_scalar(v[:, i:i + 1], s[:, 2 * i:2 * i + 1],
                                                           s[:, 2 * i + 1:2 * i + 2], EPS, ALU.add, ALU.add), tk)
                tks.append(rsqrt(r[:, i:i + 1], v[:, i:i + 1], 1, tk))
            return r, tks

        def add_normed(g, t_g, after):
            r, tks = ssq_psum(after)
            out = []
            for i in range(2):
                for n in range(2):
                    b, sl = ACC[i][n], slice(n * 512, (n + 1) * 512)
                    s = sc[n]
                    tk = dve.do(lambda e, i=i, b=b, sl=sl, s=s: e.scalar_tensor_tensor(
                        out=s[:, :], in0=ps[b][:, :], scalar=r[:, i:i + 1], in1=g[:, sl], op0=ALU.mult,
                        op1=ALU.mult), tks[i], t_g, sc_free[n])
                    free[b] = tk
                    tk = dve.do(lambda e, i=i, sl=sl, s=s: e.tensor_tensor(x[:, i, sl], x[:, i, sl], s[:, :], ALU.add),
                                tk)
                    sc_free[n] = tk
                    out.append(tk)
            return out

        def add_half(after):
            out = []
            for i in range(2):
                for n in range(2):
                    b, sl = ACC[i][n], slice(n * 512, (n + 1) * 512)
                    free[b] = dve.do(lambda e, i=i, b=b, sl=sl: e.scalar_tensor_tensor(
                        out=x[:, i, sl], in0=ps[b][:, :], scalar=0.5, in1=x[:, i, sl], op0=ALU.mult, op1=ALU.add),
                        after)
                    out.append(free[b])
            return out

        def add_plain(after):
            out = []
            for i in range(2):
                for n in range(2):
                    b, sl = ACC[i][n], slice(n * 512, (n + 1) * 512)
                    free[b] = dve.do(lambda e, i=i, b=b, sl=sl: e.tensor_tensor(
                        x[:, i, sl], ps[b][:, :], x[:, i, sl], ALU.add), after)
                    out.append(free[b])
            return out

        def row_stats(t_x):
            s, v, r = stat(4), stat(2), stat(2)
            tks = []
            for i in range(2):
                for n in range(2):
                    tk = square_sum(x[:, i, n * 512:(n + 1) * 512], 512, 1 / 32, s[:, 2 * i + n:2 * i + n + 1],
                                    t_x[2 * i + n])
                tk = dve.do(lambda e, i=i: e.tensor_scalar(v[:, i:i + 1], s[:, 2 * i:2 * i + 1],
                                                           s[:, 2 * i + 1:2 * i + 2], EPS, ALU.add, ALU.add), tk)
                tks.append(rsqrt(r[:, i:i + 1], v[:, i:i + 1], 1, tk))
            return r, tks

        def norm_turn(t_x, gain, shift, *after):
            r, tks = row_stats(t_x)
            t_n = [dve.do(lambda e, i=i: e.tensor_scalar(xn[:, i, :], x[:, i, :], r[:, i:i + 1], None, ALU.mult),
                          tks[i], *after) for i in range(2)]
            for k in range(KT):
                b = take(ALL)

                def body(e, k=k, b=b):
                    for i in range(2):
                        m = e.transpose(ps[b][:, i * P:(i + 1) * P], xn[:, i, k * P:(k + 1) * P], ident)
                    return m
                tk = pe.do(body, *t_n, free[b])
                t_last = tk
                if shift is None:
                    tk = act.do(lambda e, k=k, b=b: e.activation(Th[:, k, 0:L], ps[b][:, 0:L], ACT.Copy,
                                                                 scale=gain[:, k:k + 1]), tk)
                    free[b] = dve.do(lambda e, k=k, b=b: e.scalar_tensor_tensor(
                        out=Tl[:, k, 0:L], in0=ps[b][:, 0:L], scalar=gain[:, k:k + 1], in1=Th[:, k, 0:L],
                        op0=ALU.mult, op1=ALU.subtract), tk)
                    tk = free[b]
                else:
                    f, j = sc[k % 3], k % 3
                    free[b] = act.do(lambda e, k=k, b=b, f=f: e.activation(
                        f[:, 0:L], ps[b][:, 0:L], ACT.Identity, bias=shift[:, k:k + 1], scale=gain[:, k:k + 1]),
                        tk, sc_free[j])
                    tk = dve.do(lambda e, k=k, f=f: e.tensor_copy(Th[:, k, 0:L], f[:, 0:L]), free[b])
                    tk = dve.do(lambda e, k=k, f=f: e.tensor_tensor(Tl[:, k, 0:L], f[:, 0:L], Th[:, k, 0:L],
                                                                    ALU.subtract), tk)
                    sc_free[j] = tk
            return tk, t_last

        tk = project_out([k for k in t_mixT if k])
        t_x = add_normed(G1, t_G1, tk)
        t_T, _ = norm_turn(t_x, A2, sh2, t_A2, t_sh2, t_attn1)

        fbuf = [PT[0][:, i, :] for i in range(4)]
        rbuf = [PT[1][:, i, :] for i in range(4)]
        f_free, r_free = [None] * 4, [None] * 4

        def hidden_parts(f, tk):
            i, j = f % 4, f % 8
            th = act.do(lambda e: e.activation(Th[:, j, L:], fbuf[i], ACT.Copy), tk, down_done.get(f - 8))
            tl = dve.do(lambda e: e.tensor_tensor(Tl[:, j, L:], fbuf[i], Th[:, j, L:], ALU.subtract), th)
            f_free[i] = tl
            return tl

        def down(f, n, t_h):
            j = f % 8
            down_done[f] = feed(tstat(ACC, [[xt(j, L, 0), xt(j, L, 1)]], 512, f == 0, f == n - 1), t_h,
                                *([free[b] for r in ACC for b in r] if f == 0 else []))
            return down_done[f]

        down_done = {}
        hid = {}
        t_G2 = None
        for what, f in mlp_order(FM, MLP_LAG):
            if what == "up":
                b = take(ROT)
                tk = feed(wstat(b, 0, L), t_T, free[b])
                i = f % 4
                free[b] = act.do(lambda e, b=b, i=i: e.activation(rbuf[i], ps[b][:, 0:L], ACT.Relu), tk, r_free[i],
                                 *junk_free)
                tk = dve.do(lambda e, i=i: e.tensor_tensor(fbuf[i], rbuf[i], rbuf[i], ALU.mult), free[b], f_free[i],
                            pt_read[0], pt_read[1])
                r_free[i] = tk
                hid[f] = hidden_parts(f, tk)
            else:
                tk = down(f, FM, hid.pop(f))
                if f == 24:
                    refill()
                    assert state["m"] == 32
                    take_all, ALL[:] = list(ALL), ROT
                    t_G2 = mod_row(3, G2, (s_g2, 16), (s_gp, 32))
                    ALL[:] = take_all
        junk_free[0] = junk_free[1] = r_free[3]
        t_x = add_normed(G2, t_G2, tk)
        extra[130] = [("gp3", gp[:, :], t["rows"][4:5, :].partition_broadcast(P), s_gp, t_G2)]

        def swiglu(gain, t_x):
            t_T, _ = norm_turn(t_x, gain, None)
            down_done.clear()
            for i in range(4):
                r_free[i] = junk_free[1]
            for what, f in mlp_order(F2, FFN_LAG):
                if what == "up":
                    bg, bu, i = take(ROT), take(ROT), f % 4
                    tk = feed(wstat(bg, 0, L), t_T, free[bg])
                    free[bg] = act.do(lambda e, b=bg, i=i: e.activation(rbuf[i], ps[b][:, 0:L], ACT.Silu), tk,
                                      r_free[i], *junk_free)
                    tg = free[bg]
                    tk = feed(wstat(bu, 0, L), t_T, free[bu])
                    free[bu] = dve.do(lambda e, b=bu, i=i: e.tensor_tensor(fbuf[i], rbuf[i], ps[b][:, 0:L], ALU.mult),
                                      tk, tg, f_free[i])
                    r_free[i] = free[bu]
                    hid[f] = hidden_parts(f, free[bu])
                else:
                    tk = down(f, F2, hid.pop(f))
            junk_free[0] = junk_free[1] = r_free[(F2 - 1) % 4]
            return add_half(tk)

        t_x = swiglu(col("g_ffn1"), t_x)

        t_T, t_turned = norm_turn(t_x, col("g_mix2"), None)
        s_bA = sem("s_biasA")
        n0 = next(n for n, c in enumerate(plan) if c[0] == "w_uq")
        extra[n0] = [("biasA", arena[:, 0:4096], t["bias2"], s_bA, t_turned)]
        qTa = big[:, 0:1024].rearrange("p (a b) -> p a b", a=4)
        kTa = big[:, 1024:2048].rearrange("p (a b) -> p a b", a=4)
        Va = big[:, 2048:3072].rearrange("p (a b) -> p a b", a=2)
        qTb = big[:, 3072:5120].rearrange("p (a b) -> p a b", a=8)
        kTb = big[:, 5120:7168].rearrange("p (a b) -> p a b", a=8)
        Vb = big[:, 7168:8192].rearrange("p (a b) -> p a b", a=2)
        qf = big[:, 8192:9728].rearrange("p (t h d) -> p t h d", t=2, h=8)
        kf = big[:, 9728:11264].rearrange("p (t h d) -> p t h d", t=2, h=8)
        ropet = big[:, 11264:11520].rearrange("p (t h d) -> p t h d", t=1, h=8)[:, 0]
        rab = [PT[0][:, 0, :].rearrange("p (h d) -> p h d", h=8), PT[0][:, 1, :].rearrange("p (h d) -> p h d", h=8)]
        qn = [PT[0][:, 2:4, :].rearrange("p a b -> p (a b)"), sc[2][:, :]]
        qn_free = [f_free[3], sc_free[2]]
        sq = [sc[0], sc[1]]
        sq_free = [sc_free[0], sc_free[1]]
        sqn = [0]

        def squares(src, shape, *after):
            i = sqn[0] % 2
            sqn[0] += 1
            n = shape[0] * shape[1]
            o = sq[i][:, 0:n].rearrange("p (h d) -> p h d", h=shape[0])
            return i, o, act.do(lambda e: e.activation(o, src, ACT.Square), sq_free[i], *after)

        def inv_rms(src, n, d, *after):
            v, r = stat(n), stat(n)
            tk = dve.do(lambda e: e.tensor_scalar(v, src, 1.0 / d, EPS, ALU.mult, ALU.add), *after)
            return r, rsqrt(r, v, n, tk)

        cq, sq_t, ck, sk = (big[:, 11520 + 64 * i:11520 + 64 * (i + 1)].rearrange("p (t d) -> p t d", t=2)
                            for i in range(4))
        t_rot = []
        for dst, tab, g in ((cq, "cos2", "g_qr"), (sq_t, "sin2", "g_qr"), (ck, "cos2", "g_kr"), (sk, "sin2", "g_kr")):
            t_rot.append(dve.do(lambda e, dst=dst, tab=tab, g=g: e.tensor_tensor(
                dst, col(tab).rearrange("p (t d) -> p t d", t=2), col(g).unsqueeze(1).broadcast_to([P, 2, 32]),
                ALU.mult), t_attn1))
        t_rot = t_rot[-1]
        gq8 = stat(1)
        t_gq8 = dve.do(lambda e: e.tensor_scalar(gq8, col("g_aq"), 0.125, None, ALU.mult))

        lb = [take(ALL), take(ALL)]
        for j in range(4):
            lhs = [[xt(2 * j + i, 0, 0), xt(2 * j + i, 0, 1)] for i in range(2)]
            tk = feed(tstat([[b] for b in lb], lhs, 416, j == 0, j == 3), t_T, *[free[b] for b in lb])
        t_lat = []
        krn = stat(64)
        qln = [PT[1][:, 0:2, :].rearrange("p a b -> p (a b)")[:, 0:384],
               PT[1][:, 2:4, :].rearrange("p a b -> p (a b)")[:, 0:384]]
        for i in range(2):
            s, v = stat(3), stat(3)
            for n, (c0, c1) in enumerate(((0, 256), (256, 384), (384, 416))):
                j = sqn[0] % 2
                sqn[0] += 1
                tq = act.do(lambda e, i=i, n=n, c0=c0, c1=c1, j=j, s=s: e.activation(
                    sq[j][:, 0:c1 - c0], ps[lb[i]][:, c0:c1], ACT.Square, accum_out=s[:, n:n + 1]), tk, sq_free[j])
                sq_free[j] = tq
            tq = dve.do(lambda e, s=s, v=v: e.tensor_tensor(v, s, col("invd", 0, 3), ALU.mult), tq)
            tq = dve.do(lambda e, v=v: e.tensor_scalar(v, v, EPS, None, ALU.add), tq)
            r = stat(3)
            tq = rsqrt(r, v, 3, tq)
            for n, (c0, c1, dst) in enumerate(((0, 256, qln[i][:, 0:256]), (256, 384, qln[i][:, 256:384]),
                                               (384, 416, krn[:, 32 * i:32 * i + 32]))):
                tn = dve.do(lambda e, i=i, n=n, c0=c0, c1=c1, dst=dst, r=r: e.tensor_scalar(
                    dst, ps[lb[i]][:, c0:c1], r[:, n:n + 1], None, ALU.mult), tq, *junk_free)
            free[lb[i]] = tn
            t_lat.append(tn)

        def qk_rows(dstT, g, t_g, name):
            bb = [take(ALL), take(ALL)]
            for j in range(4):
                lhs = [[xt(2 * j + i, 0, 0), xt(2 * j + i, 0, 1)] for i in range(2)]
                tk = feed(tstat([[b] for b in bb], lhs, 512, j == 0, j == 3), *[free[b] for b in bb])
            return bb, tk

        def qk_norm(bb, tk, dstT, g, t_g):
            tns = []
            for i in range(2):
                b = bb[i]
                j, o, tq = squares(ps[b][:, :].rearrange("p (h d) -> p h d", h=8), (8, 64), tk)
                s = stat(8)
                tq = dve.do(lambda e, o=o, s=s: e.tensor_reduce(s, o, AX_X, ALU.add), tq)
                sq_free[j] = tq
                r, tq = inv_rms(s, 8, 64, tq)
                tn = dve.do(lambda e, i=i, b=b, r=r: e.tensor_tensor(
                    qn[i].rearrange("p (h d) -> p h d", h=8), ps[b][:, :].rearrange("p (h d) -> p h d", h=8),
                    r.unsqueeze(2).broadcast_to([P, 8, 64]), ALU.mult), tq, qn_free[i])
                free[b] = tn
                tns.append(tn)

            def finish():
                out = []
                for i in range(2):
                    b2 = take(ALL)

                    def body(e, i=i, b2=b2):
                        for a in range(4):
                            m = e.transpose(ps[b2][:, a * P:(a + 1) * P], qn[i][:, a * P:(a + 1) * P], ident)
                        return m
                    tt = pe.do(body, tns[i], free[b2])
                    qn_free[i] = tt
                    free[b2] = act.do(lambda e, i=i, b2=b2: e.activation(
                        dstT[:, :, i * P:(i + 1) * P], ps[b2][:, :].rearrange("p (a q) -> p a q", a=4), ACT.Copy,
                        scale=g), tt, t_g, t_attn1)
                    out.append(free[b2])
                return out
            return finish

        bq, tkq = qk_rows(qTa, gq8, t_gq8, "q")
        fin_q = qk_norm(bq, tkq, qTa, gq8, t_gq8)
        t_L = []
        for c, g in ((0, col("g_ql", 0, 1)), (1, col("g_ql", 1, 2)), (2, col("g_kvl"))):
            b = take(ALL)

            def body(e, c=c, b=b):
                for i in range(2):
                    m = e.transpose(ps[b][:, i * P:(i + 1) * P], qln[i][:, c * P:(c + 1) * P], ident)
                return m
            tt = pe.do(body, *t_lat, free[b])
            junk_free[0] = junk_free[1] = tt
            tt = act.do(lambda e, c=c, b=b, g=g: e.activation(Th[:, c, L:], ps[b][:, 0:L], ACT.Copy, scale=g), tt)
            free[b] = dve.do(lambda e, c=c, b=b, g=g: e.scalar_tensor_tensor(
                out=Tl[:, c, L:], in0=ps[b][:, 0:L], scalar=g, in1=Th[:, c, L:], op0=ALU.mult, op1=ALU.subtract), tt)
            t_L.append(free[b])
        t_qa = fin_q()

        ub = [[take(ALL), take(ALL)], [take(ALL), take(ALL)]]
        for k in range(2):
            tk_uq = feed(tstat(ub, [[xt(k, L, 0), xt(k, L, 1)]], 384, k == 0, k == 1), *t_L,
                         *[free[b] for r in ub for b in r])
        refill()
        t_qf = [[], []]
        rope_free = [None]

        def rotate(i, src, cos, sin, heads, dst, *after):
            a, b = (u[:, 0:heads, :] for u in rab)
            ta = dve.do(lambda e: e.tensor_tensor(a, src, cos[:, i, :].unsqueeze(1).broadcast_to([P, heads, 32]),
                                                  ALU.mult), *after, rope_free[0], t_rot)
            tb = dve.do(lambda e: e.tensor_tensor(b, src, sin[:, i, :].unsqueeze(1).broadcast_to([P, heads, 32]),
                                                  ALU.mult), ta)

            def wide(u, c0):
                v = u[:, :, c0:c0 + 16]
                return v.broadcast_to([P, 8, 16]) if heads == 1 else v
            t1 = dve.do(lambda e: e.tensor_tensor(dst[:, :, 64:80], wide(a, 0), wide(b, 16), ALU.subtract), tb)
            rope_free[0] = dve.do(lambda e: e.tensor_tensor(dst[:, :, 80:96], wide(b, 0), wide(a, 16), ALU.add), t1)
            return rope_free[0]

        for i in range(2):
            for n in range(2):
                b = ub[i][n]
                j, o, tq = squares(ps[b][:, 0:384].rearrange("p (h d) -> p h d", h=4), (4, 96), tk_uq)
                s1_, s2_ = stat(4), stat(4)
                dve.do(lambda e, o=o, s=s1_: e.tensor_reduce(s, o[:, :, 0:64], AX_X, ALU.add), tq)
                tq = dve.do(lambda e, o=o, s=s2_: e.tensor_reduce(s, o[:, :, 64:96], AX_X, ALU.add), tq)
                sq_free[j] = tq
                v = stat(8)
                dve.do(lambda e, v=v, s=s1_: e.tensor_scalar(v[:, 0:4], s, 1 / 64, EPS, ALU.mult, ALU.add), tq)
                tq = dve.do(lambda e, v=v, s=s2_: e.tensor_scalar(v[:, 4:8], s, 1 / 32, EPS, ALU.mult, ALU.add), tq)
                r = stat(8)
                tq = rsqrt(r, v, 8, tq)
                src = ps[b][:, 0:384].rearrange("p (h d) -> p h d", h=4)
                t_qf[i].append(dve.do(lambda e, i=i, n=n, src=src, r=r: e.tensor_tensor(
                    qf[:, i, 4 * n:4 * n + 4, 0:64], src[:, :, 0:64], r[:, 0:4].unsqueeze(2).broadcast_to([P, 4, 64]),
                    ALU.mult), tq))
                tq = dve.do(lambda e, n=n, src=src, r=r: e.tensor_tensor(
                    ropet[:, 4 * n:4 * n + 4, :], src[:, :, 64:96], r[:, 4:8].unsqueeze(2).broadcast_to([P, 4, 32]),
                    ALU.mult), tq, rope_free[0])
                free[b] = tq
            t_qf[i].append(rotate(i, ropet, cq, sq_t, 8, qf[:, i], tq))
        kb = [[take(ALL), take(ALL)], [take(ALL), take(ALL)]]
        tk_kv = feed(tstat(kb, [[xt(2, L, 0), xt(2, L, 1)]], 512, True, True), *[free[b] for r in kb for b in r])
        refill()
        t_kf, t_vb = [[], []], []
        for i in range(2):
            for n in range(2):
                b = kb[i][n]
                src = ps[b][:, :].rearrange("p (h d) -> p h d", h=4)
                j, o, tq = squares(src[:, :, 0:64], (4, 64), tk_kv)
                tv = act.do(lambda e, i=i, n=n, src=src: e.activation(
                    Vb[:, i, n * 256:(n + 1) * 256].rearrange("p (h d) -> p h d", h=4), src[:, :, 64:128], ACT.Copy))
                t_vb.append(tv)
                s = stat(4)
                tq = dve.do(lambda e, o=o, s=s: e.tensor_reduce(s, o, AX_X, ALU.add), tq)
                sq_free[j] = tq
                r, tq = inv_rms(s, 4, 64, tq)
                free[b] = dve.do(lambda e, i=i, n=n, src=src, r=r: e.tensor_tensor(
                    kf[:, i, 4 * n:4 * n + 4, 0:64], src[:, :, 0:64], r.unsqueeze(2).broadcast_to([P, 4, 64]),
                    ALU.mult), tq, tv)
                t_kf[i].append(free[b])
            t_kf[i].append(rotate(i, krn[:, 32 * i:32 * i + 32].unsqueeze(1), ck, sk, 1, kf[:, i], t_lat[i]))

        bk_, tkk = qk_rows(kTa, col("g_ak"), None, "k")
        fin_k = qk_norm(bk_, tkk, kTa, col("g_ak"), None)
        vbk = [take(ALL), take(ALL)]
        for j in range(4):
            lhs = [[xt(2 * j + i, 0, 0), xt(2 * j + i, 0, 1)] for i in range(2)]
            tk = feed(tstat([[b] for b in vbk], lhs, 512, j == 0, j == 3), *[free[b] for b in vbk])
        t_va = []
        for i, b in enumerate(vbk):
            free[b] = act.do(lambda e, b=b, i=i: e.activation(Va[:, i, :], ps[b][:, :], ACT.Copy), tk)
            t_va.append(free[b])
        refill()
        t_ka = fin_k()
        t_qb, t_kb = [], []
        for src, dst, g, tin, tout in ((qf, qTb, "g_bq", t_qf, t_qb), (kf, kTb, "g_bk", t_kf, t_kb)):
            for i in range(2):
                for n in range(2):
                    b = take(ALL)

                    def body(e, src=src, i=i, n=n, b=b):
                        for h in range(4):
                            m = e.transpose(ps[b][0:96, h * P:(h + 1) * P], src[:, i, 4 * n + h, :], ident)
                        return m
                    tt = pe.do(body, *tin[i], free[b])
                    o = dst[0:96, 4 * n:4 * n + 4, i * P:(i + 1) * P]
                    v = ps[b][0:96, :].rearrange("p (h q) -> p h q", h=4)
                    gc = cols[0:96, COLS[g][0]:COLS[g][0] + 1]
                    if n == 0:
                        free[b] = act.do(lambda e, o=o, v=v, gc=gc: e.activation(o, v, ACT.Copy, scale=gc), tt)
                    else:
                        free[b] = dve.do(lambda e, o=o, v=v, gc=gc: e.tensor_scalar(o, v, gc, None, ALU.mult), tt)
                    tout.append(free[b])

        for i in range(3):
            sc_free[i] = [sq_free[0], sq_free[1], qn_free[1]][i]
        t_rope = rope_free[0]
        pt_read[0], pt_read[1] = t_rope, None

        def sA(e, o, h, i, n):
            r0 = 64 * (h % 2)
            return e.matmul(o[:, 0:n], qTa[r0:r0 + 64, h // 2, i * P:(i + 1) * P], kTa[r0:r0 + 64, h // 2, 0:n],
                            start=True, stop=True)

        def sB(e, o, h, i, n):
            return e.matmul(o[:, 0:n], qTb[0:96, h, i * P:(i + 1) * P], kTb[0:96, h, 0:n], start=True, stop=True)

        def biasA(h, i, n):
            j = 8 * i + h
            return arena[:, j * L:j * L + n]

        mask = col("mask").rearrange("p (t w) -> p t w", t=2)
        mixA = attention(8, (128, 256), sA, lambda h: (*t_qa, *t_ka), (biasA, [(s_bA, 16)]), 1.0,
                         lambda h, c: Va[:, c, h * 64:(h + 1) * 64], t_va, 0)
        mixB = attention(8, (128, 256), sB, lambda h: (*t_qb, *t_kb), (lambda h, i, n: mask[:, i, 0:n], [d_cols]),
                         float(96 ** -0.5), lambda h, c: Vb[:, c, h * 64:(h + 1) * 64], t_vb, 4)
        tk = project_out([mixA, mixB])
        t_x = add_plain(tk)
        for i in range(4):
            f_free[i] = pt_read[0]
            r_free[i] = pt_read[1]
        junk_free[0] = junk_free[1] = pt_read[1]
        t_x = swiglu(col("g_ffn2"), t_x)

        r, tks = row_stats(t_x)
        s_out = sem("s_out")
        for i in range(2):
            tk = dve.do(lambda e, i=i: e.scalar_tensor_tensor(out=xn[:, i, :], in0=x[:, i, :], scalar=r[:, i:i + 1],
                                                              in1=gp[:, :], op0=ALU.mult, op1=ALU.mult),
                        tks[i], (s_gp, 48))
            out_after = tk
            extra.setdefault("end", []).append((i, tk))

        assert state["h"] == len(H), (state["h"], len(H))

        for n, (name, j, w, kind) in enumerate(plan):
            for item in extra.get(n, ()):
                dst, src, s = item[1], item[2], item[3]
                sp.go(lambda e, dst=dst, src=src, s=s: e.dma_start(dst, src).then_inc(s, 16), *item[4:])
            sp.go(lambda e, n=n, name=name, j=j, w=w: e.dma_start(raw[n % RAW][:, 0:w], t[name][j, :, :])
                  .then_inc(s_raw[n % RAW], 16), freed.get(n - RAW))
        for i, tk in extra["end"]:
            sp.go(lambda e, i=i: e.dma_start(t["out"][i * P:(i + 1) * P, :], xn[:, i, :]).then_inc(s_out, 16), tk)

        block = ctx.enter_context(nc.Block())

        @block.sync
        def _(e):
            sp.play(e)
            e.wait_ge(s_out, 32)

        @block.scalar
        def _(e):
            act.play(e)

        @block.vector
        def _(e):
            dve.play(e)

        @block.gpsimd
        def _(e):
            pool.play(e)

        @block.tensor
        def _(e):
            pe.play(e)


def _column(v):
    return v.reshape(-1, P).T


def _tiles(w):
    k, j = w.shape[0] // P, w.shape[1] // P
    return np.ascontiguousarray(w.reshape(k, P, j, P).transpose(2, 1, 0, 3).reshape(j, P, k * P))


def _rows(w):
    return np.ascontiguousarray(w.reshape(-1, P, w.shape[1]))


def _row_pairs(w):
    k, c = w.shape[0] // P, w.shape[1]
    return np.ascontiguousarray(w.reshape(k // 2, 2, P, c).transpose(0, 2, 1, 3).reshape(k // 2, P, 2 * c))


def _bias1(rpb):
    out = np.full((8, 4, 64, 4, 64), NEG, np.float32)
    qc = np.arange(64)
    start = np.clip(qc - 8, 0, 48)
    for qr in range(4):
        for kr in range(4):
            for c in range(64):
                k0 = start[c]
                out[:, qr, c, kr, k0:k0 + 16] = rpb[:, kr - qr + 7, k0 - c + 15:k0 - c + 31]
    return np.ascontiguousarray(out.reshape(8, 2, P, L).transpose(2, 1, 0, 3).reshape(P, 2 * 8 * L))


def _bias2(rb):
    i, j = np.arange(L)[:, None], np.arange(L)[None, :]
    rel = np.clip(i - j, -128, 128) + 128
    out = np.where((j // 64 <= i // 64)[None], rb[:, rel], np.float32(NEG)).astype(np.float32)
    return np.ascontiguousarray(out.reshape(8, 2, P, L).transpose(2, 1, 0, 3).reshape(P, 2 * 8 * L))


def _shape_tables():
    i, j = np.arange(L)[:, None], np.arange(L)[None, :]
    mask = np.where(j // 64 <= i // 64, 0.0, NEG).astype(np.float32)
    mask = mask.reshape(2, P, L).transpose(1, 0, 2).reshape(P, 2 * L)
    inv = 1.0 / (10000.0 ** (np.arange(0, 32, 2, dtype=np.float32) / np.float32(32)))
    ang = np.arange(L, dtype=np.float32)[:, None] * inv.astype(np.float32)[None, :]

    def twice(a):
        a = np.concatenate([a, a], axis=1).astype(np.float32)
        return a.reshape(2, P, 32).transpose(1, 0, 2).reshape(P, 64)
    t = np.arange(L)
    cnt = [np.clip(t + w - w // 2, 0, L) - np.clip(t - w // 2, 0, L) for w in (2, 4, 8, 16)]
    invcnt = (1.0 / np.stack(cnt).astype(np.float32)).astype(np.float32).reshape(1, 4 * L)
    invd = np.zeros((P, 16), np.float32)
    invd[:, 0:3] = [1 / 256, 1 / 128, 1 / 32]
    return mask, twice(np.cos(ang)), twice(np.sin(ang)), invcnt, invd


def kernel(**inputs):
    import concourse.bacc as bacc
    from concourse.bass_utils import run_bass_kernel_spmd

    v = {k: np.asarray(a) for k, a in inputs.items()}
    mask, cos2, sin2, invcnt, invd = _shape_tables()
    ones32 = np.ones(32, np.float32)
    w_mod, b_mod, w_in = v["w_mod"][0], v["b_mod"][0], v["w_in"][0]
    w_in2 = v["w_in_2"][0]
    cc = np.stack([_column(v["c"][0]), _column(v["c_ctx"])], axis=2).reshape(P, 16)
    parts = {
        "ident": np.eye(P, dtype=np.float32), "cc": cc,
        "b_sh1": _column(b_mod[0:1024]), "b_sc1": _column(b_mod[1024:2048]),
        "b_sh2": _column(b_mod[3072:4096]), "b_sc2": _column(b_mod[4096:5120]),
        "g_mix": _column(v["g_pre_mix"][0]), "g_mlp": _column(v["g_pre_mlp"][0]),
        "pool_scale": _column(v["pool_scale"][0]), "g_ffn1": _column(v["ffn1_norm_2"][0]),
        "g_mix2": _column(v["mix_norm_2"][0]), "g_ffn2": _column(v["ffn2_norm_2"][0]),
        "g_aq": np.tile(v["a_q_norm_2"][0], 2)[:, None], "g_ak": np.tile(v["a_k_norm_2"][0], 2)[:, None],
        "g_bq": np.concatenate([v["b_q_nope_norm_2"][0], ones32, ones32])[:, None],
        "g_bk": np.concatenate([v["b_k_nope_norm_2"][0], ones32, ones32])[:, None],
        "g_ql": _column(v["b_q_lat_norm_2"][0]), "g_kvl": _column(v["b_kv_lat_norm_2"][0]),
        "g_qr": np.broadcast_to(v["b_q_rope_norm_2"][0], (P, 32)),
        "g_kr": np.broadcast_to(v["b_k_rope_norm_2"][0], (P, 32)),
        "cos2": cos2, "sin2": sin2, "invd": invd, "mask": mask,
        "pool_w": v["pool_w"][0].transpose(1, 0, 2).reshape(P, 512),
    }
    arrays = {
        "cols": np.ascontiguousarray(np.concatenate([parts[k] for k in COLS], axis=1)),
        "x": v["x"][0], "ctx": v["ctx"][0],
        "rows": np.stack([b_mod[2048:3072], v["g_post_mix"][0], b_mod[5120:6144], v["g_post_mlp"][0],
                          v["final_norm_2"][0]]),
        "invcnt": invcnt, "bias1": _bias1(v["rpb"][0]), "bias2": _bias2(v["a_rel_bias_2"][0]),
        "w_mod_c": _tiles(w_mod[:, 0:2048]),
        "w_mod_r": np.concatenate([_rows(w_mod[:, a:a + 1024]) for a in (2048, 3072, 4096, 5120)]),
        "w_in_u": _tiles(w_in[:, 0:512]), "w_in_q": _tiles(w_in[:, 512:1024]),
        "w_in_k": _tiles(w_in[:, 1024:1536]), "w_in_v": _row_pairs(w_in[:, 1536:2048]),
        "w_out": _rows(v["w_out"][0]), "w_mlp_in": _tiles(v["w_mlp_in"][0]), "w_mlp_out": _rows(v["w_mlp_out"][0]),
        "w_in2_q": _row_pairs(w_in2[:, 0:512]), "w_in2_k": _row_pairs(w_in2[:, 512:1024]),
        "w_in2_v": _row_pairs(w_in2[:, 1024:1536]), "w_in2_l": _row_pairs(w_in2[:, 1536:1952]),
        "w_uq": _rows(v["b_w_uq_2"][0]), "w_ukv": _rows(v["b_w_ukv_2"][0]), "w_out2": _rows(v["w_out_2"][0]),
    }
    for a in ("ffn1", "ffn2"):
        arrays[a + "_gate"] = _tiles(v[a + "_w_gate_2"][0])
        arrays[a + "_up"] = _tiles(v[a + "_w_up_2"][0])
        arrays[a + "_down"] = _rows(v[a + "_w_down_2"][0])
    arrays = {k: np.ascontiguousarray(a) for k, a in arrays.items()}

    nc = bacc.Bacc("TRN2", target_bir_lowering=False, num_devices=1)
    t = {k: nc.dram_tensor("in_" + k, a.shape, F32, kind="ExternalInput").ap() for k, a in arrays.items()}
    t["out"] = nc.dram_tensor("out_0", (L, D), F32, kind="ExternalOutput").ap()
    build(nc, t)
    res = run_bass_kernel_spmd(nc, [{"in_" + k: a for k, a in arrays.items()}], core_ids=[0])
    return res.results[0]["out_0"].reshape(1, L, D)
```

```python
from contextlib import ExitStack

import numpy as np

import concourse.bass as bass
from concourse import mybir

F32 = mybir.dt.float32
F32R = mybir.dt.float32r
ALU = mybir.AluOpType
ACT = mybir.ActivationFunctionType
AX_X = mybir.AxisListType.X

P = 128
D = 1024
KT = D // P
L = 256
FM = 32
F2 = 22
EPS = 1e-6
NEG = -1e30
W = 1024
RAW = 7
RING = 5

COLS = {}
_at = 0
for _name, _n in [("ident", 128), ("cc", 16), ("b_sh1", 8), ("b_sc1", 8), ("b_sh2", 8), ("b_sc2", 8),
                  ("g_mix", 8), ("g_mlp", 8), ("pool_scale", 4), ("g_ffn1", 8), ("g_mix2", 8), ("g_ffn2", 8),
                  ("g_aq", 1), ("g_ak", 1), ("g_bq", 1), ("g_bk", 1), ("g_ql", 2), ("g_kvl", 1),
                  ("invd", 16), ("pool_w", 512), ("mask", 512), ("g_qr", 32), ("g_kr", 32), ("cos2", 64),
                  ("sin2", 64)]:
    COLS[_name] = (_at, _n)
    _at += _n
NCOLS = _at
EARLY = COLS["pool_w"][0]


TAIL = 4


def mlp_order(n, lag):
    out, done = [], 0
    for f in range(n):
        out.append(("up", f))
        if lag <= f and done < n - TAIL:
            out.append(("down", done))
            done += 1
    return out + [("down", f) for f in range(done, n)]


MLP_LAG = 2
FFN_LAG = 1


def stream_plan():
    s = [("w_mod_c", j, 1024, "C") for j in range(16)]
    h = [("w_in_u", j, 1024, "H") for j in range(4)] + [("w_in_q", j, 1024, "H") for j in range(4)]
    h += [("w_in_k", j, 1024, "H") for j in range(4)] + [("w_in_v", j, 1024, "H") for j in range(4)]
    m = [("w_mod_r", j, 1024, "M") for j in range(32)]
    s += h[:5]
    mi = 0
    for c in h[5:]:
        s += m[mi:mi + 2]
        mi += 2
        s.append(c)
    s += m[mi:24]
    mi = 24
    s += [("w_out", k, 1024, "H") for k in range(8)]
    for n, (what, f) in enumerate(mlp_order(FM, MLP_LAG)):
        s.append(("w_mlp_in" if what == "up" else "w_mlp_out", f, 1024, "H"))
        if n >= 4 and n % 2 == 0 and mi < 32:
            s.append(m[mi])
            mi += 1

    def ffn(a):
        for what, f in mlp_order(F2, FFN_LAG):
            if what == "up":
                s.append((a + "_gate", f, 1024, "H"))
                s.append((a + "_up", f, 1024, "H"))
            else:
                s.append((a + "_down", f, 1024, "H"))

    ffn("ffn1")
    s.extend(("w_in2_l", j, 832, "H") for j in range(4))
    s.extend(("w_in2_q", j, 1024, "H") for j in range(4))
    s.extend(("w_in2_k", j, 1024, "H") for j in range(4))
    s.extend(("w_uq", j, 768, "H") for j in range(2))
    s.extend(("w_in2_v", j, 1024, "H") for j in range(4))
    s.append(("w_ukv", 0, 1024, "H"))
    s.extend(("w_out2", k, 1024, "H") for k in range(8))
    ffn("ffn2")
    return s


class Queue:

    def __init__(self, sem):
        self.sem, self.n, self.items = sem, 0, []

    def do(self, fn, *after):
        self.n += 1
        self.items.append((fn, after, True))
        return (self.sem, self.n)

    def go(self, fn, *after):
        self.items.append((fn, after, False))

    def play(self, eng):
        passed = {}
        for fn, after, counts in self.items:
            for w in after:
                if w is not None and passed.get(w[0].name, 0) < w[1]:
                    eng.wait_ge(w[0], w[1])
                    passed[w[0].name] = w[1]
            ins = fn(eng)
            if counts:
                ins.then_inc(self.sem, 1)


def build(nc, t):
    ctx = ExitStack()
    with ctx:
        def sb(name, shape, dt=F32):
            return ctx.enter_context(nc.sbuf_tensor(name, shape, dt))

        def sem(name):
            return ctx.enter_context(nc.semaphore(name))

        raw = [sb(f"raw{i}", [P, W]) for i in range(RAW)]
        hi = [sb(f"hi{i}", [P, W], F32R) for i in range(RING)]
        lo = [sb(f"lo{i}", [P, W], F32R) for i in range(RING)]
        x = sb("x", [P, 2, D])
        arena = sb("arena", [P, 4096 + 256])
        Th = sb("Th", [P, KT, 512], F32R)
        Tl = sb("Tl", [P, KT, 512], F32R)
        G1 = sb("G1", [P, D])
        G2 = sb("G2", [P, D])
        gp = sb("gp", [P, D])
        cols = sb("cols", [P, NCOLS])
        sc = [sb(f"sc{i}", [P, 512]) for i in range(3)]
        PT = [sb(f"PT{i}", [P, 4, L]) for i in range(2)]
        big = sb("big", [P, 11776])
        st = sb("st", [P, 1152])
        ones = sb("ones", [P, P])
        ps = [ctx.enter_context(nc.psum_tensor(f"ps{i}", [P, 512], F32)) for i in range(8)]

        pe, act, dve, pool, sp = (Queue(sem("s_" + n)) for n in ("pe", "act", "dve", "pool", "sp"))
        s_raw = [sem(f"s_raw{i}") for i in range(RAW)]

        def col(name, a=0, b=None):
            at, n = COLS[name]
            return cols[:, at + a:at + (n if b is None else b)]

        ident = col("ident")
        xn = arena[:, 0:2048].rearrange("p (t d) -> p t d", t=2)
        cx = arena[:, 2048:4096].rearrange("p (t d) -> p t d", t=2)
        stat_at = [0]

        def stat(n):
            a = stat_at[0]
            stat_at[0] += n
            assert stat_at[0] <= 1152
            return st[:, a:a + n]

        def load(name, dst, src, *after):
            s = sem("s_" + name)
            sp.go(lambda e: e.dma_start(dst, src).then_inc(s, 16), *after)
            return (s, 16)

        d_cols = load("cols", cols[:, 0:EARLY], t["cols"][:, 0:EARLY])

        plan = stream_plan()
        freed = {}
        H = [n for n, c in enumerate(plan) if c[3] == "H"]
        used, ready = {}, {}
        state = {"h": 0, "m": 0, "split": 0, "owed": [], "acc": None}
        extra = {}

        def landed(n):
            return (s_raw[n % RAW], 16 * (n // RAW + 1))

        M = [n for n, c in enumerate(plan) if c[3] == "M"]
        acc = [big[:, 0:1024], big[:, 1024:2048]]
        acc_read = {}
        acc_done = {}

        def sum_mod():
            m = state["m"]
            state["m"] += 1
            n, q, k = M[m], m // 8, m % 8
            a = acc[q % 2]
            r = raw[n % RAW]
            s_k = silu_c[:, 2 * k:2 * k + 1]
            if k == 0:
                tk = dve.do(lambda e: e.tensor_scalar(a, r[:, :], s_k, None, ALU.mult), landed(n), t_silu,
                            acc_read[q - 2])
            else:
                tk = dve.do(lambda e: e.scalar_tensor_tensor(out=a, in0=r[:, :], scalar=s_k, in1=a,
                                                             op0=ALU.mult, op1=ALU.add),
                            landed(n), state["acc"])
            state["acc"] = tk
            acc_done[q] = tk
            freed[n] = tk

        def split(h):
            n = H[h]
            while state["m"] < len(M) and M[state["m"]] < n:
                sum_mod()
            w, s, r = plan[n][2], h % RING, raw[n % RAW]
            t_hi = act.do(lambda e: e.activation(hi[s][:, 0:w], r[:, 0:w], ACT.Copy), landed(n), used.get(h - RING))
            t_lo = dve.do(lambda e: e.tensor_tensor(lo[s][:, 0:w], r[:, 0:w], hi[s][:, 0:w], ALU.subtract), t_hi)
            ready[h] = t_lo
            freed[n] = t_lo

        def refill():
            for h in state["owed"]:
                if h < len(H):
                    split(h)
            state["owed"] = []

        def feed(body, *after):
            refill()
            h = state["h"]
            state["h"] += 1
            return last_part(h, body, *after)

        def part(h, body, *after):
            a, b = hi[h % RING], lo[h % RING]
            return pe.do(lambda e: body(e, a, b), ready[h], *after)

        def last_part(h, body, *after):
            used[h] = part(h, body, *after)
            state["owed"].append(h + RING)
            return used[h]

        def feed_by_k(body_k, waits):
            refill()
            h = state["h"]
            state["h"] += 1
            a, b = hi[h % RING], lo[h % RING]
            for k in range(KT - 1):
                pe.go(lambda e, k=k: body_k(e, a, b, k), ready[h], *waits[k])
            used[h] = pe.do(lambda e: body_k(e, a, b, KT - 1), *waits[KT - 1])
            state["owed"].append(h + RING)
            return used[h]

        free = [None] * 8

        def wstat(bank, c0, c1):
            def body(e, a, b):
                for k in range(KT):
                    m = wstat_k(bank, c0, c1)(e, a, b, k)
                return m
            return body

        def wstat_k(bank, c0, c1):
            def body(e, a, b, k):
                w1, w2 = a[:, k * P:(k + 1) * P], b[:, k * P:(k + 1) * P]
                o = ps[bank][:, 0:c1 - c0]
                e.matmul(o, w1, Th[:, k, c0:c1], start=(k == 0), stop=False)
                e.matmul(o, w1, Tl[:, k, c0:c1], start=False, stop=False)
                return e.matmul(o, w2, Th[:, k, c0:c1], start=False, stop=(k == KT - 1))
            return body

        def tstat(banks, lhs, n_w, first, last):
            def body(e, a, b):
                for i, tiles in enumerate(lhs):
                    for j, (lh, ll) in enumerate(tiles):
                        nb = len(banks[j])
                        at = [i * nb * n_w + n * n_w for n in range(nb)]
                        f, z = first and i == 0, last and i == len(lhs) - 1
                        for n in range(nb):
                            e.matmul(ps[banks[j][n]][:, 0:n_w], lh, a[:, at[n]:at[n] + n_w], start=f, stop=False)
                        for n in range(nb):
                            e.matmul(ps[banks[j][n]][:, 0:n_w], lh, b[:, at[n]:at[n] + n_w], start=False, stop=False)
                        for n in range(nb):
                            m = e.matmul(ps[banks[j][n]][:, 0:n_w], ll, a[:, at[n]:at[n] + n_w],
                                         start=False, stop=z)
                return m
            return body

        def xt(k, off, i):
            return (Th[:, k, off + i * P:off + (i + 1) * P], Tl[:, k, off + i * P:off + (i + 1) * P])

        half = stat(8)
        t_half = pool.do(lambda e: e.memset(half, -0.5))
        t_ones = dve.do(lambda e: e.memset(ones[:, :], 1.0))
        t_zero = dve.do(lambda e: e.memset(arena[:, 4096:4352], 0.0))

        junk_free = [None, None]
        junk_n = [0]

        def square_sum(src, n, scale, dst, *after):
            i = junk_n[0] % 2
            junk_n[0] += 1
            j = PT[1][:, 2 * i:2 * i + 2, :].rearrange("p a b -> p (a b)")[:, 0:n]
            tk = act.do(lambda e: e.activation(j, src, ACT.Square, scale=scale, accum_out=dst), junk_free[i], *after)
            junk_free[i] = tk
            return tk

        def rsqrt(dst, src, n, *after):
            return pool.do(lambda e: e.tensor_tensor(dst, src, half[:, 0:n], ALU.pow), t_half, *after)

        silu_c = stat(16)
        t_silu = act.do(lambda e: e.activation(silu_c, col("cc"), ACT.Silu), d_cols)

        def mod_row_products(n):
            k, hf = n // 2, n % 2

            def body(e):
                for m in range(2):
                    i = e.matmul(ps[2 * hf + m][0:2, :], silu_c[:, 2 * k:2 * k + 2],
                                 raw[n % RAW][:, m * 512:(m + 1) * 512], start=(k == 0), stop=(k == KT - 1))
                return i
            freed[n] = pe.do(body, landed(n), t_silu)
            return freed[n]

        s_x, s_cx, s_late = sem("s_x"), sem("s_cx"), sem("s_late")
        extra[2] = [("x", x[:, :, :], t["x"].rearrange("(i p) d -> p i d", p=P), s_x)]
        extra[5] = [("cx", cx, t["ctx"].rearrange("(i p) d -> p i d", p=P), s_cx)]
        ss1, v1, r1 = stat(8), stat(4), stat(4)
        srcs = [x[:, 0, :], x[:, 1, :], cx[:, 0, :], cx[:, 1, :]]
        dsts = [xn[:, 0, :], xn[:, 1, :], cx[:, 0, :], cx[:, 1, :]]
        xT = big[:, 6272:10368].rearrange("p (k w) -> p k w", k=KT)
        t_xn = []
        for i in range(4):
            d = ((s_x, 16), (s_cx, 16))[i // 2]
            for n in range(2):
                tk = square_sum(srcs[i][:, n * 512:(n + 1) * 512], 512, 1 / 32, ss1[:, 2 * i + n:2 * i + n + 1], d)
            tk = dve.do(lambda e, i=i: e.tensor_scalar(v1[:, i:i + 1], ss1[:, 2 * i:2 * i + 1],
                                                       ss1[:, 2 * i + 1:2 * i + 2], EPS, ALU.add, ALU.add), tk)
            tk = rsqrt(r1[:, i:i + 1], v1[:, i:i + 1], 1, tk)
            t_xn.append(dve.do(lambda e, i=i: e.tensor_scalar(dsts[i], srcs[i], r1[:, i:i + 1], None, ALU.mult), tk))

        t_xT = {}
        turned1 = []

        def turn_rows(c, k, b):
            def body(e):
                for j in range(2):
                    for i in range(2):
                        m = e.transpose(ps[b][:, (2 * j + i) * P:(2 * j + i + 1) * P],
                                        dsts[2 * c + i][:, (k + j) * P:(k + j + 1) * P], ident)
                return m
            tk = pe.do(body, d_cols, *t_xn[2 * c:2 * c + 2], free[b])
            turned1.append(tk)
            dst = xT[:, k:k + 2, c * L:(c + 1) * L]
            src = ps[b][:, :].rearrange("p (j w) -> p j w", j=2)
            if k % 4 == 0:
                tk = act.do(lambda e: e.activation(dst, src, ACT.Copy), tk)
            else:
                tk = dve.do(lambda e: e.tensor_copy(dst, src), tk)
            free[b] = tk
            t_xT[(c, k)] = t_xT[(c, k + 1)] = tk

        for n in range(16):
            t_row = mod_row_products(n)
            if n in (7, 8, 9, 10):
                turn_rows(0, 2 * (n - 7), 4 + (n - 7) % 4)
            if n in (11, 12, 13, 14):
                turn_rows(1, 2 * (n - 11), 4 + (n - 11) % 4)
        t_turn1 = turned1[-1]

        modr = big[0:2, 0:2048]
        t_mr = []
        for m in range(4):
            o = modr[:, m * 512:(m + 1) * 512]
            if m % 2 == 0:
                free[m] = act.do(lambda e, o=o, m=m: e.activation(o, ps[m][0:2, :], ACT.Copy), t_row)
            else:
                free[m] = dve.do(lambda e, o=o, m=m: e.tensor_copy(o, ps[m][0:2, :]), t_row)
            t_mr.append(free[m])

        def turn_mod(e):
            for j in range(16):
                m = e.transpose(ps[4][:, 2 * j:2 * j + 2], modr[:, j * P:(j + 1) * P], ident[0:2, 0:2])
            return m
        t_modT = pe.do(turn_mod, *t_mr, free[4])
        acc_read[-2] = acc_read[-1] = t_modT
        modc, A1 = stat(32), stat(16)
        b2 = cols[:, COLS["b_sh1"][0]:COLS["b_sh1"][0] + 16]
        tk = dve.do(lambda e: e.tensor_tensor(modc.rearrange("p (j c) -> p j c", c=2),
                                              ps[4][:, 0:32].rearrange("p (j c) -> p j c", c=2),
                                              b2.unsqueeze(2).broadcast_to([P, 16, 2]), ALU.add), t_modT)
        free[4] = tk
        t_mod = dve.do(lambda e: e.scalar_tensor_tensor(
            out=A1.rearrange("p (j c) -> p j c", c=2), in0=modc[:, 16:32].rearrange("p (j c) -> p j c", c=2),
            scalar=1.0, in1=col("g_mix").unsqueeze(2).broadcast_to([P, 8, 2]), op0=ALU.add, op1=ALU.mult), tk)

        sc_free = [None] * 3
        t_T1 = {}

        def modulated(c, k):
            f, j = sc[k % 3][:, 0:L], 2 * k + c
            src, sl = xT[:, k, c * L:(c + 1) * L], slice(c * L, (c + 1) * L)
            th = act.do(lambda e: e.activation(Th[:, k, sl], src, ACT.Identity, bias=modc[:, j:j + 1],
                                               scale=A1[:, j:j + 1]), t_mod, t_xT[(c, k)])
            tf = dve.do(lambda e: e.tensor_scalar(f, src, A1[:, j:j + 1], modc[:, j:j + 1], ALU.mult, ALU.add),
                        t_mod, t_xT[(c, k)], sc_free[k % 3])
            sc_free[k % 3] = dve.do(lambda e: e.tensor_tensor(Tl[:, k, sl], f, Th[:, k, sl], ALU.subtract), th, tf)
            t_T1[(c, k)] = sc_free[k % 3]

        for k in range(KT):
            modulated(0, k)
            if k in (3, 7):
                split(k // 4)
        for k in range(KT):
            modulated(1, k)
            if k in (1, 3, 5):
                split(2 + k // 2)
        t_T = t_T1[(1, KT - 1)]
        s_b1 = sem("s_bias1")
        at = H[5]
        extra[at] = [("late", cols[:, EARLY:], t["cols"][:, EARLY:], s_late)]
        d_late = (s_late, 16)

        UP = 8 + L + 8
        uT = big[:, 2048:2048 + 4 * UP].rearrange("p (g w) -> p g w", g=4)
        qT = big[:, 3200:4224].rearrange("p (a b) -> p a b", a=4)
        kT = big[:, 4224:6272].rearrange("p (a b) -> p a b", a=4)
        V = big[:, 6272:8320].rearrange("p (a b) -> p a b", a=4)
        t_uz = dve.do(lambda e: e.memset(big[:, 2048:2048 + 4 * UP], 0.0))
        t_pw = dve.do(lambda e: e.memset(big[:, 8320:8320 + 4 * UP], 0.0), t_T)
        t_u, t_q, t_k = [], [], []
        rot = [0]

        def take(group):
            rot[0] += 1
            return group[rot[0] % len(group)]

        ALL = list(range(8))
        for g in range(4):
            b = take(ALL)
            if g == 0:
                tk = feed_by_k(wstat_k(b, 0, L), [[t_T1[(0, k)], free[b]] for k in range(KT)])
            else:
                tk = feed(wstat(b, 0, L), free[b])
            free[b] = act.do(lambda e, b=b, g=g: e.activation(uT[:, g, 8:8 + L], ps[b][:, 0:L], ACT.Copy), tk, t_uz)
            t_u.append(free[b])
        def mod_row(q, g, t_b, t_g):
            bb = [take(ALL), take(ALL)]

            def body(e):
                for n in range(2):
                    m = e.matmul(ps[bb[n]][:, :], ones[:, :], acc[q % 2][:, n * 512:(n + 1) * 512], start=True,
                                 stop=True)
                return m
            tk = pe.do(body, acc_done[q], t_ones, free[bb[0]], free[bb[1]])
            acc_read[q] = tk
            for n in range(2):
                sl = slice(n * 512, (n + 1) * 512)
                tk2 = dve.do(lambda e, n=n, sl=sl: e.tensor_tensor(g[:, sl], ps[bb[n]][:, :], g[:, sl], ALU.add),
                             tk, t_b)
                free[bb[n]] = tk2
                tk2 = dve.do(lambda e, sl=sl: e.tensor_tensor(g[:, sl], g[:, sl], gp[:, sl], ALU.mult), tk2, t_g)
            return tk2

        def mod_col(q, dst):
            b = take(ALL)

            def body(e):
                for j in range(8):
                    m = e.matmul(ps[b][:, j:j + 1], acc[q % 2][:, j * P:(j + 1) * P], ones[:, 0:1], start=True,
                                 stop=True)
                return m
            tk = pe.do(body, acc_done[q], t_ones, free[b])
            acc_read[q] = tk
            free[b] = dve.do(lambda e: e.tensor_tensor(dst, ps[b][:, 0:8], bias_of[q], ALU.add), tk)
            return free[b]

        bias_of = {1: col("b_sh2"), 2: col("b_sc2")}
        s_g1, s_g2, s_gp = sem("s_g1"), sem("s_g2"), sem("s_gp")
        row = t["rows"]
        extra[at].append(("g1", G1[:, :], row[0:1, :].partition_broadcast(P), s_g1))
        extra[at].append(("gp", gp[:, :], row[1:2, :].partition_broadcast(P), s_gp))
        for a in range(4):
            b = take(ALL)
            tk = feed(wstat(b, 0, L), free[b])
            free[b] = act.do(lambda e, b=b, a=a: e.activation(qT[:, a, :], ps[b][:, 0:L], ACT.Copy, scale=0.125), tk)
            t_q.append(free[b])

        refill()
        t_G1 = mod_row(0, G1, (s_g1, 16), (s_gp, 16))
        extra[60] = [("gp2", gp[:, :], row[3:4, :].partition_broadcast(P), s_gp, t_G1)]
        pw = [big[:, 8320 + i * UP:8320 + (i + 1) * UP] for i in range(4)]
        dT = big[:, 9408:10432].rearrange("p (g w) -> p g w", g=4)
        inv = big[:, 10432:11456].rearrange("p (g w) -> p g w", g=4)
        s_inv = sem("s_inv")
        extra[at].append(("inv", big[:, 10432:11456], t["invcnt"].partition_broadcast(P), s_inv))
        extra[H[8]] = [("bias1", arena[:, 0:4096], t["bias1"], s_b1, t_turn1)]
        extra[H[10]] = [("g2", G2[:, :], row[2:3, :].partition_broadcast(P), s_g2)]
        t_pool = []

        def window(g):
            nonlocal t_pw
            prev, tk = uT[:, g, :], t_u[g]
            for s in range(g + 1):
                a0, a1 = (1, 0) if s == 0 else (1 << (s - 1), 1 << (s - 1))
                o, e0, e1 = pw[s], a0 if s == 0 else a0 + 1, UP - a1
                tk = dve.do(lambda e, o=o, p=prev, e0=e0, e1=e1, a0=a0, a1=a1:
                            e.tensor_tensor(o[:, e0:e1], p[:, e0 - a0:e1 - a0], p[:, e0 + a1:e1 + a1], ALU.add),
                            tk, t_pw)
                prev = o
            tk = dve.do(lambda e: e.tensor_tensor(dT[:, g, :], prev[:, 8:8 + L], inv[:, g, :], ALU.mult),
                        tk, (s_inv, 16))
            t_pw = dve.do(lambda e: e.tensor_tensor(dT[:, g, :], dT[:, g, :], uT[:, g, 8:8 + L], ALU.subtract), tk)
            t_pool.append(t_pw)

        for a in range(4):
            b = take(ALL)
            tk = feed(wstat(b, 0, 512), t_T, free[b])
            free[b] = act.do(lambda e, b=b, a=a: e.activation(kT[:, a, :], ps[b][:, :], ACT.Copy), tk)
            t_k.append(free[b])
            window(a)
        sh2 = stat(8)
        vb = [take(ALL) for _ in range(4)]
        for j in range(4):
            lhs = [[xt(2 * j + i, 0, 0), xt(2 * j + i, 0, 1), xt(2 * j + i, L, 0), xt(2 * j + i, L, 1)]
                   for i in range(2)]
            tk = feed(tstat([[b] for b in vb], lhs, 512, j == 0, j == 3), *[free[b] for b in vb])
        t_v = []
        for i, b in enumerate(vb):
            free[b] = act.do(lambda e, b=b, i=i: e.activation(V[:, i, :], ps[b][:, :], ACT.Copy), tk)
            t_v.append(free[b])
        refill()
        t_sh2 = mod_col(1, sh2)

        for g in range(4):
            b = take(ALL)
            tk = pe.do(lambda e, b=b, g=g: e.matmul(ps[b][:, 0:L], col("pool_w", g * P, (g + 1) * P), dT[:, g, :],
                                                    start=True, stop=True), t_pool[g], d_late, free[b])
            tk = act.do(lambda e, b=b, g=g: e.activation(Th[:, g, L:], ps[b][:, 0:L], ACT.Copy,
                                                         scale=col("pool_scale", g, g + 1)), tk)
            free[b] = dve.do(lambda e, b=b, g=g: e.scalar_tensor_tensor(
                out=Tl[:, g, L:], in0=ps[b][:, 0:L], scalar=col("pool_scale", g, g + 1), in1=Th[:, g, L:],
                op0=ALU.mult, op1=ALU.subtract), tk)

        SB, TB, OB = [4, 5], [6], [7]
        pt_read = [None, None]
        scn = [0]

        def attention(n_heads, tiles, s_mm, s_after, bias, scale, v_of, v_after, out_k, fill):
            items = [(h, i) for h in range(n_heads) for i in range(2)]
            live = {}
            turned = {}
            done = []

            def scores(h, i):
                b = take(SB)
                n = tiles[i]
                s = scn[0] % 3
                scn[0] += 1
                tk = pe.do(lambda e: s_mm(e, ps[b], h, i, n), free[b], *s_after(h))
                m, r, ri = stat(1), stat(1), stat(1)
                tk = dve.do(lambda e: e.tensor_tensor_reduce(
                    out=sc[s][:, 0:n], in0=ps[b][:, 0:n], in1=bias[0](h, i, n), scale=-scale, scalar=3e38,
                    op0=ALU.add, op1=ALU.min, accum_out=m), tk, sc_free[s], *bias[1])
                free[b] = tk
                tk = act.do(lambda e: e.activation(sc[s][:, 0:n], sc[s][:, 0:n], ACT.Exp, bias=m, scale=-1.0,
                                                   accum_out=r), tk)
                tk = dve.do(lambda e: e.reciprocal(ri, r), tk)
                live[(h, i)] = (s, dve.do(lambda e: e.tensor_scalar(sc[s][:, 0:n], sc[s][:, 0:n], ri, None, ALU.mult),
                                          tk))

            def turn(h, i):
                s, tk = live.pop((h, i))
                b = take(TB)
                n = tiles[i] // P

                def body(e):
                    for c in range(n):
                        m = e.transpose(ps[b][:, c * P:(c + 1) * P], sc[s][:, c * P:(c + 1) * P], ident)
                    return m
                tk = pe.do(body, tk, free[b])
                sc_free[s] = tk
                dst = PT[h % 2][:, 0:n, i * P:(i + 1) * P]
                src = ps[b][:, 0:n * P].rearrange("p (c q) -> p c q", c=n)
                if (2 * h + i) % 3 == 2:
                    tk = dve.do(lambda e: e.tensor_copy(dst, src), tk, pt_read[h % 2], *junk_free)
                else:
                    tk = act.do(lambda e: e.activation(dst, src, ACT.Copy), tk, pt_read[h % 2])
                free[b] = tk
                turned[(h, i)] = tk

            def values(h):
                if h % 2 == 0:
                    done.append(take(OB))
                b = done[-1]
                r0 = 64 * (h % 2)
                nk = tiles[1] // P

                def body(e):
                    for c in range(nk):
                        q0 = 0 if c * P < tiles[0] else P
                        m = e.matmul(ps[b][r0:r0 + 64, q0:L], v_of(h, c), PT[h % 2][:, c, q0:L], start=(c == 0),
                                     stop=(c == nk - 1), skip_group_check=True)
                    return m
                tk = pe.do(body, turned[(h, 0)], turned[(h, 1)], free[b], *v_after)
                pt_read[h % 2] = tk
                if h % 2 == 1:
                    k = out_k + h // 2
                    tk = act.do(lambda e: e.activation(Th[:, k, L:], ps[b][:, 0:L], ACT.Copy), tk)
                    free[b] = dve.do(lambda e: e.tensor_tensor(Tl[:, k, L:], ps[b][:, 0:L], Th[:, k, L:],
                                                               ALU.subtract), tk)
                    return free[b]
                return None

            out = []
            for n in range(len(items) + 3):
                if n < len(items):
                    scores(*items[n])
                if 2 <= n < len(items) + 2:
                    turn(*items[n - 2])
                if n >= 3 and items[n - 3][1] == 1:
                    tk = values(items[n - 3][0])
                    if tk:
                        out.append(tk)
                for thunk in fill.get(n, ()):
                    thunk(out)
            return out

        def s1(e, o, h, i, n):
            r0 = 64 * (h % 2)
            return e.matmul(o[:, 0:n], qT[r0:r0 + 64, h // 2, i * P:(i + 1) * P], kT[r0:r0 + 64, h // 2, 0:n],
                            start=True, stop=True)

        def bias1(h, i, n):
            j = 8 * i + h
            a = arena[:, j * L:4352].rearrange("p (c w) -> p c w", w=L)
            return a[:, 0::(16 - j), :]

        ACC = [[0, 1], [2, 3]]
        ROT = [4, 5, 6, 7]

        def out_project(k, tiles, body_of, *after):
            h = out_h0[0] + k
            banks = [free[b] for i in tiles for b in ACC[i]] if k == 0 else []
            body = tstat([ACC[i] for i in tiles], [[xt(k, L, i) for i in tiles]], 512, k == 0, k == 7)
            return body_of(h, body, *after, *banks)

        out_h0 = [0]

        def whole(k, *after):
            refill()
            state["h"] += 1
            return out_project(k, [0, 1], last_part, *after)

        def first_tile(k, *after):
            refill()
            state["h"] += 1
            return out_project(k, [0], part, *after)

        def second_tile(k):
            return out_project(k, [1], last_part)

        out_h0[0] = state["h"]
        fill = {n: [lambda out, k=k: whole(k)] for n, k in ((2, 0), (4, 1), (6, 2), (8, 3))}
        fill[11] = [lambda out: first_tile(4, out[0])]
        fill[13] = [lambda out: first_tile(5, out[1])]
        fill[17] = [lambda out: first_tile(6, out[2])]
        heads1 = attention(8, (512, 512), s1, lambda h: (t_q[h // 2], t_k[h // 2]),
                           (bias1, [(s_b1, 16), t_zero]), 1.0, lambda h, c: V[:, c, h * 64:(h + 1) * 64], t_v, 4, fill)
        t_attn1 = heads1[-1]
        sc2, A2 = stat(8), stat(8)
        t_sc2 = mod_col(2, sc2)
        t_A2 = dve.do(lambda e: e.scalar_tensor_tensor(out=A2, in0=sc2, scalar=1.0, in1=col("g_mlp"), op0=ALU.add,
                                                       op1=ALU.mult), t_sc2)

        def row_scale(parts, after):
            s, v, r = stat(2), stat(1), stat(1)
            for n in range(2):
                tk = square_sum(parts[n], 512, 1 / 32, s[:, n:n + 1], after[n])
            tk = dve.do(lambda e: e.tensor_scalar(v, s[:, 0:1], s[:, 1:2], EPS, ALU.add, ALU.add), tk)
            return r, rsqrt(r, v, 1, tk)

        def add_normed(g, t_g):
            def add(i, after):
                r, tr = row_scale([ps[b][:, :] for b in ACC[i]], [after, after])
                out = []
                for n in range(2):
                    b, sl, s = ACC[i][n], slice(n * 512, (n + 1) * 512), sc[n]
                    tk = dve.do(lambda e, b=b, sl=sl, s=s: e.scalar_tensor_tensor(
                        out=s[:, :], in0=ps[b][:, :], scalar=r, in1=g[:, sl], op0=ALU.mult, op1=ALU.mult),
                        tr, t_g, sc_free[n])
                    free[b] = tk
                    sc_free[n] = dve.do(lambda e, sl=sl, s=s: e.tensor_tensor(x[:, i, sl], x[:, i, sl], s[:, :],
                                                                              ALU.add), tk)
                    out.append(sc_free[n])
                return out
            return add

        def add_scaled(c):
            def add(i, after):
                for n in range(2):
                    b, sl = ACC[i][n], slice(n * 512, (n + 1) * 512)
                    free[b] = dve.do(lambda e, b=b, sl=sl: e.scalar_tensor_tensor(
                        out=x[:, i, sl], in0=ps[b][:, :], scalar=c, in1=x[:, i, sl], op0=ALU.mult, op1=ALU.add),
                        after)
                return [free[b] for b in ACC[i]]
            return add

        def add_and_norm(i, add, after, *xn_free):
            t_x = add(i, after)
            r, tr = row_scale([x[:, i, 0:512], x[:, i, 512:1024]], t_x)
            t0 = dve.do(lambda e: e.tensor_scalar(xn[:, i, 0:512], x[:, i, 0:512], r, None, ALU.mult), tr, *xn_free)
            t1 = act.do(lambda e: e.activation(xn[:, i, 512:1024], x[:, i, 512:1024], ACT.Copy, scale=r), tr, *xn_free)
            return t0, t1

        def turn_tile(i, t_n, banks, gain, shift):
            out = []
            cols_i = slice(i * P, (i + 1) * P)
            for k in range(KT):
                b = take(banks)
                src = ps[b][:, 0:P]
                tk = pe.do(lambda e, k=k, src=src: e.transpose(src, xn[:, i, k * P:(k + 1) * P], ident),
                           t_n[k // 4], free[b])
                t_turned[i] = tk
                if shift is None:
                    th = act.do(lambda e, k=k, src=src: e.activation(Th[:, k, cols_i], src, ACT.Copy,
                                                                     scale=gain[:, k:k + 1]), tk)
                    tk = dve.do(lambda e, k=k, src=src: e.scalar_tensor_tensor(
                        out=Tl[:, k, cols_i], in0=src, scalar=gain[:, k:k + 1], in1=Th[:, k, cols_i],
                        op0=ALU.mult, op1=ALU.subtract), th)
                    free[b] = tk
                else:
                    f, j = sc[2][:, (k % 4) * P:(k % 4 + 1) * P], k % 4
                    th = act.do(lambda e, k=k, src=src: e.activation(
                        Th[:, k, cols_i], src, ACT.Identity, bias=shift[:, k:k + 1], scale=gain[:, k:k + 1]), tk)
                    free[b] = dve.do(lambda e, k=k, src=src, f=f: e.tensor_scalar(
                        f, src, gain[:, k:k + 1], shift[:, k:k + 1], ALU.mult, ALU.add), th, sc_free[2], f4_free[j])
                    tk = dve.do(lambda e, k=k, f=f: e.tensor_tensor(Tl[:, k, cols_i], f, Th[:, k, cols_i],
                                                                    ALU.subtract), free[b])
                    f4_free[j] = tk
                out.append(tk)
            return out

        f4_free = [None] * 4
        t_turned = [None, None]

        def boundary(first, second, add, gain, shift, *after):
            for thunk in first:
                tk = thunk()
            t_n = add_and_norm(0, add, tk, *after)
            for thunk in second[:-1]:
                tk = thunk()
            if len(second) > 1:
                ta = turn_tile(0, t_n, [0, 1, 4, 5, 6, 7], gain, shift)
                tk = second[-1]()
            else:
                tk = second[-1]()
                ta = turn_tile(0, t_n, [0, 1, 4, 5, 6, 7], gain, shift)
            t_n = add_and_norm(1, add, tk, *after)
            tb = turn_tile(1, t_n, ALL, gain, shift)
            return [[p, q] for p, q in zip(ta, tb)]

        t_T = boundary([lambda: first_tile(7, t_attn1)], [lambda k=k: second_tile(k) for k in range(4, 8)],
                       add_normed(G1, t_G1), A2, sh2, t_A2, t_sh2, t_attn1)
        refill()

        fbuf = [PT[0][:, i, :] for i in range(4)]
        rbuf = [PT[1][:, i, :] for i in range(4)]
        f_free, r_free = [None] * 4, [None] * 4

        def hidden_parts(f, tk):
            i, j = f % 4, f % 8
            th = act.do(lambda e: e.activation(Th[:, j, L:], fbuf[i], ACT.Copy), tk, down_done.get(f - 8))
            tl = dve.do(lambda e: e.tensor_tensor(Tl[:, j, L:], fbuf[i], Th[:, j, L:], ALU.subtract), th)
            f_free[i] = tl
            return tl

        def down(f, t_h):
            j = f % 8
            down_done[f] = feed(tstat(ACC, [[xt(j, L, 0), xt(j, L, 1)]], 512, f == 0, False), t_h,
                                *([free[b] for r in ACC for b in r] if f == 0 else []))

        def tail(n):
            refill()
            h0 = state["h"]
            state["h"] += TAIL

            def products(c, i, body_of):
                f = n - TAIL + c
                return body_of(h0 + c, tstat([ACC[i]], [[xt(f % 8, L, i)]], 512, False, c == TAIL - 1), hid[f])

            return ([lambda c=c: products(c, 0, part) for c in range(TAIL)],
                    [lambda c=c: products(c, 1, last_part) for c in range(TAIL)])

        def first_chunk(f, b, t_T):
            if f == 0:
                return feed_by_k(wstat_k(b, 0, L), [w + [free[b]] for w in t_T])
            return feed(wstat(b, 0, L), free[b])

        down_done = {}
        hid = {}
        t_G2 = None
        for i in range(4):
            r_free[i] = junk_free[1]
        for what, f in mlp_order(FM, MLP_LAG):
            if what == "up":
                b = take(ROT)
                tk = first_chunk(f, b, t_T)
                i = f % 4
                free[b] = act.do(lambda e, b=b, i=i: e.activation(rbuf[i], ps[b][:, 0:L], ACT.Relu), tk, r_free[i],
                                 *junk_free)
                tk = dve.do(lambda e, i=i: e.tensor_tensor(fbuf[i], rbuf[i], rbuf[i], ALU.mult), free[b], f_free[i],
                            pt_read[0], pt_read[1])
                r_free[i] = tk
                hid[f] = hidden_parts(f, tk)
            elif f < FM - TAIL:
                down(f, hid[f])
                if f == 24:
                    refill()
                    assert state["m"] == 32
                    take_all, ALL[:] = list(ALL), ROT
                    t_G2 = mod_row(3, G2, (s_g2, 16), (s_gp, 32))
                    ALL[:] = take_all
        junk_free[0] = junk_free[1] = r_free[3]
        extra[130] = [("gp3", gp[:, :], t["rows"][4:5, :].partition_broadcast(P), s_gp, t_G2)]
        t_T = boundary(*tail(FM), add_normed(G2, t_G2), col("g_ffn1"), None)

        def swiglu(t_T):
            down_done.clear()
            hid.clear()
            for i in range(4):
                r_free[i] = junk_free[1]
            for what, f in mlp_order(F2, FFN_LAG):
                if what == "up":
                    bg, bu, i = take(ROT), take(ROT), f % 4
                    tk = first_chunk(f, bg, t_T)
                    free[bg] = act.do(lambda e, b=bg, i=i: e.activation(rbuf[i], ps[b][:, 0:L], ACT.Silu), tk,
                                      r_free[i], *junk_free)
                    tg = free[bg]
                    tk = feed(wstat(bu, 0, L), free[bu])
                    free[bu] = dve.do(lambda e, b=bu, i=i: e.tensor_tensor(fbuf[i], rbuf[i], ps[b][:, 0:L], ALU.mult),
                                      tk, tg, f_free[i])
                    r_free[i] = free[bu]
                    hid[f] = hidden_parts(f, free[bu])
                elif f < F2 - TAIL:
                    down(f, hid[f])
            junk_free[0] = junk_free[1] = r_free[(F2 - 1) % 4]
            return tail(F2)

        t_T = boundary(*swiglu(t_T), add_scaled(0.5), col("g_mix2"), None)

        t_x_last = t_T[-1][1]
        s_bA = sem("s_biasA")
        n0 = next(n for n, c in enumerate(plan) if c[0] == "w_uq")
        extra[n0] = [("biasA", arena[:, 0:4096], t["bias2"], s_bA, t_turned[1])]
        qTa = big[:, 0:1024].rearrange("p (a b) -> p a b", a=4)
        kTa = big[:, 1024:2048].rearrange("p (a b) -> p a b", a=4)
        Va = big[:, 2048:3072].rearrange("p (a b) -> p a b", a=2)
        qTb = big[:, 3072:5120].rearrange("p (a b) -> p a b", a=8)
        kTb = big[:, 5120:7168].rearrange("p (a b) -> p a b", a=8)
        Vb = big[:, 7168:8192].rearrange("p (a b) -> p a b", a=2)
        qf = big[:, 8192:9728].rearrange("p (t h d) -> p t h d", t=2, h=8)
        kf = big[:, 9728:11264].rearrange("p (t h d) -> p t h d", t=2, h=8)
        ropet = big[:, 11264:11520].rearrange("p (t h d) -> p t h d", t=1, h=8)[:, 0]
        rab = [stat(256).rearrange("p (h d) -> p h d", h=8), stat(256).rearrange("p (h d) -> p h d", h=8)]
        qn = [G2[:, 0:512], G2[:, 512:1024]]
        qn_free = [t_x_last, t_x_last]
        sq = [G1[:, 0:512], G1[:, 512:1024]]
        sq_free = [t_x_last, t_x_last]
        sqn = [0]

        def squares(src, shape, *after):
            i = sqn[0] % 2
            sqn[0] += 1
            n = shape[0] * shape[1]
            o = sq[i][:, 0:n].rearrange("p (h d) -> p h d", h=shape[0])
            return i, o, act.do(lambda e: e.activation(o, src, ACT.Square), sq_free[i], *after)

        def inv_rms(src, n, d, *after):
            v, r = stat(n), stat(n)
            tk = dve.do(lambda e: e.tensor_scalar(v, src, 1.0 / d, EPS, ALU.mult, ALU.add), *after)
            return r, rsqrt(r, v, n, tk)

        cq, sq_t, ck, sk = (big[:, 11520 + 64 * i:11520 + 64 * (i + 1)].rearrange("p (t d) -> p t d", t=2)
                            for i in range(4))
        t_rot = []
        for dst, tab, g in ((cq, "cos2", "g_qr"), (sq_t, "sin2", "g_qr"), (ck, "cos2", "g_kr"), (sk, "sin2", "g_kr")):
            t_rot.append(dve.do(lambda e, dst=dst, tab=tab, g=g: e.tensor_tensor(
                dst, col(tab).rearrange("p (t d) -> p t d", t=2), col(g).unsqueeze(1).broadcast_to([P, 2, 32]),
                ALU.mult), t_attn1, d_late))
        t_rot = t_rot[-1]
        gq8 = stat(1)
        t_gq8 = dve.do(lambda e: e.tensor_scalar(gq8, col("g_aq"), 0.125, None, ALU.mult))

        lb = [take(ALL), take(ALL)]
        for j in range(4):
            lhs = [[xt(2 * j + i, 0, 0), xt(2 * j + i, 0, 1)] for i in range(2)]
            tk = feed(tstat([[b] for b in lb], lhs, 416, j == 0, j == 3), *t_T[2 * j], *t_T[2 * j + 1],
                      *[free[b] for b in lb])
        t_lat = []
        krn = stat(64)
        qln = [PT[1][:, 0:2, :].rearrange("p a b -> p (a b)")[:, 0:384],
               PT[1][:, 2:4, :].rearrange("p a b -> p (a b)")[:, 0:384]]
        for i in range(2):
            s, v = stat(3), stat(3)
            for n, (c0, c1) in enumerate(((0, 256), (256, 384), (384, 416))):
                j = sqn[0] % 2
                sqn[0] += 1
                tq = act.do(lambda e, i=i, n=n, c0=c0, c1=c1, j=j, s=s: e.activation(
                    sq[j][:, 0:c1 - c0], ps[lb[i]][:, c0:c1], ACT.Square, accum_out=s[:, n:n + 1]), tk, sq_free[j])
                sq_free[j] = tq
            tq = dve.do(lambda e, s=s, v=v: e.tensor_tensor(v, s, col("invd", 0, 3), ALU.mult), tq)
            tq = dve.do(lambda e, v=v: e.tensor_scalar(v, v, EPS, None, ALU.add), tq)
            r = stat(3)
            tq = rsqrt(r, v, 3, tq)
            for n, (c0, c1, dst) in enumerate(((0, 256, qln[i][:, 0:256]), (256, 384, qln[i][:, 256:384]),
                                               (384, 416, krn[:, 32 * i:32 * i + 32]))):
                tn = dve.do(lambda e, i=i, n=n, c0=c0, c1=c1, dst=dst, r=r: e.tensor_scalar(
                    dst, ps[lb[i]][:, c0:c1], r[:, n:n + 1], None, ALU.mult), tq, *junk_free)
            free[lb[i]] = tn
            t_lat.append(tn)

        def qk_rows():
            bb = [take(ALL), take(ALL)]
            for j in range(4):
                lhs = [[xt(2 * j + i, 0, 0), xt(2 * j + i, 0, 1)] for i in range(2)]
                tk = feed(tstat([[b] for b in bb], lhs, 512, j == 0, j == 3), *[free[b] for b in bb])
            return bb, tk

        def qk_norm(bb, tk, dstT, g, t_g):
            tns = []
            for i in range(2):
                b = bb[i]
                j, o, tq = squares(ps[b][:, :].rearrange("p (h d) -> p h d", h=8), (8, 64), tk)
                s = stat(8)
                tq = dve.do(lambda e, o=o, s=s: e.tensor_reduce(s, o, AX_X, ALU.add), tq)
                sq_free[j] = tq
                r, tq = inv_rms(s, 8, 64, tq)
                tn = dve.do(lambda e, i=i, b=b, r=r: e.tensor_tensor(
                    qn[i].rearrange("p (h d) -> p h d", h=8), ps[b][:, :].rearrange("p (h d) -> p h d", h=8),
                    r.unsqueeze(2).broadcast_to([P, 8, 64]), ALU.mult), tq, qn_free[i])
                free[b] = tn
                tns.append(tn)

            def finish():
                out = []
                for i in range(2):
                    b2 = take(ALL)

                    def body(e, i=i, b2=b2):
                        for a in range(4):
                            m = e.transpose(ps[b2][:, a * P:(a + 1) * P], qn[i][:, a * P:(a + 1) * P], ident)
                        return m
                    tt = pe.do(body, tns[i], free[b2])
                    qn_free[i] = tt
                    free[b2] = act.do(lambda e, i=i, b2=b2: e.activation(
                        dstT[:, :, i * P:(i + 1) * P], ps[b2][:, :].rearrange("p (a q) -> p a q", a=4), ACT.Copy,
                        scale=g), tt, t_g, t_attn1)
                    out.append(free[b2])
                return out
            return finish

        bq, tkq = qk_rows()
        t_L = []
        for c, g in ((0, col("g_ql", 0, 1)), (1, col("g_ql", 1, 2)), (2, col("g_kvl"))):
            b = take(ALL)

            def body(e, c=c, b=b):
                for i in range(2):
                    m = e.transpose(ps[b][:, i * P:(i + 1) * P], qln[i][:, c * P:(c + 1) * P], ident)
                return m
            tt = pe.do(body, *t_lat, free[b])
            junk_free[0] = junk_free[1] = tt
            tt = act.do(lambda e, c=c, b=b, g=g: e.activation(Th[:, c, L:], ps[b][:, 0:L], ACT.Copy, scale=g), tt)
            free[b] = dve.do(lambda e, c=c, b=b, g=g: e.scalar_tensor_tensor(
                out=Tl[:, c, L:], in0=ps[b][:, 0:L], scalar=g, in1=Th[:, c, L:], op0=ALU.mult, op1=ALU.subtract), tt)
            t_L.append(free[b])
        fin_q = qk_norm(bq, tkq, qTa, gq8, t_gq8)
        bk_, tkk = qk_rows()
        t_qa = fin_q()
        fin_k = qk_norm(bk_, tkk, kTa, col("g_ak"), None)

        FB = [[0, 1], [2, 3]]
        for k in range(2):
            tk_uq = feed(tstat(FB, [[xt(k, L, 0), xt(k, L, 1)]], 384, k == 0, k == 1), *t_L,
                         *[free[b] for r in FB for b in r])
        t_qf, t_kf, t_vb = [[], []], [[], []], []
        rope_free = [None]

        def rotate(i, src, cos, sin, heads, dst, *after):
            a, b = (u[:, 0:heads, :] for u in rab)
            ta = dve.do(lambda e: e.tensor_tensor(a, src, cos[:, i, :].unsqueeze(1).broadcast_to([P, heads, 32]),
                                                  ALU.mult), *after, rope_free[0], t_rot)
            tb = dve.do(lambda e: e.tensor_tensor(b, src, sin[:, i, :].unsqueeze(1).broadcast_to([P, heads, 32]),
                                                  ALU.mult), ta)

            def wide(u, c0):
                v = u[:, :, c0:c0 + 16]
                return v.broadcast_to([P, 8, 16]) if heads == 1 else v
            t1 = dve.do(lambda e: e.tensor_tensor(dst[:, :, 64:80], wide(a, 0), wide(b, 16), ALU.subtract), tb)
            rope_free[0] = dve.do(lambda e: e.tensor_tensor(dst[:, :, 80:96], wide(b, 0), wide(a, 16), ALU.add), t1)
            return rope_free[0]

        def q_heads(i, n):
            b = FB[i][n]
            src = ps[b][:, 0:384].rearrange("p (h d) -> p h d", h=4)
            j, o, tq = squares(src, (4, 96), tk_uq)
            s, v, r = stat(8), stat(8), stat(8)
            ta = dve.do(lambda e: e.tensor_reduce(s[:, 0:4], o[:, :, 0:64], AX_X, ALU.add), tq)
            tq = dve.do(lambda e: e.tensor_reduce(s[:, 4:8], o[:, :, 64:96], AX_X, ALU.add), tq)
            sq_free[j] = tq
            dve.do(lambda e: e.tensor_scalar(v[:, 0:4], s[:, 0:4], 1 / 64, EPS, ALU.mult, ALU.add), ta)
            tq = dve.do(lambda e: e.tensor_scalar(v[:, 4:8], s[:, 4:8], 1 / 32, EPS, ALU.mult, ALU.add), tq)
            tq = rsqrt(r, v, 8, tq)
            t_qf[i].append(dve.do(lambda e: e.tensor_tensor(
                qf[:, i, 4 * n:4 * n + 4, 0:64], src[:, :, 0:64], r[:, 0:4].unsqueeze(2).broadcast_to([P, 4, 64]),
                ALU.mult), tq))
            free[b] = dve.do(lambda e: e.tensor_tensor(
                ropet[:, 4 * n:4 * n + 4, :], src[:, :, 64:96], r[:, 4:8].unsqueeze(2).broadcast_to([P, 4, 32]),
                ALU.mult), tq, rope_free[0])
            if n == 1:
                t_qf[i].append(rotate(i, ropet, cq, sq_t, 8, qf[:, i], free[b]))

        def k_heads(i, n):
            b = FB[i][n]
            src = ps[b][:, :].rearrange("p (h d) -> p h d", h=4)
            j, o, tq = squares(src[:, :, 0:64], (4, 64), tk_kv[0])
            tv = act.do(lambda e: e.activation(Vb[:, i, n * 256:(n + 1) * 256].rearrange("p (h d) -> p h d", h=4),
                                               src[:, :, 64:128], ACT.Copy), tk_kv[0])
            t_vb.append(tv)
            s = stat(4)
            tq = dve.do(lambda e: e.tensor_reduce(s, o, AX_X, ALU.add), tq)
            sq_free[j] = tq
            r, tq = inv_rms(s, 4, 64, tq)
            free[b] = dve.do(lambda e: e.tensor_tensor(
                kf[:, i, 4 * n:4 * n + 4, 0:64], src[:, :, 0:64], r.unsqueeze(2).broadcast_to([P, 4, 64]),
                ALU.mult), tq, tv)
            t_kf[i].append(free[b])
            if n == 1:
                t_kf[i].append(rotate(i, krn[:, 32 * i:32 * i + 32].unsqueeze(1), ck, sk, 1, kf[:, i], t_lat[i]))

        vbk = [4, 5]
        for j in range(4):
            lhs = [[xt(2 * j + i, 0, 0), xt(2 * j + i, 0, 1)] for i in range(2)]
            tk = feed(tstat([[b] for b in vbk], lhs, 512, j == 0, j == 3), *[free[b] for b in vbk])
        t_va = []
        refill()
        t_ka = fin_k()
        for i, b in enumerate(vbk):
            free[b] = act.do(lambda e, b=b, i=i: e.activation(Va[:, i, :], ps[b][:, :], ACT.Copy), tk)
            t_va.append(free[b])
        for i in range(2):
            for n in range(2):
                q_heads(i, n)
        tk_kv = [feed(tstat(FB, [[xt(2, L, 0), xt(2, L, 1)]], 512, True, True), *t_L,
                      *[free[b] for r in FB for b in r])]
        t_qb, t_kb = [], []

        def turn_heads(src, dst, g, tin, tout, i, n):
            b = 2 * i + n

            def body(e):
                for h in range(4):
                    m = e.transpose(ps[b][0:96, h * P:(h + 1) * P], src[:, i, 4 * n + h, :], ident)
                return m
            tt = pe.do(body, *tin[i], free[b])
            o = dst[0:96, 4 * n:4 * n + 4, i * P:(i + 1) * P]
            v = ps[b][0:96, :].rearrange("p (h q) -> p h q", h=4)
            gc = cols[0:96, COLS[g][0]:COLS[g][0] + 1]
            free[b] = act.do(lambda e: e.activation(o, v, ACT.Copy, scale=gc), tt)
            tout.append(free[b])

        def sA(e, o, h, i, n):
            r0 = 64 * (h % 2)
            return e.matmul(o[:, 0:n], qTa[r0:r0 + 64, h // 2, i * P:(i + 1) * P], kTa[r0:r0 + 64, h // 2, 0:n],
                            start=True, stop=True)

        def sB(e, o, h, i, n):
            return e.matmul(o[:, 0:n], qTb[0:96, h, i * P:(i + 1) * P], kTb[0:96, h, 0:n], start=True, stop=True)

        def biasA(h, i, n):
            j = 8 * i + h
            return arena[:, j * L:j * L + n]

        mask = col("mask").rearrange("p (t w) -> p t w", t=2)
        fillA = {n: [lambda out, i=i, c=c: k_heads(i, c)] for n, i, c in ((1, 0, 0), (3, 0, 1), (5, 1, 0), (7, 1, 1))}
        for n in range(4):
            fillA[2 + 2 * n] = [lambda out, i=n // 2, c=n % 2: turn_heads(qf, qTb, "g_bq", t_qf, t_qb, i, c)]
        for n in range(4):
            fillA[12 + n] = [lambda out, i=n // 2, c=n % 2: turn_heads(kf, kTb, "g_bk", t_kf, t_kb, i, c)]
        attention(8, (128, 256), sA, lambda h: (*t_qa, *t_ka), (biasA, [(s_bA, 16)]), 1.0,
                  lambda h, c: Va[:, c, h * 64:(h + 1) * 64], t_va, 0, fillA)
        refill()
        out_h0[0] = state["h"]
        fill = {n: [lambda out, k=k: whole(k)] for n, k in ((1, 0), (3, 1), (5, 2), (7, 3))}
        fill[10] = [lambda out: first_tile(4, out[0])]
        fill[13] = [lambda out: first_tile(5, out[1])]
        fill[17] = [lambda out: first_tile(6, out[2])]
        headsB = attention(8, (128, 256), sB, lambda h: (*t_qb, *t_kb), (lambda h, i, n: mask[:, i, 0:n], [d_late]),
                           float(96 ** -0.5), lambda h, c: Vb[:, c, h * 64:(h + 1) * 64], t_vb, 4, fill)
        t_T = boundary([lambda: first_tile(7, headsB[-1])], [lambda k=k: second_tile(k) for k in range(4, 8)],
                       add_scaled(1.0), col("g_ffn2"), None, headsB[-1])
        refill()
        for i in range(4):
            f_free[i] = pt_read[0]
            r_free[i] = pt_read[1]
        first, second = swiglu(t_T)
        add = add_scaled(0.5)

        s_out = sem("s_out")

        def last_norm(i, after):
            r, tr = row_scale([x[:, i, 0:512], x[:, i, 512:1024]], add(i, after))
            for n in range(2):
                sl = slice(n * 512, (n + 1) * 512)
                tk = dve.do(lambda e, sl=sl: e.scalar_tensor_tensor(
                    out=xn[:, i, sl], in0=x[:, i, sl], scalar=r, in1=gp[:, sl], op0=ALU.mult, op1=ALU.mult),
                    tr, (s_gp, 48))
                extra.setdefault("end", []).append((i, sl, tk))

        for i, thunks in enumerate((first, second)):
            for thunk in thunks:
                tk = thunk()
            last_norm(i, tk)

        assert state["h"] == len(H), (state["h"], len(H))

        for n, (name, j, w, kind) in enumerate(plan):
            for item in extra.get(n, ()):
                dst, src, s = item[1], item[2], item[3]
                sp.go(lambda e, dst=dst, src=src, s=s: e.dma_start(dst, src).then_inc(s, 16), *item[4:])
            sp.go(lambda e, n=n, name=name, j=j, w=w: e.dma_start(raw[n % RAW][:, 0:w], t[name][j, :, :])
                  .then_inc(s_raw[n % RAW], 16), freed.get(n - RAW))
        for i, sl, tk in extra["end"]:
            sp.go(lambda e, i=i, sl=sl: e.dma_start(t["out"][i * P:(i + 1) * P, sl], xn[:, i, sl])
                  .then_inc(s_out, 16), tk)

        block = ctx.enter_context(nc.Block())

        @block.sync
        def _(e):
            sp.play(e)
            e.wait_ge(s_out, 64)

        @block.scalar
        def _(e):
            act.play(e)

        @block.vector
        def _(e):
            dve.play(e)

        @block.gpsimd
        def _(e):
            pool.play(e)

        @block.tensor
        def _(e):
            pe.play(e)


def _column(v):
    return v.reshape(-1, P).T


def _tiles(w):
    k, j = w.shape[0] // P, w.shape[1] // P
    return np.ascontiguousarray(w.reshape(k, P, j, P).transpose(2, 1, 0, 3).reshape(j, P, k * P))


def _rows(w):
    return np.ascontiguousarray(w.reshape(-1, P, w.shape[1]))


def _row_pairs(w):
    k, c = w.shape[0] // P, w.shape[1]
    return np.ascontiguousarray(w.reshape(k // 2, 2, P, c).transpose(0, 2, 1, 3).reshape(k // 2, P, 2 * c))


def _bias1(rpb):
    out = np.full((8, 4, 64, 4, 64), NEG, np.float32)
    qc = np.arange(64)
    start = np.clip(qc - 8, 0, 48)
    for qr in range(4):
        for kr in range(4):
            for c in range(64):
                k0 = start[c]
                out[:, qr, c, kr, k0:k0 + 16] = rpb[:, kr - qr + 7, k0 - c + 15:k0 - c + 31]
    return np.ascontiguousarray(out.reshape(8, 2, P, L).transpose(2, 1, 0, 3).reshape(P, 2 * 8 * L))


def _bias2(rb):
    i, j = np.arange(L)[:, None], np.arange(L)[None, :]
    rel = np.clip(i - j, -128, 128) + 128
    out = np.where((j // 64 <= i // 64)[None], rb[:, rel], np.float32(NEG)).astype(np.float32)
    return np.ascontiguousarray(out.reshape(8, 2, P, L).transpose(2, 1, 0, 3).reshape(P, 2 * 8 * L))


def _shape_tables():
    i, j = np.arange(L)[:, None], np.arange(L)[None, :]
    mask = np.where(j // 64 <= i // 64, 0.0, NEG).astype(np.float32)
    mask = mask.reshape(2, P, L).transpose(1, 0, 2).reshape(P, 2 * L)
    inv = 1.0 / (10000.0 ** (np.arange(0, 32, 2, dtype=np.float32) / np.float32(32)))
    ang = np.arange(L, dtype=np.float32)[:, None] * inv.astype(np.float32)[None, :]

    def twice(a):
        a = np.concatenate([a, a], axis=1).astype(np.float32)
        return a.reshape(2, P, 32).transpose(1, 0, 2).reshape(P, 64)
    t = np.arange(L)
    cnt = [np.clip(t + w - w // 2, 0, L) - np.clip(t - w // 2, 0, L) for w in (2, 4, 8, 16)]
    invcnt = (1.0 / np.stack(cnt).astype(np.float32)).astype(np.float32).reshape(1, 4 * L)
    invd = np.zeros((P, 16), np.float32)
    invd[:, 0:3] = [1 / 256, 1 / 128, 1 / 32]
    return mask, twice(np.cos(ang)), twice(np.sin(ang)), invcnt, invd


def kernel(**inputs):
    import concourse.bacc as bacc
    from concourse.bass_utils import run_bass_kernel_spmd

    v = {k: np.asarray(a) for k, a in inputs.items()}
    mask, cos2, sin2, invcnt, invd = _shape_tables()
    ones32 = np.ones(32, np.float32)
    w_mod, b_mod, w_in = v["w_mod"][0], v["b_mod"][0], v["w_in"][0]
    w_in2 = v["w_in_2"][0]
    cc = np.stack([_column(v["c"][0]), _column(v["c_ctx"])], axis=2).reshape(P, 16)
    parts = {
        "ident": np.eye(P, dtype=np.float32), "cc": cc,
        "b_sh1": _column(b_mod[0:1024]), "b_sc1": _column(b_mod[1024:2048]),
        "b_sh2": _column(b_mod[3072:4096]), "b_sc2": _column(b_mod[4096:5120]),
        "g_mix": _column(v["g_pre_mix"][0]), "g_mlp": _column(v["g_pre_mlp"][0]),
        "pool_scale": _column(v["pool_scale"][0]), "g_ffn1": _column(v["ffn1_norm_2"][0]),
        "g_mix2": _column(v["mix_norm_2"][0]), "g_ffn2": _column(v["ffn2_norm_2"][0]),
        "g_aq": np.tile(v["a_q_norm_2"][0], 2)[:, None], "g_ak": np.tile(v["a_k_norm_2"][0], 2)[:, None],
        "g_bq": np.concatenate([v["b_q_nope_norm_2"][0], ones32, ones32])[:, None],
        "g_bk": np.concatenate([v["b_k_nope_norm_2"][0], ones32, ones32])[:, None],
        "g_ql": _column(v["b_q_lat_norm_2"][0]), "g_kvl": _column(v["b_kv_lat_norm_2"][0]),
        "g_qr": np.broadcast_to(v["b_q_rope_norm_2"][0], (P, 32)),
        "g_kr": np.broadcast_to(v["b_k_rope_norm_2"][0], (P, 32)),
        "cos2": cos2, "sin2": sin2, "invd": invd, "mask": mask,
        "pool_w": v["pool_w"][0].transpose(1, 0, 2).reshape(P, 512),
    }
    arrays = {
        "cols": np.ascontiguousarray(np.concatenate([parts[k] for k in COLS], axis=1)),
        "x": v["x"][0], "ctx": v["ctx"][0],
        "rows": np.stack([b_mod[2048:3072], v["g_post_mix"][0], b_mod[5120:6144], v["g_post_mlp"][0],
                          v["final_norm_2"][0]]),
        "invcnt": invcnt, "bias1": _bias1(v["rpb"][0]), "bias2": _bias2(v["a_rel_bias_2"][0]),
        "w_mod_c": w_mod[:, 0:2048].reshape(KT, P, 2, 1024).transpose(0, 2, 1, 3).reshape(16, P, 1024),
        "w_mod_r": np.concatenate([_rows(w_mod[:, a:a + 1024]) for a in (2048, 3072, 4096, 5120)]),
        "w_in_u": _tiles(w_in[:, 0:512]), "w_in_q": _tiles(w_in[:, 512:1024]),
        "w_in_k": _tiles(w_in[:, 1024:1536]), "w_in_v": _row_pairs(w_in[:, 1536:2048]),
        "w_out": _rows(v["w_out"][0]), "w_mlp_in": _tiles(v["w_mlp_in"][0]), "w_mlp_out": _rows(v["w_mlp_out"][0]),
        "w_in2_q": _row_pairs(w_in2[:, 0:512]), "w_in2_k": _row_pairs(w_in2[:, 512:1024]),
        "w_in2_v": _row_pairs(w_in2[:, 1024:1536]), "w_in2_l": _row_pairs(w_in2[:, 1536:1952]),
        "w_uq": _rows(v["b_w_uq_2"][0]), "w_ukv": _rows(v["b_w_ukv_2"][0]), "w_out2": _rows(v["w_out_2"][0]),
    }
    for a in ("ffn1", "ffn2"):
        arrays[a + "_gate"] = _tiles(v[a + "_w_gate_2"][0])
        arrays[a + "_up"] = _tiles(v[a + "_w_up_2"][0])
        arrays[a + "_down"] = _rows(v[a + "_w_down_2"][0])
    arrays = {k: np.ascontiguousarray(a) for k, a in arrays.items()}

    nc = bacc.Bacc("TRN2", target_bir_lowering=False, num_devices=1)
    t = {k: nc.dram_tensor("in_" + k, a.shape, F32, kind="ExternalInput").ap() for k, a in arrays.items()}
    t["out"] = nc.dram_tensor("out_0", (L, D), F32, kind="ExternalOutput").ap()
    build(nc, t)
    res = run_bass_kernel_spmd(nc, [{"in_" + k: a for k, a in arrays.items()}], core_ids=[0])
    return res.results[0]["out_0"].reshape(1, L, D)
```

```python
from contextlib import ExitStack

import numpy as np

import concourse.bass as bass
from concourse import mybir

F32 = mybir.dt.float32
F32R = mybir.dt.float32r
ALU = mybir.AluOpType
ACT = mybir.ActivationFunctionType
AX_X = mybir.AxisListType.X

P = 128
D = 1024
KT = D // P
L = 256
FM = 32
F2 = 22
EPS = 1e-6
NEG = -1e30
W = 1024
RAW = 7
RING = 5

COLS = {}
_at = 0
for _name, _n in [("ident", 128), ("cc", 16), ("b_sh1", 8), ("b_sc1", 8), ("b_sh2", 8), ("b_sc2", 8),
                  ("g_mix", 8), ("g_mlp", 8), ("pool_scale", 4), ("g_ffn1", 8), ("g_mix2", 8), ("g_ffn2", 8),
                  ("g_aq", 1), ("g_ak", 1), ("g_bq", 1), ("g_bk", 1), ("g_ql", 2), ("g_kvl", 1),
                  ("invd", 16), ("pool_w", 512), ("mask", 512), ("g_qr", 32), ("g_kr", 32), ("cos2", 64),
                  ("sin2", 64)]:
    COLS[_name] = (_at, _n)
    _at += _n
NCOLS = _at
EARLY = COLS["pool_w"][0]


TAIL = 4
WHOLE = (5, 9, 15)
N_SPLIT = 16 - len(WHOLE)


def mlp_order(n, lag):
    out, done = [], 0
    for f in range(n):
        out.append(("up", f))
        if lag <= f and done < n - TAIL:
            out.append(("down", done))
            done += 1
    return out + [("down", f) for f in range(done, n)]


MLP_LAG = 5
FFN_LAG = 2


def stream_plan():
    s = [("w_mod_c", j, 1024, "C" if j in WHOLE else "H") for j in range(16)]
    h = [("w_in_u", j, 1024, "H") for j in range(4)] + [("w_in_q", j, 1024, "H") for j in range(4)]
    h += [("w_in_k", j, 1024, "H") for j in range(4)] + [("w_in_v", j, 1024, "H") for j in range(4)]
    m = [("w_mod_r", j, 1024, "M") for j in range(32)]
    s += h[:11]
    mi = 0
    for n, c in enumerate(h[11:]):
        s.append(c)
        s += m[mi:mi + 3 + (n > 3)]
        mi += 3 + (n > 3)
    for k in range(8):
        s.append(("w_out", k, 1024, "H"))
        n = {4: 4, 5: 2, 6: 2}.get(k, 0)
        s += m[mi:mi + n]
        mi += n
    for n, (what, f) in enumerate(mlp_order(FM, MLP_LAG)):
        if what == "down":
            s.append(("w_mlp_out", f, 1024, "H"))
        else:
            s.append(("w_mlp_in_rows", f, 1024, "H") if f < 4 else ("w_mlp_in", f - 4, 1024, "H"))
        if n >= 16 and n % 2 == 0 and mi < 32:
            s.append(m[mi])
            mi += 1

    def ffn(a):
        for what, f in mlp_order(F2, FFN_LAG):
            if what == "up" and f < 2:
                s.extend((a + "_rows", 2 * f + j, 1024, "H") for j in range(2))
            elif what == "up":
                s.append((a + "_gate", f - 2, 1024, "H"))
                s.append((a + "_up", f - 2, 1024, "H"))
            else:
                s.append((a + "_down", f, 1024, "H"))

    ffn("ffn1")
    s.extend(("w_in2_l", j, 832, "H") for j in range(4))
    s.extend(("w_in2_q", j, 1024, "H") for j in range(4))
    s.extend(("w_in2_k", j, 1024, "H") for j in range(4))
    s.extend(("w_uq", j, 768, "H") for j in range(2))
    s.extend(("w_in2_v", j, 1024, "H") for j in range(4))
    s.append(("w_ukv", 0, 1024, "H"))
    s.extend(("w_out2", k, 1024, "H") for k in range(8))
    ffn("ffn2")
    return s


class Queue:

    def __init__(self, sem):
        self.sem, self.n, self.items = sem, 0, []

    def do(self, fn, *after):
        self.n += 1
        self.items.append((fn, after, True))
        return (self.sem, self.n)

    def go(self, fn, *after):
        self.items.append((fn, after, False))

    def last(self):
        return (self.sem, self.n) if self.n else None

    def play(self, eng):
        passed = {}
        for fn, after, counts in self.items:
            for w in after:
                if w is not None and passed.get(w[0].name, 0) < w[1]:
                    eng.wait_ge(w[0], w[1])
                    passed[w[0].name] = w[1]
            ins = fn(eng)
            if counts:
                ins.then_inc(self.sem, 1)


def build(nc, t):
    ctx = ExitStack()
    with ctx:
        def sb(name, shape, dt=F32):
            return ctx.enter_context(nc.sbuf_tensor(name, shape, dt))

        def sem(name):
            return ctx.enter_context(nc.semaphore(name))

        raw = [sb(f"raw{i}", [P, W]) for i in range(RAW)]
        hi = [sb(f"hi{i}", [P, W], F32R) for i in range(RING)]
        lo = [sb(f"lo{i}", [P, W], F32R) for i in range(RING)]
        x = sb("x", [P, 2, D])
        arena = sb("arena", [P, 4096 + 256])
        Th = sb("Th", [P, KT, 512], F32R)
        Tl = sb("Tl", [P, KT, 512], F32R)
        G1 = sb("G1", [P, D])
        G2 = sb("G2", [P, D])
        gp = sb("gp", [P, D])
        cols = sb("cols", [P, NCOLS])
        sc = [sb(f"sc{i}", [P, 512]) for i in range(3)]
        PT = [sb(f"PT{i}", [P, 4, L]) for i in range(2)]
        big = sb("big", [P, 11776])
        st = sb("st", [P, 1152])
        ones = sb("ones", [P, P])
        ps = [ctx.enter_context(nc.psum_tensor(f"ps{i}", [P, 512], F32)) for i in range(8)]

        pe, act, dve, pool, sp = (Queue(sem("s_" + n)) for n in ("pe", "act", "dve", "pool", "sp"))
        s_raw = [sem(f"s_raw{i}") for i in range(RAW)]

        def col(name, a=0, b=None):
            at, n = COLS[name]
            return cols[:, at + a:at + (n if b is None else b)]

        ident = col("ident")
        xn = arena[:, 0:2048].rearrange("p (t d) -> p t d", t=2)
        cx = arena[:, 2048:4096].rearrange("p (t d) -> p t d", t=2)
        stat_at = [0]

        def stat(n):
            a = stat_at[0]
            stat_at[0] += n
            assert stat_at[0] <= 1152
            return st[:, a:a + n]

        def load(name, dst, src, *after):
            s = sem("s_" + name)
            sp.go(lambda e: e.dma_start(dst, src).then_inc(s, 16), *after)
            return (s, 16)

        d_cols = load("cols", cols[:, 0:EARLY], t["cols"][:, 0:EARLY])

        plan = stream_plan()
        freed = {}
        H = [n for n, c in enumerate(plan) if c[3] == "H"]
        used, ready = {}, {}
        state = {"h": 0, "m": 0, "split": 0, "owed": [], "acc": None}
        extra = {}

        def side(n, *load):
            extra.setdefault(n, []).append(load)

        def landed(n):
            return (s_raw[n % RAW], 16 * (n // RAW + 1))

        M = [n for n, c in enumerate(plan) if c[3] == "M"]
        acc = [big[:, 0:1024], big[:, 1024:2048], big[:, 10432:11456], big[:, 0:1024]]
        acc_free = {}
        acc_done = {}

        def sum_mod():
            m = state["m"]
            state["m"] += 1
            n, q, k = M[m], m // 8, m % 8
            a = acc[q]
            r = raw[n % RAW]
            s_k = silu_c[:, 2 * k:2 * k + 1]
            if k == 0:
                tk = dve.do(lambda e: e.tensor_scalar(a, r[:, :], s_k, None, ALU.mult), landed(n), t_silu,
                            acc_free[q])
            else:
                tk = dve.do(lambda e: e.scalar_tensor_tensor(out=a, in0=r[:, :], scalar=s_k, in1=a,
                                                             op0=ALU.mult, op1=ALU.add),
                            landed(n), state["acc"])
            state["acc"] = tk
            acc_done[q] = tk
            freed[n] = tk

        def split(h):
            n = H[h]
            while state["m"] < len(M) and M[state["m"]] < n:
                sum_mod()
            w, s, r = plan[n][2], h % RING, raw[n % RAW]
            t_hi = act.do(lambda e: e.activation(hi[s][:, 0:w], r[:, 0:w], ACT.Copy), landed(n), used.get(h - RING))
            t_lo = dve.do(lambda e: e.tensor_tensor(lo[s][:, 0:w], r[:, 0:w], hi[s][:, 0:w], ALU.subtract), t_hi)
            ready[h] = t_lo
            freed[n] = t_lo

        def refill(most=None):
            owed = state["owed"]
            while owed and most != 0:
                h = owed.pop(0)
                if h < len(H):
                    split(h)
                    most = most and most - 1

        def feed(body, *after, most=None):
            refill(most)
            h = state["h"]
            state["h"] += 1
            while h not in ready:
                refill(1)
            return last_part(h, body, *after)

        def part(h, body, *after, by_k=None):
            a, b = hi[h % RING], lo[h % RING]
            if by_k is None:
                return pe.do(lambda e: body(e, a, b), ready[h], *after)
            for k in range(KT - 1):
                pe.go(lambda e, k=k: body(e, a, b, k), ready[h], *by_k[k])
            return pe.do(lambda e: body(e, a, b, KT - 1), *by_k[KT - 1])

        def last_part(h, body, *after, **how):
            used[h] = part(h, body, *after, **how)
            state["owed"].append(h + RING)
            return used[h]

        def feed_by_k(body_k, waits):
            h = state["h"]
            state["h"] += 1
            return last_part(h, body_k, by_k=waits)

        free = [None] * 8

        def wstat(bank, c0, c1):
            def body(e, a, b):
                for k in range(KT):
                    m = wstat_k(bank, c0, c1)(e, a, b, k)
                return m
            return body

        def wstat_k(bank, c0, c1, at=0):
            def body(e, a, b, k):
                w1, w2 = a[:, k * P:(k + 1) * P], b[:, k * P:(k + 1) * P]
                o = ps[bank][:, at:at + c1 - c0]
                e.matmul(o, w1, Th[:, k, c0:c1], start=(k == 0), stop=False)
                e.matmul(o, w1, Tl[:, k, c0:c1], start=False, stop=False)
                return e.matmul(o, w2, Th[:, k, c0:c1], start=False, stop=(k == KT - 1))
            return body

        def tstat(banks, lhs, n_w, first, last):
            def body(e, a, b):
                for i, tiles in enumerate(lhs):
                    for j, (lh, ll) in enumerate(tiles):
                        nb = len(banks[j])
                        at = [i * nb * n_w + n * n_w for n in range(nb)]
                        f, z = first and i == 0, last and i == len(lhs) - 1
                        for n in range(nb):
                            e.matmul(ps[banks[j][n]][:, 0:n_w], lh, a[:, at[n]:at[n] + n_w], start=f, stop=False)
                        for n in range(nb):
                            e.matmul(ps[banks[j][n]][:, 0:n_w], lh, b[:, at[n]:at[n] + n_w], start=False, stop=False)
                        for n in range(nb):
                            m = e.matmul(ps[banks[j][n]][:, 0:n_w], ll, a[:, at[n]:at[n] + n_w],
                                         start=False, stop=z)
                return m
            return body

        def xt(k, off, i):
            return (Th[:, k, off + i * P:off + (i + 1) * P], Tl[:, k, off + i * P:off + (i + 1) * P])

        half = stat(8)
        t_half = pool.do(lambda e: e.memset(half, -0.5))
        t_ones = dve.do(lambda e: e.memset(ones[:, :], 1.0))
        t_zero = dve.do(lambda e: e.memset(arena[:, 4096:4352], 0.0))

        junk_free = [None, None]
        junk_n = [0]

        def square_sum(src, n, scale, dst, *after):
            i = junk_n[0] % 2
            junk_n[0] += 1
            j = PT[1][:, 2 * i:2 * i + 2, :].rearrange("p a b -> p (a b)")[:, 0:n]
            tk = act.do(lambda e: e.activation(j, src, ACT.Square, scale=scale, accum_out=dst), junk_free[i], *after)
            junk_free[i] = tk
            return tk

        idle = stat(1)

        def load_table(fn):
            act.do(lambda e: e.activation(idle, half[:, 0:1], fn), t_half, act.last())

        def rsqrt(dst, src, n, *after):
            return pool.do(lambda e: e.tensor_tensor(dst, src, half[:, 0:n], ALU.pow), t_half, *after)

        silu_c = stat(16)
        t_silu = act.do(lambda e: e.activation(silu_c, col("cc"), ACT.Silu), d_cols)

        ch, cl = sb("ch", [P, 16], F32R), sb("cl", [P, 16], F32R)
        t_ch = act.do(lambda e: e.activation(ch[:, :], silu_c, ACT.Copy), t_silu)
        t_cl = dve.do(lambda e: e.tensor_tensor(cl[:, :], silu_c, ch[:, :], ALU.subtract), t_ch)

        def mod_row_products(n):
            hf, k = n // KT, n % KT

            def whole(e, w):
                for m in range(2):
                    i = e.matmul(ps[2 * hf + m][0:2, :], silu_c[:, 2 * k:2 * k + 2], w[:, m * 512:(m + 1) * 512],
                                 start=(k == 0), stop=(k == KT - 1))
                return i

            def body(e, a, b):
                ck = slice(2 * k, 2 * k + 2)
                for w, u, f, z in ((a, ch, k == 0, False), (b, ch, False, False), (a, cl, False, k == KT - 1)):
                    for m in range(2):
                        i = e.matmul(ps[2 * hf + m][0:2, :], u[:, ck], w[:, m * 512:(m + 1) * 512], start=f, stop=z)
                return i
            if n in WHOLE:
                freed[n] = pe.do(lambda e: whole(e, raw[n % RAW]), landed(n), t_silu)
                return freed[n]
            return feed(body, t_cl, most=None if state["h"] < N_SPLIT - RING + 1 else 0)

        s_x, s_cx, s_late = sem("s_x"), sem("s_cx"), sem("s_late")
        side(2, "x", x[:, :, :], t["x"].rearrange("(i p) d -> p i d", p=P), s_x)
        side(5, "cx", cx, t["ctx"].rearrange("(i p) d -> p i d", p=P), s_cx)
        ss1, v1, r1 = stat(8), stat(4), stat(4)
        srcs = [x[:, 0, :], x[:, 1, :], cx[:, 0, :], cx[:, 1, :]]
        dsts = [xn[:, 0, :], xn[:, 1, :], cx[:, 0, :], cx[:, 1, :]]
        xT = big[:, 6272:10368].rearrange("p (k w) -> p k w", k=KT)
        t_xn = []

        def first_norm(i):
            d = ((s_x, 16), (s_cx, 16))[i // 2]
            for n in range(2):
                tk = square_sum(srcs[i][:, n * 512:(n + 1) * 512], 512, 1 / 32, ss1[:, 2 * i + n:2 * i + n + 1], d)
            tk = dve.do(lambda e, i=i: e.tensor_scalar(v1[:, i:i + 1], ss1[:, 2 * i:2 * i + 1],
                                                       ss1[:, 2 * i + 1:2 * i + 2], EPS, ALU.add, ALU.add), tk)
            tk = rsqrt(r1[:, i:i + 1], v1[:, i:i + 1], 1, tk)

            def finish():
                t_xn.append(dve.do(lambda e: e.tensor_scalar(dsts[i], srcs[i], r1[:, i:i + 1], None, ALU.mult), tk))
            return finish

        split(0)
        split(1)
        finish = [first_norm(0), first_norm(1)]
        split(2)
        finish[0]()
        split(3)
        finish[1]()
        split(4)
        finish = [first_norm(2), first_norm(3)]

        t_xT = {}
        turned1 = []

        def turn_rows(c, k, b):
            def body(e):
                for j in range(2):
                    for i in range(2):
                        m = e.transpose(ps[b][:, (2 * j + i) * P:(2 * j + i + 1) * P],
                                        dsts[2 * c + i][:, (k + j) * P:(k + j + 1) * P], ident)
                return m
            tk = pe.do(body, d_cols, *t_xn[2 * c:2 * c + 2], free[b])
            turned1.append(tk)
            dst = xT[:, k:k + 2, c * L:(c + 1) * L]
            src = ps[b][:, :].rearrange("p (j w) -> p j w", j=2)
            if k % 4 == 0:
                tk = act.do(lambda e: e.activation(dst, src, ACT.Copy), tk)
            else:
                tk = dve.do(lambda e: e.tensor_copy(dst, src), tk)
            free[b] = tk
            t_xT[(c, k)] = t_xT[(c, k + 1)] = tk

        modr = big[0:2, 0:2048]
        modc, A1, sc1b = stat(16), stat(16), stat(8)
        t_sc1b = dve.do(lambda e: e.tensor_scalar(sc1b, col("b_sc1"), 1.0, None, ALU.add), d_cols)

        def pairs(u):
            return u.rearrange("p (j c) -> p j c", c=2)

        def twice(u):
            return u.unsqueeze(2).broadcast_to([P, 8, 2])

        def rows_out(hf, tk):
            b, o = 2 * hf, modr[:, 1024 * hf:1024 * hf + 1024]
            free[b] = act.do(lambda e: e.activation(o[:, 0:512], ps[b][0:2, :], ACT.Copy), tk)
            free[b + 1] = dve.do(lambda e: e.tensor_copy(o[:, 512:1024], ps[b + 1][0:2, :]), tk)
            return free[b], free[b + 1]

        def rows_turned(hf, waits):
            def body(e):
                for j in range(KT):
                    m = e.transpose(ps[2 * hf][:, 2 * j:2 * j + 2],
                                    modr[:, 1024 * hf + j * P:1024 * hf + (j + 1) * P], ident[0:2, 0:2])
                return m
            return pe.do(body, *waits)

        for n in range(16):
            t_row = mod_row_products(n)
            if n == 14:
                refill(2)
            if n in (1, 2):
                finish[n - 1]()
            if n == KT - 1:
                t_sh = rows_out(0, t_row)
            if 5 <= n < 9:
                turn_rows(0, 2 * (n - 5), 4 + (n - 5) % 4)
            if 9 <= n < 13:
                turn_rows(1, 2 * (n - 9), 4 + (n - 9) % 4)
            if n == 11:
                tk = rows_turned(0, t_sh)
                free[0] = dve.do(lambda e: e.tensor_tensor(pairs(modc), pairs(ps[0][:, 0:16]), twice(col("b_sh1")),
                                                           ALU.add), tk)
                t_modc = free[0]
        t_turn1 = turned1[-1]
        t_modT = rows_turned(1, rows_out(1, t_row))
        acc_free[0] = acc_free[1] = t_modT
        free[2] = dve.do(lambda e: e.tensor_tensor(pairs(A1), pairs(ps[2][:, 0:16]), twice(sc1b), ALU.add), t_modT,
                         t_sc1b)
        t_mod = dve.do(lambda e: e.tensor_tensor(pairs(A1), pairs(A1), twice(col("g_mix")), ALU.mult), free[2], t_modc)

        sc_free = [None] * 3
        t_T1 = {}

        def modulated(c, *ks):
            late = []

            def subtract(k, sl, f, *after):
                sc_free[k % 3] = dve.do(lambda e: e.tensor_tensor(Tl[:, k, sl], f, Th[:, k, sl], ALU.subtract), *after)
                t_T1[(c, k)] = sc_free[k % 3]

            for k in ks:
                f, j = sc[k % 3][:, 0:L], 2 * k + c
                src, sl = xT[:, k, c * L:(c + 1) * L], slice(c * L, (c + 1) * L)
                th = act.do(lambda e, k=k, j=j, src=src, sl=sl: e.activation(
                    Th[:, k, sl], src, ACT.Identity, bias=modc[:, j:j + 1], scale=A1[:, j:j + 1]), t_mod, t_xT[(c, k)])
                tf = dve.do(lambda e, f=f, j=j, src=src: e.tensor_scalar(
                    f, src, A1[:, j:j + 1], modc[:, j:j + 1], ALU.mult, ALU.add), t_mod, t_xT[(c, k)], sc_free[k % 3])
                late.append((k, sl, f, th, tf))
                if len(late) > 1:
                    subtract(*late.pop(0))
            subtract(*late.pop())

        modulated(0, *range(KT))
        s_b1 = sem("s_bias1")
        side(H[N_SPLIT + 13], "late", cols[:, EARLY:], t["cols"][:, EARLY:], s_late)
        d_late = (s_late, 16)

        UP = 8 + L + 8
        uT = big[:, 2048:2048 + 4 * UP].rearrange("p (g w) -> p g w", g=4)
        qT = big[:, 3200:4224].rearrange("p (a b) -> p a b", a=4)
        kT = big[:, 4224:6272].rearrange("p (a b) -> p a b", a=4)
        V = big[:, 6272:8320].rearrange("p (a b) -> p a b", a=4)
        t_uz = pool.do(lambda e: e.memset(big[:, 2048:2048 + 4 * UP], 0.0))
        t_u, t_q, t_k = [], [], []
        taken = {}

        def take(group):
            n = taken[tuple(group)] = taken.get(tuple(group), -1) + 1
            return group[n % len(group)]

        ALL = list(range(8))
        ROT = [4, 5, 6, 7]
        for g in range(4):
            b = take(ROT)
            if g == 0:
                tk = feed_by_k(wstat_k(b, 0, L), [[t_T1[(0, k)], free[b]] for k in range(KT)])
                modulated(1, g)
            else:
                tk = feed(wstat(b, 0, L), free[b], most=2)
                modulated(1, g)
            free[b] = act.do(lambda e, b=b, g=g: e.activation(uT[:, g, 8:8 + L], ps[b][:, 0:L], ACT.Copy), tk, t_uz)
            t_u.append(free[b])
        def mod_row(q, g, t_b, t_g, bb):
            def body(e):
                for n in range(2):
                    m = e.matmul(ps[bb[n]][:, :], ones[:, :], acc[q][:, n * 512:(n + 1) * 512], start=True,
                                 stop=True)
                return m
            tk = pe.do(body, acc_done[q], t_ones, free[bb[0]], free[bb[1]])
            if q == 0:
                acc_free[3] = tk

            def finish():
                for n in range(2):
                    sl = slice(n * 512, (n + 1) * 512)
                    tk2 = dve.do(lambda e, n=n, sl=sl: e.tensor_tensor(g[:, sl], ps[bb[n]][:, :], g[:, sl], ALU.add),
                                 tk, t_b)
                    free[bb[n]] = tk2
                    tk2 = dve.do(lambda e, sl=sl: e.tensor_tensor(g[:, sl], g[:, sl], gp[:, sl], ALU.mult), tk2, t_g)
                mod_rows[q] = tk2
            return finish

        mod_rows = {}

        def mod_row_sum(q, bb):
            def body(e):
                for n in range(2):
                    m = e.matmul(ps[bb[n]][0:1, :], ones[:, 0:1], acc[q][:, n * 512:(n + 1) * 512], start=True,
                                 stop=True)
                return m
            tk = pe.do(body, acc_done[q], t_ones, free[bb[0]], free[bb[1]])
            o = acc[q][0:1, :]
            free[bb[0]] = act.do(lambda e: e.activation(o[:, 0:512], ps[bb[0]][0:1, :], ACT.Copy), tk)
            free[bb[1]] = dve.do(lambda e: e.tensor_copy(o[:, 512:1024], ps[bb[1]][0:1, :]), tk)
            row_done[q] = free[bb[0]], free[bb[1]]

        def mod_col(q, dst, b):
            def body(e):
                for j in range(8):
                    m = e.transpose(ps[b][:, j:j + 1], acc[q][0:1, j * P:(j + 1) * P], ident[0:1, 0:1])
                return m
            tk = pe.do(body, *row_done[q], free[b])
            free[b] = dve.do(lambda e: e.tensor_tensor(dst, ps[b][:, 0:8], bias_of[q], ALU.add), tk)
            col_done[q] = free[b]

        row_done, col_done = {}, {}
        bias_of = {1: col("b_sh2"), 2: col("b_sc2")}
        s_g1, s_g2, s_gp = sem("s_g1"), sem("s_g2"), sem("s_gp")
        row = t["rows"]
        side(H[N_SPLIT + 16], "g1", G1[:, :], row[0:1, :].partition_broadcast(P), s_g1)
        side(H[N_SPLIT + 16], "gp", gp[:, :], row[1:2, :].partition_broadcast(P), s_gp)
        for a in range(4):
            b = take([0, 1, 2, 3])
            tk = feed(wstat(b, 0, L), free[b], most=2)
            modulated(1, 4 + a)
            free[b] = act.do(lambda e, b=b, a=a: e.activation(qT[:, a, :], ps[b][:, 0:L], ACT.Copy, scale=0.125), tk)
            t_q.append(free[b])

        t_T = t_T1[(1, KT - 1)]
        t_pw = pool.do(lambda e: e.memset(big[:, 8320:8320 + 4 * UP], 0.0), t_T)
        pw = [big[:, 8320 + i * UP:8320 + (i + 1) * UP] for i in range(4)]
        dT = big[:, 9408:10432].rearrange("p (g w) -> p g w", g=4)
        inv = big[:, 10432:11456].rearrange("p (g w) -> p g w", g=4)
        s_inv = sem("s_inv")
        side(H[N_SPLIT + 11], "inv", big[:, 10432:11456], t["invcnt"].partition_broadcast(P), s_inv)
        side(H[N_SPLIT + 15], "bias1", arena[:, 0:4096], t["bias1"], s_b1, t_turn1)
        side(H[N_SPLIT + 20], "g2", G2[:, :], row[2:3, :].partition_broadcast(P), s_g2)
        t_pool = []

        def window(g):
            nonlocal t_pw
            prev, tk = uT[:, g, :], t_u[g]
            for s in range(g + 1):
                a0, a1 = (1, 0) if s == 0 else (1 << (s - 1), 1 << (s - 1))
                o, e0, e1 = pw[s], a0 if s == 0 else a0 + 1, UP - a1
                tk = dve.do(lambda e, o=o, p=prev, e0=e0, e1=e1, a0=a0, a1=a1:
                            e.tensor_tensor(o[:, e0:e1], p[:, e0 - a0:e1 - a0], p[:, e0 + a1:e1 + a1], ALU.add),
                            tk, t_pw)
                prev = o
            tk = dve.do(lambda e: e.tensor_tensor(dT[:, g, :], prev[:, 8:8 + L], inv[:, g, :], ALU.mult),
                        tk, (s_inv, 16))
            t_pw = dve.do(lambda e: e.tensor_tensor(dT[:, g, :], dT[:, g, :], uT[:, g, 8:8 + L], ALU.subtract), tk)
            t_pool.append(t_pw)

        for a in range(4):
            b = take(ROT)
            tk = feed(wstat(b, 0, 512), t_T, free[b])
            free[b] = act.do(lambda e, b=b, a=a: e.activation(kT[:, a, :], ps[b][:, :], ACT.Copy), tk)
            t_k.append(free[b])
            window(a)
        sh2 = stat(8)
        vb = [0, 1, 2, 3]

        def pool_product(g):
            o = ps[6 + g % 2][:, g // 2 * L:(g // 2 + 1) * L]
            return o, pe.do(lambda e: e.matmul(o, col("pool_w", g * P, (g + 1) * P), dT[:, g, :], start=True, stop=True),
                            t_pool[g], d_late, free[6 + g % 2])

        def pool_out(g, o, tk):
            gain = col("pool_scale", g, g + 1)
            tk = act.do(lambda e: e.activation(Th[:, g, L:], o, ACT.Copy, scale=gain), tk, t_xused,
                        free[6 + g % 2])
            free[6 + g % 2] = dve.do(lambda e: e.scalar_tensor_tensor(out=Tl[:, g, L:], in0=o, scalar=gain, in1=Th[:, g, L:],
                                                           op0=ALU.mult, op1=ALU.subtract), tk)

        for j in range(4):
            lhs = [[xt(2 * j + i, 0, 0), xt(2 * j + i, 0, 1), xt(2 * j + i, L, 0), xt(2 * j + i, L, 1)]
                   for i in range(2)]
            if j == 3:
                pools = [pool_product(g) for g in range(4)]
            tk = feed(tstat([[b] for b in vb], lhs, 512, j == 0, j == 3), *[free[b] for b in vb])
        t_xused = tk
        load_table(ACT.Exp)
        t_v = []
        for i, b in enumerate(vb):
            free[b] = act.do(lambda e, b=b, i=i: e.activation(V[:, i, :], ps[b][:, :], ACT.Copy), tk)
            t_v.append(free[b])
        acc_free[2] = t_pool[3]

        SB, TB, OB = [4, 5], [6], [7]
        pt_read = [None, None]

        LAG = 4

        def attention(n_heads, tiles, s_mm, s_after, bias, b_after, scale, v_of, v_after, out_k, bufs, bufs_free,
                      fill):
            items = [(h, i) for h in range(n_heads) for i in range(2)]
            live = {}
            turned = {}
            done = []
            bufs_free = list(bufs_free)

            def scores(h, i):
                b = take(SB)
                n = tiles[i]
                s = (2 * h + i) % len(bufs)
                u = bufs[s][:, 0:n]
                tk = pe.do(lambda e: s_mm(e, ps[b], h, i, n), free[b], *s_after(h))
                m, r, ri = stat(1), stat(1), stat(1)
                tk = dve.do(lambda e: e.tensor_tensor_reduce(
                    out=u, in0=ps[b][:, 0:n], in1=bias(h, i, n), scale=-scale(h), scalar=3e38,
                    op0=ALU.add, op1=ALU.min, accum_out=m), tk, bufs_free[s], *b_after(h))
                free[b] = tk
                tk = act.do(lambda e: e.activation(u, u, ACT.Exp, bias=m, scale=-1.0, accum_out=r), tk)
                live[(h, i)] = (s, u, r, ri, tk)

            def normed(h, i):
                s, u, r, ri, tk = live.pop((h, i))
                tk = dve.do(lambda e: e.reciprocal(ri, r), tk)
                live[(h, i)] = (s, u, dve.do(lambda e: e.tensor_scalar(u, u, ri, None, ALU.mult), tk))

            def turn(h, i):
                s, u, tk = live.pop((h, i))
                b = take(TB)
                n = tiles[i] // P

                def body(e):
                    for c in range(n):
                        m = e.transpose(ps[b][:, c * P:(c + 1) * P], u[:, c * P:(c + 1) * P], ident)
                    return m
                tk = pe.do(body, tk, free[b])
                bufs_free[s] = tk
                sc_free[:] = [tk] * 3
                dst = PT[h % 2][:, 0:n, i * P:(i + 1) * P]
                src = ps[b][:, 0:n * P].rearrange("p (c q) -> p c q", c=n)
                if (2 * h + i) % 3 == 2:
                    tk = dve.do(lambda e: e.tensor_copy(dst, src), tk, pt_read[h % 2], *junk_free)
                else:
                    tk = act.do(lambda e: e.activation(dst, src, ACT.Copy), tk, pt_read[h % 2])
                free[b] = tk
                turned[(h, i)] = tk

            def values(h):
                if h % 2 == 0:
                    done.append(take(OB))
                b = done[-1]
                r0 = 64 * (h % 2)
                nk = tiles[1] // P

                def body(e):
                    for c in range(nk):
                        q0 = 0 if c * P < tiles[0] else P
                        m = e.matmul(ps[b][r0:r0 + 64, q0:L], v_of(h, c), PT[h % 2][:, c, q0:L], start=(c == 0),
                                     stop=(c == nk - 1), skip_group_check=True)
                    return m
                tk = pe.do(body, turned[(h, 0)], turned[(h, 1)], free[b], *v_after(h))
                pt_read[h % 2] = tk
                if h % 2 == 1:
                    k = out_k + h // 2
                    tk = act.do(lambda e: e.activation(Th[:, k, L:], ps[b][:, 0:L], ACT.Copy), tk)
                    free[b] = dve.do(lambda e: e.tensor_tensor(Tl[:, k, L:], ps[b][:, 0:L], Th[:, k, L:],
                                                               ALU.subtract), tk)
                    return free[b]
                return None

            out = []
            for n in range(len(items) + LAG + 1):
                if LAG <= n < len(items) + LAG:
                    turn(*items[n - LAG])
                if n > LAG and items[n - LAG - 1][1] == 1:
                    tk = values(items[n - LAG - 1][0])
                    if tk:
                        out.append(tk)
                if n < len(items):
                    scores(*items[n])
                if 1 <= n < len(items) + 1:
                    normed(*items[n - 1])
                for thunk in fill.get(n, ()):
                    thunk(out)
            return out

        def s1(e, o, h, i, n):
            r0 = 64 * (h % 2)
            return e.matmul(o[:, 0:n], qT[r0:r0 + 64, h // 2, i * P:(i + 1) * P], kT[r0:r0 + 64, h // 2, 0:n],
                            start=True, stop=True)

        def bias1(h, i, n):
            j = 8 * i + h
            a = arena[:, j * L:4352].rearrange("p (c w) -> p c w", w=L)
            return a[:, 0::(16 - j), :]

        ACC = [[0, 1], [2, 3]]

        def out_project(k, tiles, body_of, *after):
            h = out_h0[0] + k
            banks = [free[b] for i in tiles for b in ACC[i]] if k == 0 else []
            body = tstat([ACC[i] for i in tiles], [[xt(k, L, i) for i in tiles]], 512, k == 0, k == 7)
            return body_of(h, body, *after, *banks)

        out_h0 = [0]

        def whole(k, *after):
            refill()
            if k == 0:
                out_h0[0] = state["h"]
            state["h"] += 1
            return out_project(k, [0, 1], last_part, *after)

        def first_tile(k, *after):
            refill()
            state["h"] += 1
            return out_project(k, [0], part, *after)

        def second_tile(k):
            return out_project(k, [1], last_part)

        fill = {n: [lambda out, k=k: whole(k)] for n, k in ((4, 0), (5, 1), (7, 2), (9, 3))}
        fill.setdefault(12, []).append(lambda out: first_tile(4, out[0]))
        fill.setdefault(14, []).append(lambda out: first_tile(5, out[1]))
        fill.setdefault(17, []).append(lambda out: first_tile(6, out[2]))
        for n in range(24):
            n < 16 or fill.setdefault(n - 14, []).append(lambda out: state["m"] < 24 and sum_mod())
        bufs1 = [s[:, :] for s in sc] + [big[:, 8320 + 512 * n:8320 + 512 * (n + 1)] for n in range(2)]
        def start_G1(out):
            for g in range(4):
                pool_out(g, *pools[g])
            finish_G1.append(mod_row(0, G1, (s_g1, 16), (s_gp, 16), [0, 1]))

        finish_G1 = []
        sc2, A2 = stat(8), stat(8)
        fill[0] = [start_G1]
        fill[1] = [lambda out: finish_G1[0]()]
        fill.setdefault(16, []).append(lambda out: mod_row_sum(1, SB))
        fill.setdefault(17, []).append(lambda out: mod_row_sum(2, SB))
        fill.setdefault(18, []).extend([lambda out: mod_col(1, sh2, 4), lambda out: mod_col(2, sc2, 4)])
        heads1 = attention(8, (512, 512), s1, lambda h: (t_q[h // 2], t_k[h // 2]),
                           bias1, lambda h: [(s_b1, 16), t_zero], lambda h: 1.0,
                           lambda h, c: V[:, c, h * 64:(h + 1) * 64], lambda h: t_v, 4, bufs1, sc_free + t_pool[3:] * 2, fill)
        t_attn1 = heads1[-1]
        t_G1 = mod_rows[0]
        side(H[N_SPLIT + 26], "gp2", gp[:, :], row[3:4, :].partition_broadcast(P), s_gp, mod_rows[0])
        t_sh2, t_sc2 = col_done[1], col_done[2]
        t_A2 = dve.do(lambda e: e.scalar_tensor_tensor(out=A2, in0=sc2, scalar=1.0, in1=col("g_mlp"), op0=ALU.add,
                                                       op1=ALU.mult), t_sc2)

        def row_scale(parts, after):
            s, v, r = stat(2), stat(1), stat(1)
            for n in range(2):
                tk = square_sum(parts[n], 512, 1 / 32, s[:, n:n + 1], after[n])
            tk = dve.do(lambda e: e.tensor_scalar(v, s[:, 0:1], s[:, 1:2], EPS, ALU.add, ALU.add), tk)
            return r, rsqrt(r, v, 1, tk)

        def add_normed(g, t_g):
            def add(i, after):
                s, v, r = stat(2), stat(1), stat(1)
                b0, b1 = ACC[i]
                t0 = square_sum(ps[b0][:, :], 512, 1 / 32, s[:, 0:1], after)
                t1 = dve.do(lambda e: e.tensor_tensor(sc[1][:, :], ps[b1][:, :], g[:, 512:1024], ALU.mult), after, t_g,
                            sc_free[1])
                free[b1] = square_sum(ps[b1][:, :], 512, 1 / 32, s[:, 1:2], t1)
                free[b0] = dve.do(lambda e: e.tensor_tensor(sc[0][:, :], ps[b0][:, :], g[:, 0:512], ALU.mult), t0, t_g,
                                  sc_free[0])
                tk = dve.do(lambda e: e.tensor_scalar(v, s[:, 0:1], s[:, 1:2], EPS, ALU.add, ALU.add), free[b1])
                tr = rsqrt(r, v, 1, tk)
                yield
                for n, ready_n in enumerate((free[b0], t1)):
                    sl = slice(n * 512, (n + 1) * 512)
                    sc_free[n] = dve.do(lambda e, n=n, sl=sl: e.scalar_tensor_tensor(
                        out=x[:, i, sl], in0=sc[n][:, :], scalar=r, in1=x[:, i, sl], op0=ALU.mult, op1=ALU.add),
                        tr, ready_n)
                return sc_free[0:2]
            return add

        def add_scaled(c):
            def add(i, after):
                for n in range(2):
                    b, sl = ACC[i][n], slice(n * 512, (n + 1) * 512)
                    free[b] = dve.do(lambda e, b=b, sl=sl: e.scalar_tensor_tensor(
                        out=x[:, i, sl], in0=ps[b][:, :], scalar=c, in1=x[:, i, sl], op0=ALU.mult, op1=ALU.add),
                        after)
                yield
                return [free[b] for b in ACC[i]]
            return add

        def add_and_norm(i, add, after, *xn_free):
            t_x = yield from add(i, after)
            r, tr = row_scale([x[:, i, 0:512], x[:, i, 512:1024]], t_x)
            yield
            t0 = dve.do(lambda e: e.tensor_scalar(xn[:, i, 0:512], x[:, i, 0:512], r, None, ALU.mult), tr, *xn_free)
            t1 = act.do(lambda e: e.activation(xn[:, i, 512:1024], x[:, i, 512:1024], ACT.Copy, scale=r), tr, *xn_free)
            return t0, t1

        def run(steps, between):
            while True:
                try:
                    next(steps)
                except StopIteration as end:
                    return end.value
                between()

        def turn_tile(i, t_n, banks, gain, shift):
            out, late = [], []
            cols_i = slice(i * P, (i + 1) * P)

            def subtract(k, f, *after):
                f4_free[k % 4] = dve.do(lambda e: e.tensor_tensor(Tl[:, k, cols_i], f, Th[:, k, cols_i],
                                                                  ALU.subtract), *after)
                return f4_free[k % 4]

            for k in range(KT):
                b = take(banks)
                src = ps[b][:, 0:P]
                tk = pe.do(lambda e, k=k, src=src: e.transpose(src, xn[:, i, k * P:(k + 1) * P], ident),
                           t_n[k // 4], free[b])
                t_turned[i] = tk
                if shift is None:
                    th = act.do(lambda e, k=k, src=src: e.activation(Th[:, k, cols_i], src, ACT.Copy,
                                                                     scale=gain[:, k:k + 1]), tk)
                    tk = dve.do(lambda e, k=k, src=src: e.scalar_tensor_tensor(
                        out=Tl[:, k, cols_i], in0=src, scalar=gain[:, k:k + 1], in1=Th[:, k, cols_i],
                        op0=ALU.mult, op1=ALU.subtract), th)
                    free[b] = tk
                else:
                    f, j = sc[2][:, (k % 4) * P:(k % 4 + 1) * P], k % 4
                    th = act.do(lambda e, k=k, src=src: e.activation(
                        Th[:, k, cols_i], src, ACT.Identity, bias=shift[:, k:k + 1], scale=gain[:, k:k + 1]), tk)
                    free[b] = dve.do(lambda e, k=k, src=src, f=f: e.tensor_scalar(
                        f, src, gain[:, k:k + 1], shift[:, k:k + 1], ALU.mult, ALU.add), th, sc_free[2], f4_free[j])
                    late.append((k, f, th, free[b]))
                    if k == 0:
                        continue
                    tk = subtract(*late.pop(0))
                out.append(tk)
            if late:
                out.append(subtract(*late.pop()))
            return out

        f4_free = [None] * 4
        t_turned = [None, None]

        def boundary(first, second, add, gain, shift, ahead, n_w, *after):
            for thunk in first:
                tk = thunk()
            rest = add_and_norm(0, add, tk, *after)
            next(rest)
            for thunk in second:
                tk = thunk()
            t_n = run(rest, lambda: refill(1))
            rest = add_and_norm(1, add, tk, *after)
            next(rest)
            ta = turn_tile(0, t_n, [0, 1] + [b for b in ROT if b not in ahead], gain, shift)
            refill(1)
            t_n = run(rest, lambda: refill(1))
            h0 = state["h"]
            state["h"] += 4
            while h0 + 3 not in ready:
                refill(1)
            refill()

            def products(i, c):
                return tstat([[ahead[i]]], [[xt(2 * c + j, 0, i)] for j in range(2)], n_w, c == 0, c == 3)

            for c in range(4):
                t0 = part(h0 + c, products(0, c), *ta[2 * c:2 * c + 2], free[ahead[0]])
            tb = turn_tile(1, t_n, [0, 1, 2, 3], gain, shift)
            for c in range(4):
                t1 = last_part(h0 + c, products(1, c), *tb[2 * c:2 * c + 2], free[ahead[1]])
            return t0, t1

        t_T = boundary([lambda: first_tile(7, t_attn1)], [lambda k=k: second_tile(k) for k in range(4, 8)],
                       add_normed(G1, t_G1), A2, sh2, [4, 5], 512, t_A2, t_sh2, t_attn1)

        fbuf = [PT[0][:, i, :] for i in range(4)]
        rbuf = [PT[1][:, i, :] for i in range(4)]
        f_free, r_free = [None] * 4, [None] * 4

        def hidden_parts(f, tk):
            i, j = f % 4, f % 8
            th = act.do(lambda e: e.activation(Th[:, j, L:], fbuf[i], ACT.Copy), tk, down_done.get(f - 8))
            tl = dve.do(lambda e: e.tensor_tensor(Tl[:, j, L:], fbuf[i], Th[:, j, L:], ALU.subtract), th)
            f_free[i] = tl
            return tl

        def down(f, t_h):
            j = f % 8
            down_done[f] = feed(tstat(ACC, [[xt(j, L, 0), xt(j, L, 1)]], 512, f == 0, False), t_h,
                                *([free[b] for r in ACC for b in r] if f == 0 else []))

        def tail(n):
            refill()
            h0 = state["h"]
            state["h"] += TAIL

            def products(c, i, body_of):
                f = n - TAIL + c
                return body_of(h0 + c, tstat([ACC[i]], [[xt(f % 8, L, i)]], 512, False, c == TAIL - 1), hid[f])

            return ([lambda c=c: products(c, 0, part) for c in range(TAIL)],
                    [lambda c=c: products(c, 1, last_part) for c in range(TAIL)])

        def hidden_rows(made, n):
            for g in range(n // 2):
                def body(e, g=g):
                    for f in range(2):
                        for i in range(2):
                            m = e.transpose(ps[6 + g][:, f * L + i * P:f * L + (i + 1) * P],
                                            rows_of(PT[0], i)[:, (2 * g + f) * P:(2 * g + f + 1) * P], ident)
                    return m
                tk = pe.do(body, *made, free[6 + g])
                f_free[:] = [tk] * 4
                dst = slice(2 * g, 2 * g + 2)
                src = ps[6 + g][:, :].rearrange("p (f w) -> p f w", f=2)
                tk = act.do(lambda e, dst=dst, src=src: e.activation(Th[:, dst, L:], src, ACT.Copy), tk)
                free[6 + g] = dve.do(lambda e, dst=dst, src=src: e.tensor_tensor(Tl[:, dst, L:], src, Th[:, dst, L:],
                                                                                 ALU.subtract), tk)
                hid[2 * g] = hid[2 * g + 1] = free[6 + g]

        def rows_of(buf, i):
            return buf[:, 2 * i:2 * i + 2, :].rearrange("p a b -> p (a b)")

        down_done = {}
        hid = {}
        t_G2 = None
        made = []
        for i in range(2):
            r, f = rows_of(PT[1], i), rows_of(PT[0], i)
            free[4 + i] = act.do(lambda e, i=i, r=r: e.activation(r, ps[4 + i][:, :], ACT.Relu), t_T[i], *junk_free)
            made.append(dve.do(lambda e, r=r, f=f: e.tensor_tensor(f, r, r, ALU.mult), free[4 + i], *pt_read))
        r_free[:] = made[1:] * 4
        for what, f in mlp_order(FM, MLP_LAG):
            if what == "up" and f >= 4:
                i = f % 4
                b = 4 if f == 4 else take(ROT)
                tk = feed(wstat(b, 0, L), free[b], most=2)
                if f == 4:
                    hidden_rows(made, 4)
                if f == 8:
                    load_table(ACT.Silu)
                free[b] = act.do(lambda e, b=b, i=i: e.activation(rbuf[i], ps[b][:, 0:L], ACT.Relu), tk, r_free[i])
                tk = dve.do(lambda e, i=i: e.tensor_tensor(fbuf[i], rbuf[i], rbuf[i], ALU.mult), free[b], f_free[i])
                r_free[i] = tk
                hid[f] = hidden_parts(f, tk)
            elif what == "up":
                pass
            elif f < FM - TAIL:
                down(f, hid[f])
                if f == 24:
                    refill()
                    assert state["m"] == 32
                    mod_row(3, G2, (s_g2, 16), (s_gp, 32), [6, 7])()
                    t_G2 = mod_rows[3]
        junk_free[0] = junk_free[1] = r_free[3]
        side(next(n for n, c in enumerate(plan) if c[0] == "ffn1_gate") + 8, "gp3", gp[:, :], t["rows"][4:5, :].partition_broadcast(P), s_gp, t_G2)
        t_T = boundary(*tail(FM), add_normed(G2, t_G2), col("g_ffn1"), None, [4, 5], 512)

        def swiglu(t_T):
            down_done.clear()
            hid.clear()
            made = []
            for i in range(2):
                r, f = rows_of(PT[1], i)[:, 0:L], rows_of(PT[0], i)[:, 0:L]
                tk = act.do(lambda e, i=i, r=r: e.activation(r, ps[4 + i][:, 0:L], ACT.Silu), t_T[i], *junk_free)
                free[4 + i] = dve.do(lambda e, i=i, r=r, f=f: e.tensor_tensor(f, r, ps[4 + i][:, L:], ALU.mult), tk,
                                     *f_free, *pt_read)
                made.append(free[4 + i])
            r_free[:] = made[1:] * 4
            for what, f in mlp_order(F2, FFN_LAG):
                if what == "up" and f >= 2:
                    i = f % 4
                    bg, bu = (4, 5) if f == 2 else (take(ROT), take(ROT))
                    tk = feed(wstat(bg, 0, L), free[bg], most=2)
                    if f == 2:
                        hidden_rows(made, 2)
                    free[bg] = act.do(lambda e, b=bg, i=i: e.activation(rbuf[i], ps[b][:, 0:L], ACT.Silu), tk,
                                      r_free[i])
                    tg = free[bg]
                    tk = feed(wstat(bu, 0, L), free[bu], most=2)
                    free[bu] = dve.do(lambda e, b=bu, i=i: e.tensor_tensor(fbuf[i], rbuf[i], ps[b][:, 0:L], ALU.mult),
                                      tk, tg, f_free[i])
                    r_free[i] = free[bu]
                    hid[f] = hidden_parts(f, free[bu])
                elif what == "up":
                    pass
                elif f < F2 - TAIL:
                    down(f, hid[f])
            junk_free[0] = junk_free[1] = r_free[(F2 - 1) % 4]
            return tail(F2)

        LB = [6, 7]

        t_l = boundary(*swiglu(t_T), add_scaled(0.5), col("g_mix2"), None, LB, 416)

        t_x_last = t_l[1]
        s_bA = sem("s_biasA")
        n0 = next(n for n, c in enumerate(plan) if c[0] == "w_uq")
        side(n0, "biasA", arena[:, 0:4096], t["bias2"], s_bA, t_turned[1])
        qTa = big[:, 0:1024].rearrange("p (a b) -> p a b", a=4)
        kTa = big[:, 1024:2048].rearrange("p (a b) -> p a b", a=4)
        Va = big[:, 2048:3072].rearrange("p (a b) -> p a b", a=2)
        qTb = big[:, 3072:5120].rearrange("p (a b) -> p a b", a=8)
        kTb = big[:, 5120:7168].rearrange("p (a b) -> p a b", a=8)
        Vb = big[:, 7168:8192].rearrange("p (a b) -> p a b", a=2)
        qf = big[:, 8192:9728].rearrange("p (t h d) -> p t h d", t=2, h=8)
        kf = big[:, 9728:11264].rearrange("p (t h d) -> p t h d", t=2, h=8)
        ropet = big[:, 11264:11520].rearrange("p (t h d) -> p t h d", t=1, h=8)[:, 0]
        rab = [stat(256).rearrange("p (h d) -> p h d", h=8), stat(256).rearrange("p (h d) -> p h d", h=8)]
        qn = [G2[:, 0:512], G2[:, 512:1024]]
        qn_free = [t_x_last, t_x_last]
        sq = [G1[:, 0:512], G1[:, 512:1024]]
        sq_free = [t_x_last, t_x_last]
        sqn = [0]

        def squares(src, shape, *after):
            i = sqn[0] % 2
            sqn[0] += 1
            n = shape[0] * shape[1]
            o = sq[i][:, 0:n].rearrange("p (h d) -> p h d", h=shape[0])
            return i, o, act.do(lambda e: e.activation(o, src, ACT.Square), sq_free[i], *after)

        def inv_rms(src, n, d, *after):
            v, r = stat(n), stat(n)
            tk = dve.do(lambda e: e.tensor_scalar(v, src, 1.0 / d, EPS, ALU.mult, ALU.add), *after)
            return r, rsqrt(r, v, n, tk)

        cq, sq_t, ck, sk = (big[:, 11520 + 64 * i:11520 + 64 * (i + 1)].rearrange("p (t d) -> p t d", t=2)
                            for i in range(4))
        t_rot = []
        for dst, tab, g in ((cq, "cos2", "g_qr"), (sq_t, "sin2", "g_qr"), (ck, "cos2", "g_kr"), (sk, "sin2", "g_kr")):
            t_rot.append(dve.do(lambda e, dst=dst, tab=tab, g=g: e.tensor_tensor(
                dst, col(tab).rearrange("p (t d) -> p t d", t=2), col(g).unsqueeze(1).broadcast_to([P, 2, 32]),
                ALU.mult), t_attn1, d_late))
        t_rot = t_rot[-1]
        gq8 = stat(1)
        t_gq8 = dve.do(lambda e: e.tensor_scalar(gq8, col("g_aq"), 0.125, None, ALU.mult))

        def by_row(banks, n_w):
            out = []
            for j in range(4):
                lhs = [[xt(2 * j + i, 0, 0), xt(2 * j + i, 0, 1)] for i in range(2)]
                body = tstat([[b] for b in banks], lhs, n_w, j == 0, j == 3)
                out.append(lambda body=body, j=j: feed(body, *([free[b] for b in banks] if j == 0 else [])))
            return out

        QB, KB, VB = [4, 5], [6, 7], [4, 5]
        FB = [[0, 1], [2, 3]]

        qln = [PT[1][:, 0:2, :].rearrange("p a b -> p (a b)")[:, 0:384],
               PT[1][:, 2:4, :].rearrange("p a b -> p (a b)")[:, 0:384]]
        krn = stat(64)
        t_lat, t_L = [], []

        def latents_a(tk):
            s, v, r = stat(6), stat(6), stat(6)
            for i in range(2):
                for n, (c0, c1) in enumerate(((0, 256), (256, 384), (384, 416))):
                    j = sqn[0] % 2
                    sqn[0] += 1
                    tq = act.do(lambda e, i=i, n=n, c0=c0, c1=c1, j=j: e.activation(
                        sq[j][:, 0:c1 - c0], ps[LB[i]][:, c0:c1], ACT.Square,
                        accum_out=s[:, 3 * i + n:3 * i + n + 1]), tk, sq_free[j])
                    sq_free[j] = tq
            tq = dve.do(lambda e: e.tensor_tensor(v, s, col("invd", 0, 6), ALU.mult), tq)
            tq = dve.do(lambda e: e.tensor_scalar(v, v, EPS, None, ALU.add), tq)
            return r, rsqrt(r, v, 6, tq)

        def latents_b(r, tq):
            for i in range(2):
                for n, (c0, c1, dst) in enumerate(((0, 256, qln[i][:, 0:256]), (256, 384, qln[i][:, 256:384]),
                                                   (384, 416, krn[:, 32 * i:32 * i + 32]))):
                    tn = dve.do(lambda e, i=i, n=n, c0=c0, c1=c1, dst=dst: e.tensor_scalar(
                        dst, ps[LB[i]][:, c0:c1], r[:, 3 * i + n:3 * i + n + 1], None, ALU.mult), tq, *junk_free)
                free[LB[i]] = tn
                t_lat.append(tn)

        def latents_turn():
            for c, g in ((0, col("g_ql", 0, 1)), (1, col("g_ql", 1, 2)), (2, col("g_kvl"))):
                def body(e, c=c):
                    for i in range(2):
                        m = e.transpose(ps[c][:, i * P:(i + 1) * P], qln[i][:, c * P:(c + 1) * P], ident)
                    return m
                tt = pe.do(body, *t_lat, free[c])
                junk_free[0] = junk_free[1] = tt
                tt = act.do(lambda e, c=c, g=g: e.activation(Th[:, c, L:], ps[c][:, 0:L], ACT.Copy, scale=g), tt)
                free[c] = dve.do(lambda e, c=c, g=g: e.scalar_tensor_tensor(
                    out=Tl[:, c, L:], in0=ps[c][:, 0:L], scalar=g, in1=Th[:, c, L:], op0=ALU.mult,
                    op1=ALU.subtract), tt)
                t_L.append(free[c])

        def qk_a(banks, tk):
            out = []
            for i in range(2):
                j, o, tq = squares(ps[banks[i]][:, :].rearrange("p (h d) -> p h d", h=8), (8, 64), tk)
                s = stat(8)
                tq = dve.do(lambda e, o=o, s=s: e.tensor_reduce(s, o, AX_X, ALU.add), tq)
                sq_free[j] = tq
                out.append(inv_rms(s, 8, 64, tq))
            return out

        def qk_b(banks, scales):
            out = []
            for i, (r, tq) in enumerate(scales):
                b = banks[i]
                free[b] = dve.do(lambda e, i=i, b=b, r=r: e.tensor_tensor(
                    qn[i].rearrange("p (h d) -> p h d", h=8), ps[b][:, :].rearrange("p (h d) -> p h d", h=8),
                    r.unsqueeze(2).broadcast_to([P, 8, 64]), ALU.mult), tq, qn_free[i])
                out.append(free[b])
            return out

        def qk_turn(banks, tns, dstT, g, t_g):
            out = []
            for i in range(2):
                b = banks[i]

                def body(e, i=i, b=b):
                    for a in range(4):
                        m = e.transpose(ps[b][:, a * P:(a + 1) * P], qn[i][:, a * P:(a + 1) * P], ident)
                    return m
                tt = pe.do(body, tns[i], free[b])
                qn_free[i] = tt
                free[b] = act.do(lambda e, i=i, b=b: e.activation(
                    dstT[:, :, i * P:(i + 1) * P], ps[b][:, :].rearrange("p (a q) -> p a q", a=4), ACT.Copy,
                    scale=g), tt, t_g, t_attn1)
                out.append(free[b])
            return out

        t_qf, t_kf, t_vb = [[], []], [[], []], []
        rope_free = [None]
        scale_of = {}

        def rotate(i, src, cos, sin, heads, dst, *after):
            a, b = (u[:, 0:heads, :] for u in rab)
            ta = pool.do(lambda e: e.tensor_tensor(a, src, cos[:, i, :].unsqueeze(1).broadcast_to([P, heads, 32]),
                                                  ALU.mult), *after, rope_free[0], t_rot)
            tb = pool.do(lambda e: e.tensor_tensor(b, src, sin[:, i, :].unsqueeze(1).broadcast_to([P, heads, 32]),
                                                  ALU.mult), ta)

            def wide(u, c0):
                v = u[:, :, c0:c0 + 16]
                return v.broadcast_to([P, 8, 16]) if heads == 1 else v
            t1 = pool.do(lambda e: e.tensor_tensor(dst[:, :, 64:80], wide(a, 0), wide(b, 16), ALU.subtract), tb)
            rope_free[0] = pool.do(lambda e: e.tensor_tensor(dst[:, :, 80:96], wide(b, 0), wide(a, 16), ALU.add), t1)
            return rope_free[0]

        def q_heads_a(i, n, tk):
            src = ps[FB[i][n]][:, 0:384].rearrange("p (h d) -> p h d", h=4)
            j, o, tq = squares(src, (4, 96), tk)
            s, v, r = stat(8), stat(8), stat(8)
            ta = dve.do(lambda e: e.tensor_reduce(s[:, 0:4], o[:, :, 0:64], AX_X, ALU.add), tq)
            tq = dve.do(lambda e: e.tensor_reduce(s[:, 4:8], o[:, :, 64:96], AX_X, ALU.add), tq)
            sq_free[j] = tq
            dve.do(lambda e: e.tensor_scalar(v[:, 0:4], s[:, 0:4], 1 / 64, EPS, ALU.mult, ALU.add), ta)
            tq = dve.do(lambda e: e.tensor_scalar(v[:, 4:8], s[:, 4:8], 1 / 32, EPS, ALU.mult, ALU.add), tq)
            scale_of["q", i, n] = (r, rsqrt(r, v, 8, tq))

        def q_heads_b(i, n):
            b = FB[i][n]
            src = ps[b][:, 0:384].rearrange("p (h d) -> p h d", h=4)
            r, tq = scale_of["q", i, n]
            t_qf[i].append(dve.do(lambda e: e.tensor_tensor(
                qf[:, i, 4 * n:4 * n + 4, 0:64], src[:, :, 0:64], r[:, 0:4].unsqueeze(2).broadcast_to([P, 4, 64]),
                ALU.mult), tq))
            free[b] = dve.do(lambda e: e.tensor_tensor(
                ropet[:, 4 * n:4 * n + 4, :], src[:, :, 64:96], r[:, 4:8].unsqueeze(2).broadcast_to([P, 4, 32]),
                ALU.mult), tq, rope_free[0])
            if n == 1:
                t_qf[i].append(rotate(i, ropet, cq, sq_t, 8, qf[:, i], free[b]))

        t_kv = [None]

        def keys_values():
            t_kv[0] = feed(tstat(FB, [[xt(2, L, 0), xt(2, L, 1)]], 512, True, True), *t_L,
                           *[free[b] for r in FB for b in r])

        def k_heads_a(i, n):
            b = FB[i][n]
            src = ps[b][:, :].rearrange("p (h d) -> p h d", h=4)
            j, o, tq = squares(src[:, :, 0:64], (4, 64), t_kv[0])
            free[b] = act.do(lambda e: e.activation(
                Vb[:, i, n * 256:(n + 1) * 256].rearrange("p (h d) -> p h d", h=4), src[:, :, 64:128], ACT.Copy),
                t_kv[0])
            t_vb.append(free[b])
            scale_of["k", i, n] = (j, o, tq)

        def k_heads_b(i, n):
            j, o, tq = scale_of["k", i, n]
            s = stat(4)
            tq = dve.do(lambda e: e.tensor_reduce(s, o, AX_X, ALU.add), tq)
            sq_free[j] = tq
            scale_of["k", i, n] = inv_rms(s, 4, 64, tq)

        def k_heads_c(i, n):
            b = FB[i][n]
            src = ps[b][:, :].rearrange("p (h d) -> p h d", h=4)
            r, tq = scale_of["k", i, n]
            free[b] = dve.do(lambda e: e.tensor_tensor(
                kf[:, i, 4 * n:4 * n + 4, 0:64], src[:, :, 0:64], r.unsqueeze(2).broadcast_to([P, 4, 64]),
                ALU.mult), tq, free[b])
            t_kf[i].append(free[b])

        t_qb, t_kb = [], []

        def turn_heads(src, dst, g, tin, tout, i, n):
            b = FB[i][n]

            def body(e):
                for h in range(4):
                    m = e.transpose(ps[b][0:96, h * P:(h + 1) * P], src[:, i, 4 * n + h, :], ident)
                return m
            tt = pe.do(body, *tin[i], free[b])
            o = dst[0:96, 4 * n:4 * n + 4, i * P:(i + 1) * P]
            v = ps[b][0:96, :].rearrange("p (h q) -> p h q", h=4)
            gc = cols[0:96, COLS[g][0]:COLS[g][0] + 1]
            free[b] = act.do(lambda e: e.activation(o, v, ACT.Copy, scale=gc), tt)
            tout.append(free[b])

        refill(2)
        lat = latents_a(t_l[1])
        q4 = by_row(QB, 512)
        q4[0]()
        q4[1]()
        latents_b(*lat)
        q4[2]()
        tk = q4[3]()
        latents_turn()
        for i in range(2):
            t_kf[i].append(rotate(i, krn[:, 32 * i:32 * i + 32].unsqueeze(1), ck, sk, 1, kf[:, i], t_lat[i]))
        scales = qk_a(QB, tk)
        k4 = by_row(KB, 512)
        k4[0]()
        k4[1]()
        tns = qk_b(QB, scales)
        k4[2]()
        tk = k4[3]()
        load_table(ACT.Exp)
        t_qa = qk_turn(QB, tns, qTa, gq8, t_gq8)
        scales = qk_a(KB, tk)
        for k in range(2):
            t_uq = feed(tstat(FB, [[xt(k, L, 0), xt(k, L, 1)]], 384, k == 0, k == 1), *t_L,
                        *[free[b] for r in FB for b in r])
        v4 = by_row(VB, 512)
        v4[0]()
        tns = qk_b(KB, scales)
        for n in range(2):
            q_heads_a(0, n, t_uq)
        v4[1]()
        t_ka = qk_turn(KB, tns, kTa, col("g_ak"), None)
        for n in range(2):
            q_heads_a(1, n, t_uq)
        v4[2]()
        for n in range(2):
            q_heads_b(0, n)
        tk = v4[3]()
        t_va = []
        for i, b in enumerate(VB):
            free[b] = act.do(lambda e, b=b, i=i: e.activation(Va[:, i, :], ps[b][:, :], ACT.Copy), tk)
            t_va.append(free[b])
        refill()

        def sA(e, o, h, i, n):
            r0 = 64 * (h % 2)
            return e.matmul(o[:, 0:n], qTa[r0:r0 + 64, h // 2, i * P:(i + 1) * P], kTa[r0:r0 + 64, h // 2, 0:n],
                            start=True, stop=True)

        def sB(e, o, h, i, n):
            return e.matmul(o[:, 0:n], qTb[0:96, h, i * P:(i + 1) * P], kTb[0:96, h, 0:n], start=True, stop=True)

        def biasA(h, i, n):
            j = 8 * i + h
            return arena[:, j * L:j * L + n]

        mask = col("mask").rearrange("p (t w) -> p t w", t=2)
        fill = {}

        def at_step(n, fn, *args):
            fill.setdefault(n, []).append(lambda out: fn(*args))

        for m, (i, c) in enumerate([(0, 0), (0, 1), (1, 0), (1, 1)]):
            if i == 1:
                at_step(c, q_heads_b, i, c)
            at_step(2 + m + i, turn_heads, qf, qTb, "g_bq", t_qf, t_qb, i, c)
            at_step(9 + m, k_heads_a, i, c)
            at_step(9 + m, k_heads_b, i, c)
            at_step(10 + m, k_heads_c, i, c)
            at_step(11 + m, turn_heads, kf, kTb, "g_bk", t_kf, t_kb, i, c)
        at_step(7, keys_values)
        at_step(32, load_table, ACT.Silu)
        for n, k in ((17, 0), (19, 1), (21, 2), (25, 3)):
            at_step(n, whole, k)
        for n, k in ((28, 4), (29, 5), (33, 6)):
            fill.setdefault(n, []).append(lambda out, k=k: first_tile(k, out[k]))
        bufs2 = [sc[n % 3][:, L * (n // 3):L * (n // 3 + 1)] for n in range(6)]
        heads2 = attention(
            16, (128, 256), lambda e, o, h, i, n: sA(e, o, h, i, n) if h < 8 else sB(e, o, h - 8, i, n),
            lambda h: (*t_qa, *t_ka) if h < 8 else (*t_qb, *t_kb),
            lambda h, i, n: biasA(h, i, n) if h < 8 else mask[:, i, 0:n], lambda h: [(s_bA, 16) if h < 8 else d_late],
            lambda h: 1.0 if h < 8 else float(96 ** -0.5),
            lambda h, c: (Va if h < 8 else Vb)[:, c, (h % 8) * 64:(h % 8 + 1) * 64],
            lambda h: t_va if h < 8 else t_vb, 0, bufs2, sc_free * 2, fill)
        t_T = boundary([lambda: first_tile(7, heads2[-1])], [lambda k=k: second_tile(k) for k in range(4, 8)],
                       add_scaled(1.0), col("g_ffn2"), None, [4, 5], 512, heads2[-1])
        for i in range(4):
            f_free[i] = pt_read[0]
            r_free[i] = pt_read[1]
        first, second = swiglu(t_T)
        add = add_scaled(0.5)

        s_out = sem("s_out")

        def last_norm(i, after):
            t_x = run(add(i, after), lambda: None)
            r, tr = row_scale([x[:, i, 0:512], x[:, i, 512:1024]], t_x)
            for n in range(2):
                sl = slice(n * 512, (n + 1) * 512)
                tk = dve.do(lambda e, sl=sl: e.tensor_tensor(xn[:, i, sl], x[:, i, sl], gp[:, sl], ALU.mult),
                            t_x[n], (s_gp, 48))
                if n == 0:
                    tk = act.do(lambda e, sl=sl: e.activation(xn[:, i, sl], xn[:, i, sl], ACT.Copy, scale=r), tr, tk)
                else:
                    tk = dve.do(lambda e, sl=sl: e.tensor_scalar(xn[:, i, sl], xn[:, i, sl], r, None, ALU.mult), tr, tk)
                extra.setdefault("end", []).append((i, sl, tk))

        for i, thunks in enumerate((first, second)):
            for thunk in thunks:
                tk = thunk()
            last_norm(i, tk)

        assert state["h"] == len(H), (state["h"], len(H))

        for n, (name, j, w, kind) in enumerate(plan):
            for item in extra.get(n, ()):
                dst, src, s = item[1], item[2], item[3]
                sp.go(lambda e, dst=dst, src=src, s=s: e.dma_start(dst, src).then_inc(s, 16), *item[4:])
            sp.go(lambda e, n=n, name=name, j=j, w=w: e.dma_start(raw[n % RAW][:, 0:w], t[name][j, :, :])
                  .then_inc(s_raw[n % RAW], 16), freed.get(n - RAW))
        for i, sl, tk in extra["end"]:
            sp.go(lambda e, i=i, sl=sl: e.dma_start(t["out"][i * P:(i + 1) * P, sl], xn[:, i, sl])
                  .then_inc(s_out, 16), tk)

        block = ctx.enter_context(nc.Block())

        @block.sync
        def _(e):
            sp.play(e)
            e.wait_ge(s_out, 64)

        @block.scalar
        def _(e):
            act.play(e)

        @block.vector
        def _(e):
            dve.play(e)

        @block.gpsimd
        def _(e):
            pool.play(e)

        @block.tensor
        def _(e):
            pe.play(e)


def _column(v):
    return v.reshape(-1, P).T


def _tiles(w):
    k, j = w.shape[0] // P, w.shape[1] // P
    return np.ascontiguousarray(w.reshape(k, P, j, P).transpose(2, 1, 0, 3).reshape(j, P, k * P))


def _rows(w):
    return np.ascontiguousarray(w.reshape(-1, P, w.shape[1]))


def _row_pairs(w):
    k, c = w.shape[0] // P, w.shape[1]
    return np.ascontiguousarray(w.reshape(k // 2, 2, P, c).transpose(0, 2, 1, 3).reshape(k // 2, P, 2 * c))


def _bias1(rpb):
    out = np.full((8, 4, 64, 4, 64), NEG, np.float32)
    qc = np.arange(64)
    start = np.clip(qc - 8, 0, 48)
    for qr in range(4):
        for kr in range(4):
            for c in range(64):
                k0 = start[c]
                out[:, qr, c, kr, k0:k0 + 16] = rpb[:, kr - qr + 7, k0 - c + 15:k0 - c + 31]
    return np.ascontiguousarray(out.reshape(8, 2, P, L).transpose(2, 1, 0, 3).reshape(P, 2 * 8 * L))


def _bias2(rb):
    i, j = np.arange(L)[:, None], np.arange(L)[None, :]
    rel = np.clip(i - j, -128, 128) + 128
    out = np.where((j // 64 <= i // 64)[None], rb[:, rel], np.float32(NEG)).astype(np.float32)
    return np.ascontiguousarray(out.reshape(8, 2, P, L).transpose(2, 1, 0, 3).reshape(P, 2 * 8 * L))


def _shape_tables():
    i, j = np.arange(L)[:, None], np.arange(L)[None, :]
    mask = np.where(j // 64 <= i // 64, 0.0, NEG).astype(np.float32)
    mask = mask.reshape(2, P, L).transpose(1, 0, 2).reshape(P, 2 * L)
    inv = 1.0 / (10000.0 ** (np.arange(0, 32, 2, dtype=np.float32) / np.float32(32)))
    ang = np.arange(L, dtype=np.float32)[:, None] * inv.astype(np.float32)[None, :]

    def twice(a):
        a = np.concatenate([a, a], axis=1).astype(np.float32)
        return a.reshape(2, P, 32).transpose(1, 0, 2).reshape(P, 64)
    t = np.arange(L)
    cnt = [np.clip(t + w - w // 2, 0, L) - np.clip(t - w // 2, 0, L) for w in (2, 4, 8, 16)]
    invcnt = (1.0 / np.stack(cnt).astype(np.float32)).astype(np.float32).reshape(1, 4 * L)
    invd = np.zeros((P, 16), np.float32)
    invd[:, 0:6] = [1 / 256, 1 / 128, 1 / 32] * 2
    return mask, twice(np.cos(ang)), twice(np.sin(ang)), invcnt, invd


def kernel(**inputs):
    import concourse.bacc as bacc
    from concourse.bass_utils import run_bass_kernel_spmd

    v = {k: np.asarray(a) for k, a in inputs.items()}
    mask, cos2, sin2, invcnt, invd = _shape_tables()
    ones32 = np.ones(32, np.float32)
    w_mod, b_mod, w_in = v["w_mod"][0], v["b_mod"][0], v["w_in"][0]
    w_in2 = v["w_in_2"][0]
    cc = np.stack([_column(v["c"][0]), _column(v["c_ctx"])], axis=2).reshape(P, 16)
    parts = {
        "ident": np.eye(P, dtype=np.float32), "cc": cc,
        "b_sh1": _column(b_mod[0:1024]), "b_sc1": _column(b_mod[1024:2048]),
        "b_sh2": _column(b_mod[3072:4096]), "b_sc2": _column(b_mod[4096:5120]),
        "g_mix": _column(v["g_pre_mix"][0]), "g_mlp": _column(v["g_pre_mlp"][0]),
        "pool_scale": _column(v["pool_scale"][0]), "g_ffn1": _column(v["ffn1_norm_2"][0]),
        "g_mix2": _column(v["mix_norm_2"][0]), "g_ffn2": _column(v["ffn2_norm_2"][0]),
        "g_aq": np.tile(v["a_q_norm_2"][0], 2)[:, None], "g_ak": np.tile(v["a_k_norm_2"][0], 2)[:, None],
        "g_bq": np.concatenate([v["b_q_nope_norm_2"][0], ones32, ones32])[:, None],
        "g_bk": np.concatenate([v["b_k_nope_norm_2"][0], ones32, ones32])[:, None],
        "g_ql": _column(v["b_q_lat_norm_2"][0]), "g_kvl": _column(v["b_kv_lat_norm_2"][0]),
        "g_qr": np.broadcast_to(v["b_q_rope_norm_2"][0], (P, 32)),
        "g_kr": np.broadcast_to(v["b_k_rope_norm_2"][0], (P, 32)),
        "cos2": cos2, "sin2": sin2, "invd": invd, "mask": mask,
        "pool_w": v["pool_w"][0].transpose(1, 0, 2).reshape(P, 512),
    }
    arrays = {
        "cols": np.ascontiguousarray(np.concatenate([parts[k] for k in COLS], axis=1)),
        "x": v["x"][0], "ctx": v["ctx"][0],
        "rows": np.stack([b_mod[2048:3072], v["g_post_mix"][0], b_mod[5120:6144], v["g_post_mlp"][0],
                          v["final_norm_2"][0]]),
        "invcnt": invcnt, "bias1": _bias1(v["rpb"][0]), "bias2": _bias2(v["a_rel_bias_2"][0]),
        "w_mod_c": w_mod[:, 0:2048].reshape(KT, P, 2, 1024).transpose(2, 0, 1, 3).reshape(16, P, 1024),
        "w_mod_r": np.concatenate([_rows(w_mod[:, a:a + 1024]) for a in (2048, 3072, 4096, 5120)]),
        "w_in_u": _tiles(w_in[:, 0:512]), "w_in_q": _tiles(w_in[:, 512:1024]),
        "w_in_k": _tiles(w_in[:, 1024:1536]), "w_in_v": _row_pairs(w_in[:, 1536:2048]),
        "w_out": _rows(v["w_out"][0]), "w_mlp_in_rows": _row_pairs(v["w_mlp_in"][0][:, 0:512]),
        "w_mlp_in": _tiles(v["w_mlp_in"][0][:, 512:]), "w_mlp_out": _rows(v["w_mlp_out"][0]),
        "w_in2_q": _row_pairs(w_in2[:, 0:512]), "w_in2_k": _row_pairs(w_in2[:, 512:1024]),
        "w_in2_v": _row_pairs(w_in2[:, 1024:1536]), "w_in2_l": _row_pairs(w_in2[:, 1536:1952]),
        "w_uq": _rows(v["b_w_uq_2"][0]), "w_ukv": _rows(v["b_w_ukv_2"][0]), "w_out2": _rows(v["w_out_2"][0]),
    }
    for a in ("ffn1", "ffn2"):
        gate, up = v[a + "_w_gate_2"][0], v[a + "_w_up_2"][0]
        arrays[a + "_rows"] = _row_pairs(np.concatenate([gate[:, 0:L], up[:, 0:L]], axis=1))
        arrays[a + "_gate"] = _tiles(gate[:, L:])
        arrays[a + "_up"] = _tiles(up[:, L:])
        arrays[a + "_down"] = _rows(v[a + "_w_down_2"][0])
    arrays = {k: np.ascontiguousarray(a) for k, a in arrays.items()}

    nc = bacc.Bacc("TRN2", target_bir_lowering=False, num_devices=1)
    t = {k: nc.dram_tensor("in_" + k, a.shape, F32, kind="ExternalInput").ap() for k, a in arrays.items()}
    t["out"] = nc.dram_tensor("out_0", (L, D), F32, kind="ExternalOutput").ap()
    build(nc, t)
    res = run_bass_kernel_spmd(nc, [{"in_" + k: a for k, a in arrays.items()}], core_ids=[0])
    return res.results[0]["out_0"].reshape(1, L, D)
```
